# Optimizing a Trainium2 kernel written in Bass

```python
import math
import jax, jax.numpy as jnp
from jax import lax
import numpy as np

D_MODEL = 1024
BATCH = 1
SEQ = 512
DEPTH = 1

GRID_W = 64
CTX_LEN = 256
HEAD_DIM = 64
ATT_W = D_MODEL // 2
NA_HEADS = ATT_W // HEAD_DIM
NA_ROWS_MAX = 8
NA_COLS = 16
NA_QCOLS = 16
SG_W = D_MODEL // 4
SG_GROUPS = 4
SG_CHUNK = 128
CV_W = D_MODEL // 4
CV_GROUPS = 4
CV_KERNEL = 31
MIX_W = ATT_W + SG_W + CV_W
N_IN = 3 * ATT_W + 2 * SG_W + 2 * CV_W
D_FF = 256 * ((8 * D_MODEL // 3 + 255) // 256)
FFN_KERNEL = 3
EPS = 1e-6
NEG_INF = -1e30


def _rmsnorm(x, g):
    x32 = x.astype(jnp.float32)
    y = x32 * lax.rsqrt(jnp.mean(x32 * x32, axis=-1, keepdims=True) + EPS)
    return y.astype(x.dtype) * g

def _layernorm(x, g, b):
    x32 = x.astype(jnp.float32)
    mu = jnp.mean(x32, axis=-1, keepdims=True)
    var = jnp.mean(jnp.square(x32 - mu), axis=-1, keepdims=True)
    return ((x32 - mu) * lax.rsqrt(var + EPS)).astype(x.dtype) * g + b

def _group_layernorm(x, g, b, groups):
    shp = x.shape
    x32 = x.astype(jnp.float32).reshape(shp[:-1] + (groups, shp[-1] // groups))
    mu = jnp.mean(x32, axis=-1, keepdims=True)
    var = jnp.mean(jnp.square(x32 - mu), axis=-1, keepdims=True)
    y = ((x32 - mu) * lax.rsqrt(var + EPS)).reshape(shp).astype(x.dtype)
    return y * g + b

def _modulate(h, shift, scale):
    return h * (1 + scale) + shift

def _dwconv(x, w, b):
    k = w.shape[0]
    ch = x.shape[-1]
    y = lax.conv_general_dilated(
        x, w[:, None, :].astype(x.dtype), window_strides=(1,),
        padding=[((k - 1) // 2, k // 2)],
        dimension_numbers=("NWC", "WIO", "NWC"), feature_group_count=ch)
    return y + b

def _heads(t):
    bn, ln, _ = t.shape
    return t.reshape(bn, ln, NA_HEADS, HEAD_DIM).transpose(0, 2, 1, 3)

def _axis_span(length, win, qblk):
    span = min(qblk + win, length)
    start = np.clip(np.arange(length) - win // 2, 0, length - win)
    a = np.clip(np.arange(0, length, qblk) - win // 2, 0, length - span)
    qpos = np.arange(length).reshape(-1, qblk)
    kpos = a[:, None] + np.arange(span)[None, :]
    s_q = start[qpos][:, :, None]
    inwin = (kpos[:, None, :] >= s_q) & (kpos[:, None, :] < s_q + win)
    off = kpos[:, None, :] - qpos[:, :, None]
    return kpos, inwin, off

def _na_index(rows):
    win_r = min(NA_ROWS_MAX, rows)
    qr = next(q for q in (8, 4, 2, 1) if rows % q == 0)
    kr, mr, dr = _axis_span(rows, win_r, qr)
    kc, mc, dc = _axis_span(GRID_W, NA_COLS, NA_QCOLS)
    nbr, nbc = kr.shape[0], kc.shape[0]
    nq = qr * NA_QCOLS
    key_idx = (kr[:, None, :, None] * GRID_W + kc[None, :, None, :]).reshape(nbr * nbc, -1)
    mask = (mr[:, None, :, None, :, None] & mc[None, :, None, :, None, :]).reshape(nbr * nbc, nq, -1)
    ridx = np.clip(dr + NA_ROWS_MAX - 1, 0, 2 * NA_ROWS_MAX - 2)
    cidx = np.clip(dc + NA_COLS - 1, 0, 2 * NA_COLS - 2)
    bias_idx = (ridx[:, None, :, None, :, None] * (2 * NA_COLS - 1)
                + cidx[None, :, None, :, None, :]).reshape(nbr * nbc, nq, -1)
    return qr, key_idx.astype(np.int32), mask, bias_idx.astype(np.int32)

def _neighbourhood_attention(q, k, v, k_ctx, v_ctx, rpb, rows):
    bn, nh, sl, dh = q.shape
    qr, key_idx, mask, bias_idx = _na_index(rows)
    nbr, nbc = rows // qr, GRID_W // NA_QCOLS
    span = key_idx.shape[-1]
    qb = q.reshape(bn, nh, nbr, qr, nbc, NA_QCOLS, dh).transpose(2, 4, 0, 1, 3, 5, 6)
    qb = qb.reshape(nbr * nbc, bn, nh, qr * NA_QCOLS, dh)
    rpb_flat = rpb.reshape(nh, -1)
    scale = dh ** -0.5

    def block(args):
        qblk, kidx, m, bidx = args
        kb = jnp.take(k, kidx, axis=2)
        vb = jnp.take(v, kidx, axis=2)
        s_loc = jnp.einsum("bhqd,bhkd->bhqk", qblk, kb).astype(jnp.float32) * scale
        s_loc = s_loc + jnp.take(rpb_flat, bidx, axis=1).astype(jnp.float32)[None]
        s_loc = jnp.where(m[None, None], s_loc, NEG_INF)
        s_ctx = jnp.einsum("bhqd,bhkd->bhqk", qblk, k_ctx).astype(jnp.float32) * scale
        p = jax.nn.softmax(jnp.concatenate([s_loc, s_ctx], axis=-1), axis=-1).astype(v.dtype)
        return (jnp.einsum("bhqk,bhkd->bhqd", p[..., :span], vb)
                + jnp.einsum("bhqk,bhkd->bhqd", p[..., span:], v_ctx))

    out = lax.map(block, (qb, jnp.asarray(key_idx), jnp.asarray(mask), jnp.asarray(bias_idx)))
    out = out.reshape(nbr, nbc, bn, nh, qr, NA_QCOLS, dh).transpose(2, 0, 4, 1, 5, 3, 6)
    return out.reshape(bn, sl, nh * dh)

def _context_attention(q, k, v):
    s = jnp.einsum("bhqd,bhkd->bhqk", q, k).astype(jnp.float32) * (q.shape[-1] ** -0.5)
    p = jax.nn.softmax(s, axis=-1).astype(v.dtype)
    o = jnp.einsum("bhqk,bhkd->bhqd", p, v)
    bn, nh, ln, dh = o.shape
    return o.transpose(0, 2, 1, 3).reshape(bn, ln, nh * dh)

def _spatial_gating(u, v, ln_g, ln_b, w_s, b_s):
    u = jax.nn.gelu(u)
    v = _layernorm(jax.nn.gelu(v), ln_g, ln_b)
    bn, ln, ch = v.shape
    vr = v.reshape(bn, ln // SG_CHUNK, SG_CHUNK, SG_GROUPS, ch // SG_GROUPS)
    mixed = jnp.einsum("gpq,bnqgc->bnpgc", w_s, vr) + b_s.T[None, None, :, :, None]
    return u * mixed.reshape(bn, ln, ch)

def _conformer_conv(a, gate, w, b, ng, nb):
    h = a * jax.nn.sigmoid(gate)
    h = _dwconv(h, w, b)
    h = _group_layernorm(h, ng, nb, CV_GROUPS)
    return jax.nn.silu(h)

def _mix_out(att, z, sg_ng, sg_nb, sg_w, sg_b, cv_w, cv_b, cv_ng, cv_nb, w_out):
    o1 = 3 * ATT_W
    o2 = o1 + 2 * SG_W
    sg = _spatial_gating(z[..., o1:o1 + SG_W], z[..., o1 + SG_W:o2], sg_ng, sg_nb, sg_w, sg_b)
    cv = _conformer_conv(z[..., o2:o2 + CV_W], z[..., o2 + CV_W:o2 + 2 * CV_W],
                         cv_w, cv_b, cv_ng, cv_nb)
    return jnp.concatenate([att, sg, cv], axis=-1) @ w_out

def _conv_ffn(h, w_up, conv_w, conv_b, w_down):
    gate, up = jnp.split(h @ w_up, 2, axis=-1)
    gate = _dwconv(gate, conv_w, conv_b)
    return (jax.nn.silu(gate) * up) @ w_down

def first_inputs(seed: int = 0) -> dict:
    key = jax.random.key(seed)
    ks = jax.random.split(key, 24)
    D = D_MODEL

    def n(k, shape, s):
        return jax.random.normal(k, shape, jnp.float32) * s

    return {
        "x": n(ks[0], (BATCH, SEQ, D), 1.0),
        "c": n(ks[1], (BATCH, D), 1.0),
        "ctx": n(ks[2], (BATCH, CTX_LEN, D), 1.0),
        "c_ctx": n(ks[3], (D,), 1.0),
        "ada_w": n(ks[4], (DEPTH, D, 6 * D), 0.5 * D ** -0.5),
        "ada_b": n(ks[5], (DEPTH, 6 * D), 0.02),
        "norm1_g": 1.0 + n(ks[6], (DEPTH, D), 0.05),
        "w_in": n(ks[7], (DEPTH, D, N_IN), D ** -0.5),
        "na_rpb": n(ks[8], (DEPTH, NA_HEADS, 2 * NA_ROWS_MAX - 1, 2 * NA_COLS - 1), 0.5),
        "sg_norm_g": 1.0 + n(ks[9], (DEPTH, SG_W), 0.05),
        "sg_norm_b": n(ks[10], (DEPTH, SG_W), 0.02),
        "sg_w": n(ks[11], (DEPTH, SG_GROUPS, SG_CHUNK, SG_CHUNK), SG_CHUNK ** -0.5),
        "sg_b": 1.0 + n(ks[12], (DEPTH, SG_GROUPS, SG_CHUNK), 0.1),
        "cv_w": n(ks[13], (DEPTH, CV_KERNEL, CV_W), CV_KERNEL ** -0.5),
        "cv_b": n(ks[14], (DEPTH, CV_W), 0.02),
        "cv_norm_g": 1.0 + n(ks[15], (DEPTH, CV_W), 0.05),
        "cv_norm_b": n(ks[16], (DEPTH, CV_W), 0.02),
        "w_out": n(ks[17], (DEPTH, MIX_W, D), MIX_W ** -0.5),
        "norm2_g": 1.0 + n(ks[18], (DEPTH, D), 0.05),
        "ffn_w_up": n(ks[19], (DEPTH, D, 2 * D_FF), D ** -0.5),
        "ffn_conv_w": n(ks[20], (DEPTH, FFN_KERNEL, D_FF), FFN_KERNEL ** -0.5),
        "ffn_conv_b": n(ks[21], (DEPTH, D_FF), 0.02),
        "ffn_w_down": n(ks[22], (DEPTH, D_FF, D), D_FF ** -0.5),
        "final_norm_g": 1.0 + n(ks[23], (D,), 0.05),
    }

def first_block(x, c, ctx, c_ctx, ada_w, ada_b, norm1_g, w_in, na_rpb, sg_norm_g, sg_norm_b,
              sg_w, sg_b, cv_w, cv_b, cv_norm_g, cv_norm_b, w_out, norm2_g, ffn_w_up,
              ffn_conv_w, ffn_conv_b, ffn_w_down, final_norm_g):
    rows = x.shape[1] // GRID_W
    xc = ctx
    for l in range(DEPTH):
        last = l == DEPTH - 1
        mod_l = jnp.split((jax.nn.silu(c) @ ada_w[l] + ada_b[l])[:, None, :], 6, axis=-1)
        mod_c = jnp.split((jax.nn.silu(c_ctx) @ ada_w[l] + ada_b[l])[None, None, :], 6, axis=-1)

        h = _modulate(_rmsnorm(x, norm1_g[l]), mod_l[0], mod_l[1])
        hc = _modulate(_rmsnorm(xc, norm1_g[l]), mod_c[0], mod_c[1])
        z = h @ w_in[l]
        q = _heads(z[..., :ATT_W])
        k = _heads(z[..., ATT_W:2 * ATT_W])
        v = _heads(z[..., 2 * ATT_W:3 * ATT_W])
        if last:
            kvc = hc @ w_in[l][:, ATT_W:3 * ATT_W]
            kc = _heads(kvc[..., :ATT_W])
            vc = _heads(kvc[..., ATT_W:])
        else:
            zc = hc @ w_in[l]
            kc = _heads(zc[..., ATT_W:2 * ATT_W])
            vc = _heads(zc[..., 2 * ATT_W:3 * ATT_W])
        att = _neighbourhood_attention(q, k, v, kc, vc, na_rpb[l], rows)
        y = _mix_out(att, z, sg_norm_g[l], sg_norm_b[l], sg_w[l], sg_b[l], cv_w[l], cv_b[l],
                     cv_norm_g[l], cv_norm_b[l], w_out[l])
        x = x + mod_l[2] * y
        if not last:
            att_c = _context_attention(_heads(zc[..., :ATT_W]), kc, vc)
            yc = _mix_out(att_c, zc, sg_norm_g[l], sg_norm_b[l], sg_w[l], sg_b[l], cv_w[l],
                          cv_b[l], cv_norm_g[l], cv_norm_b[l], w_out[l])
            xc = xc + mod_c[2] * yc

        h2 = _modulate(_rmsnorm(x, norm2_g[l]), mod_l[3], mod_l[4])
        x = x + mod_l[5] * _conv_ffn(h2, ffn_w_up[l], ffn_conv_w[l], ffn_conv_b[l], ffn_w_down[l])
        if not last:
            h2c = _modulate(_rmsnorm(xc, norm2_g[l]), mod_c[3], mod_c[4])
            xc = xc + mod_c[5] * _conv_ffn(h2c, ffn_w_up[l], ffn_conv_w[l], ffn_conv_b[l],
                                           ffn_w_down[l])
    return _rmsnorm(x, final_norm_g)


ATT_HEADS = 8
ATT_WIDTH = ATT_HEADS * HEAD_DIM
CONV_GROUPS = 8
CONV_WIDTH = D_MODEL - ATT_WIDTH
CONV_K = 3
FFN_CONV_K = 3
D_FF_2 = 2816
Q_BLOCK = 128
RMS_EPS = 1e-6
IN_COLS = 3 * ATT_WIDTH + 3 * CONV_WIDTH + 2 * D_MODEL
IN_SPLITS = (ATT_WIDTH, 2 * ATT_WIDTH, 3 * ATT_WIDTH,
             3 * ATT_WIDTH + CONV_WIDTH, 3 * ATT_WIDTH + 2 * CONV_WIDTH,
             3 * ATT_WIDTH + 3 * CONV_WIDTH, 3 * ATT_WIDTH + 3 * CONV_WIDTH + D_MODEL)


def rms_norm(x, g):
    xf = x.astype(jnp.float32)
    var = jnp.mean(xf * xf, axis=-1, keepdims=True)
    return (xf * lax.rsqrt(var + RMS_EPS) * g.astype(jnp.float32)).astype(x.dtype)

def causal_dwconv(u, w):
    kw = w.shape[0]
    s = u.shape[1]
    up = jnp.pad(u, ((0, 0), (kw - 1, 0), (0, 0)))
    y = up[:, 0:s, :] * w[0]
    for i in range(1, kw):
        y = y + up[:, i:i + s, :] * w[i]
    return y

def stick_breaking_attention(q, k, v):
    _, _, s, dh = q.shape
    scale = 1.0 / math.sqrt(dh)
    outs = []
    for blk in range(s // Q_BLOCK):
        t0 = blk * Q_BLOCK
        t1 = t0 + Q_BLOCK
        qb = q[:, :, t0:t1]
        kb = k[:, :, :t1]
        vb = v[:, :, :t1]
        z = jnp.einsum("bhqd,bhkd->bhqk", qb, kb).astype(jnp.float32) * scale
        t_idx = t0 + jnp.arange(Q_BLOCK)[:, None]
        s_idx = jnp.arange(t1)[None, :]
        strict = s_idx < t_idx
        log_keep = jnp.where(strict, jax.nn.log_sigmoid(-z), 0.0)
        later = lax.cumsum(log_keep, axis=3, reverse=True) - log_keep
        w = jnp.where(strict, jnp.exp(jax.nn.log_sigmoid(z) + later), 0.0)
        outs.append(jnp.einsum("bhqk,bhkd->bhqd", w, vb.astype(jnp.float32)))
    return jnp.concatenate(outs, axis=2).astype(q.dtype)

def second_inputs(seed: int = 0) -> dict:
    key = jax.random.key(seed)
    ks = jax.random.split(key, 14)
    f32 = jnp.float32

    def nrm(k, shape, fan_in):
        return jax.random.normal(k, shape, f32) * (fan_in ** -0.5)

    def gain(k):
        return 1.0 + 0.05 * jax.random.normal(k, (DEPTH, D_MODEL), f32)

    return {
        "x": jax.random.normal(ks[0], (BATCH, SEQ, D_MODEL), f32),
        "norm_mix_pre": gain(ks[1]),
        "w_in": nrm(ks[2], (DEPTH, D_MODEL, IN_COLS), D_MODEL),
        "conv_mix_w": nrm(ks[3], (DEPTH, CONV_K, CONV_WIDTH), CONV_K),
        "w_att_branch": nrm(ks[4], (DEPTH, ATT_WIDTH, D_MODEL), ATT_WIDTH),
        "w_conv_branch": nrm(ks[5], (DEPTH, CONV_WIDTH, D_MODEL), CONV_WIDTH),
        "w_out": nrm(ks[6], (DEPTH, D_MODEL, D_MODEL), D_MODEL),
        "norm_mix_post": gain(ks[7]),
        "norm_ffn_pre": gain(ks[8]),
        "w_up": nrm(ks[9], (DEPTH, D_MODEL, 2 * D_FF_2), D_MODEL),
        "conv_ffn_w": nrm(ks[10], (DEPTH, FFN_CONV_K, 2 * D_FF_2), FFN_CONV_K),
        "w_down": nrm(ks[11], (DEPTH, D_FF_2, D_MODEL), D_FF_2),
        "norm_ffn_post": gain(ks[12]),
    }

def second_block(x, norm_mix_pre, w_in, conv_mix_w, w_att_branch, w_conv_branch, w_out,
              norm_mix_post, norm_ffn_pre, w_up, conv_ffn_w, w_down, norm_ffn_post):
    b, s, _ = x.shape
    for l in range(DEPTH):
        h = rms_norm(x, norm_mix_pre[l])
        proj = h @ w_in[l]
        q, k, v, cb, cc, cx, g_att, g_conv = jnp.split(proj, IN_SPLITS, axis=-1)

        def heads(t):
            return t.reshape(b, s, ATT_HEADS, HEAD_DIM).transpose(0, 2, 1, 3)

        o = stick_breaking_attention(heads(q), heads(k), heads(v))
        y_att = o.transpose(0, 2, 1, 3).reshape(b, s, ATT_WIDTH) @ w_att_branch[l]

        y_conv = (cb * causal_dwconv(cc * cx, conv_mix_w[l])) @ w_conv_branch[l]

        merged = jax.nn.sigmoid(g_att) * y_att + jax.nn.sigmoid(g_conv) * y_conv
        x = x + rms_norm(merged @ w_out[l], norm_mix_post[l])

        h = rms_norm(x, norm_ffn_pre[l])
        u = causal_dwconv(h @ w_up[l], conv_ffn_w[l])
        a, g = jnp.split(u, 2, axis=-1)
        f = (jax.nn.gelu(g, approximate=True) * a) @ w_down[l]
        x = x + rms_norm(f, norm_ffn_post[l])
    return x


def setup_inputs(seed=0):
    out = dict(first_inputs(seed))
    for name, value in second_inputs(seed + 1).items():
        if name != "x":
            out[name + "_2"] = value
    return out


def reference(
    x, c, ctx, c_ctx, ada_w, ada_b, norm1_g, w_in, na_rpb, sg_norm_g, sg_norm_b, sg_w, sg_b,
    cv_w, cv_b, cv_norm_g, cv_norm_b, w_out, norm2_g, ffn_w_up, ffn_conv_w, ffn_conv_b,
    ffn_w_down, final_norm_g, norm_mix_pre_2, w_in_2, conv_mix_w_2, w_att_branch_2,
    w_conv_branch_2, w_out_2, norm_mix_post_2, norm_ffn_pre_2, w_up_2, conv_ffn_w_2, w_down_2,
    norm_ffn_post_2,
):
    x = first_block(
        x, c, ctx, c_ctx, ada_w, ada_b, norm1_g, w_in, na_rpb, sg_norm_g, sg_norm_b, sg_w, sg_b,
        cv_w, cv_b, cv_norm_g, cv_norm_b, w_out, norm2_g, ffn_w_up, ffn_conv_w, ffn_conv_b,
        ffn_w_down, final_norm_g,
    )
    return second_block(
        x, norm_mix_pre_2, w_in_2, conv_mix_w_2, w_att_branch_2, w_conv_branch_2, w_out_2,
        norm_mix_post_2, norm_ffn_pre_2, w_up_2, conv_ffn_w_2, w_down_2, norm_ffn_post_2,
    )


_drawn_inputs = setup_inputs


def setup_inputs(seed=0):
    import zlib

    import numpy as np

    out = dict(_drawn_inputs(seed))
    spreads = {}
    factors = {'norm1_g': 2.992,
     'na_rpb': 4.91,
     'sg_norm_g': 6.116,
     'sg_norm_b': 8.0,
     'sg_b': 3.152,
     'cv_b': 8.0,
     'cv_norm_g': 18.297,
     'cv_norm_b': 40.027,
     'ffn_conv_b': 21.477,
     'norm2_g': 6.006}
    for name, (base, spread) in spreads.items():
        noise = np.random.default_rng([zlib.crc32(name.encode()), seed]).standard_normal(out[name].shape)
        drawn = base * np.exp(spread * noise) if base else spread * noise
        out[name] = __import__('jax').numpy.asarray(drawn.astype(out[name].dtype))
    for name, factor in factors.items():
        out[name] = (out[name] * factor).astype(out[name].dtype)
    return out
```

```python
from contextlib import ExitStack

import numpy as np

import concourse.bass as bass
from concourse import mybir
from concourse.alu_op_type import AluOpType as ALU

F32 = mybir.dt.float32
F32R = mybir.dt.float32r
ACT = mybir.ActivationFunctionType
AX = mybir.AxisListType

P = 128
D = 1024
KC = D // P
T = 512
TT = T // P
CTX = 256
CT = CTX // P
HD = 64
HEADS = 8
ATT = HEADS * HD
AC = ATT // P
SG = 256
SC = SG // P
CV = 256
CC = CV // P
TAPS = 31
PAD = TAPS // 2
DFF = 2816
FC = DFF // P
GRID_W = 64
ROWS = T // GRID_W
WIN = 16
SPAN = 32
CBLK = GRID_W // WIN
RPB_W = 31
WINDOW = WIN + (ROWS - 1) * RPB_W + SPAN
SPAN_START = [min(max(WIN * b - WIN // 2, 0), GRID_W - SPAN) for b in range(CBLK)]
SPAN_OFFS = sorted({SPAN_START[b] - WIN * b for b in range(CBLK)}, reverse=True)
SCALE = HD ** -0.5
EPS = 1e-6
NEG = -1e30
SLOT = 1024

COLUMN_SIZES = [
    ("c", KC), ("c_ctx", KC), ("ada_b", 6 * KC), ("norm1_g", KC), ("norm2_g", KC), ("final_norm_g", KC),
    ("cv_w", CC * TAPS), ("cv_b", CC), ("cv_norm_g", CC), ("cv_norm_b", CC),
    ("ffn_conv_w", FC * 3), ("ffn_conv_b", FC),
    ("norm_mix_pre_2", KC), ("norm_mix_post_2", KC), ("norm_ffn_pre_2", KC), ("norm_ffn_post_2", KC),
    ("conv_mix_w_2", AC * 3), ("conv_ffn_w_2", 2 * FC * 3), ("eps", 1), ("one", 1),
]
COLUMNS = {}
_at = 0
for _name, _n in COLUMN_SIZES:
    COLUMNS[_name] = (_at, _n)
    _at += _n
N_COLUMNS = _at

CONST_SIZES = [
    ("identity", P), ("group_mean", P), ("minus_ones", P), ("minus_tri", P), ("causal_neg", P),
    ("window_neg", len(SPAN_OFFS) * SPAN),
]
CONSTS = {}
_at = 0
for _name, _n in CONST_SIZES:
    CONSTS[_name] = (_at, _n)
    _at += _n
N_CONSTS = _at


class Queue:

    def __init__(self, engine, sem):
        self.engine, self.sem, self.count, self.waited = engine, sem, 0, {}

    def wait(self, *after):
        need = {}
        for sem, count in flat(after):
            if count > self.waited.get(sem.num, 0):
                self.waited[sem.num] = count
                need[sem.num] = (sem, count)
        for sem, count in need.values():
            self.engine.wait_ge(sem, count)

    def do(self, step, *after):
        self.wait(*after)
        self.count += 1
        step(self.engine).then_inc(self.sem, 1)
        return (self.sem, self.count)

    def load(self, counter, dst, src, *after):
        self.wait(*after)
        counter[1] += 16
        self.engine.dma_start(dst, src).then_inc(counter[0], 16)
        return (counter[0], counter[1])


def flat(marks):
    out = []
    for m in marks:
        if m is None:
            continue
        out += flat(m) if isinstance(m, list) else [m]
    return out


class Banks:

    def __init__(self, tensors, turning):
        self.tensors, self.free, self.turning, self.at = tensors, [None] * len(tensors), turning, -1

    def take(self):
        self.at = (self.at + 1) % self.turning
        return self.at


class WeightStream:

    RAW, SPLIT = 3, 3

    def __init__(self, order, raw, hi, lo, counters, sync, act, dve):
        self.order, self.raw, self.hi, self.lo, self.counters = order, raw, hi, lo, counters
        self.sync, self.act, self.dve, self.takers = sync, act, dve, {}
        self.raw_free, self.split_free = [None] * self.RAW, [None] * self.SPLIT
        self.arrived, self.ready = {}, {}
        self.loaded = self.prepared = self.n_split = self.next = self.used = 0
        for _ in range(self.RAW):
            self.load_next()

    def load_next(self):
        i = self.loaded
        if i < len(self.order):
            _, src, n, _ = self.order[i]
            slot = i % self.RAW
            dst = self.raw[:, slot, 0:n]
            if len(src.shape) == 3:
                dst = dst.rearrange("p (k n) -> p k n", k=src.shape[1])
            self.arrived[i] = self.sync.load(self.counters[slot], dst, src, self.raw_free[slot])
            self.loaded += 1

    def prepare_next(self):
        i = self.prepared
        kind, _, n, detail = self.order[i]
        slot = i % self.RAW
        tile = self.raw[:, slot, 0:n]
        if kind == "split":
            s = self.n_split % self.SPLIT
            self.n_split += 1
            hi_s, lo_s = self.hi[:, s, 0:n], self.lo[:, s, 0:n]
            hi = self.act.do(lambda e: e.activation(hi_s, tile, ACT.Copy), self.arrived[i], self.split_free[s])
            lo = self.dve.do(lambda e: e.tensor_tensor(lo_s, tile, hi_s.bitcast(F32), ALU.subtract),
                             self.arrived[i], hi, self.split_free[s])
            self.ready[i] = (s, [hi, lo], detail)
            self.raw_free[slot] = [lo]
        else:
            self.raw_free[slot] = [self.takers[kind](tile, detail, self.arrived[i])]
        self.prepared += 1
        self.load_next()

    def next_tile(self):
        while self.prepared < len(self.order) and self.n_split < self.used + self.SPLIT:
            self.prepare_next()
        while self.order[self.next][0] != "split":
            self.next += 1
        self.next += 1
        self.used += 1
        return self.ready[self.next - 1]


def two_blocks(nc, io, out):
    with ExitStack() as whole:
        def sb(stack, name, shape, dt=F32):
            return stack.enter_context(nc.sbuf_tensor(name, shape, dt))

        def counter(name):
            return [whole.enter_context(nc.semaphore(name)), 0]

        pe, act, dve, pool, sync = (
            Queue(engine, counter(f"s_{name}")[0])
            for name, engine in (("pe", nc.tensor), ("act", nc.scalar), ("dve", nc.vector), ("pool", nc.gpsimd),
                                 ("sync", nc.sync)))

        def everyone():
            return [(q.sem, q.count) for q in (pe, act, dve, pool)]

        x = sb(whole, "x_res", [P, KC, T])
        h_hi = sb(whole, "h_hi", [P, KC, T], F32R)
        h_lo = sb(whole, "h_lo", [P, KC, T], F32R)
        cols = sb(whole, "cols_sb", [P, N_COLUMNS])
        consts = sb(whole, "consts_sb", [P, N_CONSTS])
        ones = sb(whole, "ones", [P, 1])
        mod = sb(whole, "mod", [P, 6 * KC])
        gain = sb(whole, "gain", [P, KC])
        squares = sb(whole, "squares", [P, 2, T])
        normed = sb(whole, "normed", [P, 2, T])
        exact = sb(whole, "exact", [P, 2, T])
        std = sb(whole, "std", [P, 2 * TT])
        rstd = sb(whole, "rstd", [P, 2 * TT])
        raw = sb(whole, "raw_w", [P, WeightStream.RAW, SLOT])
        w_hi = sb(whole, "w_hi", [P, WeightStream.SPLIT, SLOT], F32R)
        w_lo = sb(whole, "w_lo", [P, WeightStream.SPLIT, SLOT], F32R)
        bank = [whole.enter_context(nc.psum_tensor(f"bank{b}", [P, T], F32)) for b in range(8)]
        banks = Banks(bank, 6)
        free = banks.free
        NORM_BANKS = (6, 7)

        def col(name, i=0):
            at = COLUMNS[name][0] + i
            return cols[:, at:at + 1]

        def cols_of(name):
            at, n = COLUMNS[name]
            return cols[:, at:at + n]

        def const(name):
            at, n = CONSTS[name]
            return consts[:, at:at + n]

        identity = const("identity")

        def blocks_of(name):
            w = io[name]
            n_out, _, kc, _ = w.shape
            sizes = [kc] if kc <= KC else [8, 7, 7]
            return [[("split", w[o, :, sum(sizes[:i]):sum(sizes[:i + 1]), :], n * P, (sum(sizes[:i]), n))
                     for i, n in enumerate(sizes)] for o in range(n_out)]

        def wide_of(name):
            w = io[name]
            return [[("split", w[t, :, :, :], w.shape[2] * w.shape[3], (t * w.shape[2], w.shape[2]))]
                    for t in range(w.shape[0])]

        def in_turn(plans, extra=(), each=2):
            extra, order = list(extra), []
            for tile in (t for tiles in plans for t in tiles):
                order.append(tile)
                order += extra[:each]
                del extra[:each]
            return order + extra

        order = [("ada_product", io["ada_blocks"][j, :, :, :], SLOT, j) for j in range(2 * KC)]
        order += in_turn(blocks_of("w_cv") + wide_of("w_sg_v") + blocks_of("w_k") + wide_of("w_v")
                         + blocks_of("w_sg_u") + blocks_of("w_q"),
                         [("ada_row", io["ada_rows"][j, :, :], SLOT, 2 * KC + j) for j in range(4 * KC)])
        order += in_turn(blocks_of("w_out"))
        up = blocks_of("w_ffn_up")
        order += in_turn([up[i] for f in range(FC) for i in (f, FC + f)])
        order += in_turn(blocks_of("w_ffn_down"))
        order += in_turn(blocks_of("w_qk2") + wide_of("w_v2") + blocks_of("w_conv3"))
        gates, atts, convs = blocks_of("w_gates2"), blocks_of("w_att2"), blocks_of("w_convb2")
        order += in_turn([p for o in range(KC) for p in (gates[o], gates[KC + o], atts[o], convs[o])])
        order += in_turn(blocks_of("w_out2"))
        up = blocks_of("w_up2")
        order += in_turn([up[i] for f in range(FC) for i in (f, FC + f)])
        order += in_turn(blocks_of("w_down2"))

        cols_in = act.load(counter("s_cols"), cols[:, :], io["cols"])
        x_in = [act.load(counter(f"s_x{i}"), x[:, 2 * i:2 * i + 2, :], io["x"][:, 2 * i:2 * i + 2, :])
                for i in range(KC // 2)]
        consts_in = act.load(counter("s_consts"), consts[:, :], io["consts"])
        stream = WeightStream(order, raw, w_hi, w_lo, [counter(f"s_raw{i}") for i in range(WeightStream.RAW)],
                              sync, act, dve)
        ones_set = dve.do(lambda e: e.memset(ones[:, :], 1.0))

        def product(e, dst, lhs_hi, lhs_lo, rhs_hi, rhs_lo, first, last):
            e.matmul(dst, lhs_hi, rhs_lo, start=first, stop=False)
            e.matmul(dst, lhs_lo, rhs_hi, start=False, stop=False)
            return e.matmul(dst, lhs_hi, rhs_hi, start=False, stop=last)

        def linear(n_tiles, k_total, src_hi, src_lo, src_marks):
            b = banks.take()
            mark = None
            for _ in range(n_tiles):
                s, w_marks, (k0, n) = stream.next_tile()
                for j in range(n):
                    k, w = k0 + j, slice(j * P, (j + 1) * P)
                    mark = pe.do(lambda e: product(e, bank[b][:, :], w_hi[:, s, w], w_lo[:, s, w], src_hi[:, k, :],
                                                   src_lo[:, k, :], k == 0, k == k_total - 1),
                                 w_marks, src_marks[k], free[b] if k == 0 else None)
                stream.split_free[s] = [mark]
            return b, mark

        def split(value, mark, dst_hi, dst_lo, dst_free=None):
            hi = act.do(lambda e: e.activation(dst_hi, value, ACT.Copy), mark, dst_free)
            lo = dve.do(lambda e: e.tensor_tensor(dst_lo, value, dst_hi.bitcast(F32), ALU.subtract), mark, hi, dst_free)
            return [hi, lo]

        square_free, buffer_free = [None, None], [None, None]
        turn = {"norm": 0, "square": 0, "buffer": 0}

        class Norm:

            def __init__(self, n_tok):
                self.n_tok, self.k, self.pending = n_tok, 0, []
                self.b = NORM_BANKS[turn["norm"] % 2]
                self.at = (turn["norm"] % 2) * TT
                turn["norm"] += 1
                self.mark = None

            def square(self, v, mark):
                i = turn["square"] % 2
                turn["square"] += 1
                m = act.do(lambda e: e.activation(squares[:, i, 0:self.n_tok], v, ACT.Square), mark, square_free[i])
                self.pending.append((i, m))

            def sum(self):
                i, m = self.pending.pop(0)
                k, nt = self.k, self.n_tok // P

                def sums(e):
                    for t in range(nt):
                        mm = e.matmul(bank[self.b][:, t:t + 1], squares[:, i, t * P:(t + 1) * P], ones[:, :],
                                      start=(k == 0 and t == 0), stop=(k == KC - 1 and t == nt - 1),
                                      skip_group_check=True)
                    return mm
                self.mark = pe.do(sums, m, ones_set, free[self.b] if k == 0 else None)
                square_free[i] = [self.mark]
                self.k += 1

            def finish(self):
                while self.pending:
                    self.sum()
                nt, b, at = self.n_tok // P, self.b, self.at
                root = act.do(lambda e: e.activation(std[:, at:at + nt], bank[b][:, 0:nt], ACT.Sqrt, scale=1.0 / D,
                                                     bias=col("eps")), self.mark, cols_in)
                inverse = dve.do(lambda e: e.reciprocal(rstd[:, at:at + nt], std[:, at:at + nt]), root)

                def spread(e):
                    for t in range(nt):
                        mm = e.matmul(bank[b][:, t * P:(t + 1) * P], rstd[:, at + t:at + t + 1].to_broadcast([P, P]),
                                      identity, start=True, stop=True)
                    return mm
                return b, pe.do(spread, inverse, root, consts_in)

        def apply_norm(norm, chunk, chunk_marks, n_tok, a_of, b_of, params, dst_hi, dst_lo, dst_free):
            r, m = norm.finish()
            marks, last = [], None
            for k in range(KC):
                i = turn["buffer"] % 2
                turn["buffer"] += 1
                src, v, a = chunk(k), exact[:, i, 0:n_tok], a_of(k)
                factor = bank[r][:, 0:n_tok]
                if b_of is None:
                    value = last = dve.do(lambda e: e.scalar_tensor_tensor(
                        out=v, in0=src, scalar=a, in1=factor, op0=ALU.mult, op1=ALU.mult),
                        m, chunk_marks[k], params, buffer_free[i])
                else:
                    n = normed[:, i, 0:n_tok]
                    last = dve.do(lambda e: e.tensor_tensor(n, src, factor, ALU.mult), m, chunk_marks[k], buffer_free[i])
                    b = b_of(k)
                    value = pool.do(lambda e: e.tensor_scalar(v, n, a, b, ALU.mult, ALU.add), last, params, buffer_free[i])
                marks.append(split(v, value, dst_hi[:, k, 0:n_tok], dst_lo[:, k, 0:n_tok], dst_free))
                buffer_free[i] = marks[-1] + [value]
            free[r] = [last]
            return marks

        def causal_or_centred(src, y, w_col, w0, shifts, mark, y_free, bias=None):
            centre = shifts.index(0)
            w = col(w_col, w0 + centre)
            if bias is None:
                m = act.do(lambda e: e.activation(y, src, ACT.Copy, scale=w), mark, y_free)
            else:
                m = act.do(lambda e: e.activation(y, src, ACT.Identity, scale=w, bias=bias), mark, y_free)
            for i, s in enumerate(shifts):
                if s == 0:
                    continue
                w = col(w_col, w0 + i)
                to, frm = (slice(-s, T), slice(0, T + s)) if s < 0 else (slice(0, T - s), slice(s, T))
                m = dve.do(lambda e: e.scalar_tensor_tensor(out=y[:, to], in0=src[:, frm], scalar=w, in1=y[:, to],
                                                            op0=ALU.mult, op1=ALU.add), mark, m)
            return m

        ada = ExitStack()
        silu_cols = sb(ada, "silu_cols", [P, KC, 2])
        silu_row = sb(ada, "silu_row", [P, D])
        ada_products = sb(ada, "ada_products", [P, D])
        mod_raw = sb(ada, "mod_raw", [P, 6 * KC])
        mod_ctx = sb(ada, "mod_ctx", [P, 2 * KC])
        gain_ctx = sb(ada, "gain_ctx", [P, KC])

        mixer = ExitStack()
        k_loc = sb(mixer, "k_loc", [P, AC, T])
        q_loc = sb(mixer, "q_loc", [P, AC, T])
        k_ctx = sb(mixer, "k_ctx", [P, AC, CTX])
        v_loc = sb(mixer, "v_loc", [P, CBLK, ATT])
        v_mid = sb(mixer, "v_mid", [P, CBLK - 1, ATT])
        v_ctx = sb(mixer, "v_ctx", [P, CT, ATT])
        cv_in = sb(mixer, "cv_in", [P, CC, T + 2 * PAD])
        cv_acc = sb(mixer, "cv_acc", [P, CC, T])
        sg_out = sb(mixer, "sg_out", [P, SC, T])
        sg_v = sb(mixer, "sg_v", [P, TT, SG])
        sg_small = sb(mixer, "sg_small_sb", [P, SC * P + 2 * SG + 4 * P])
        sg_b = sg_small[:, 0:SC * P].rearrange("p (s t) -> p s t", s=SC)
        sg_norm_g = sg_small[:, SC * P:SC * P + SG]
        sg_norm_b = sg_small[:, SC * P + SG:SC * P + 2 * SG]
        sg_wT = sg_small[:, SC * P + 2 * SG:SC * P + 2 * SG + 4 * P].rearrange("p (g t) -> p g t", g=4)
        stats = sb(mixer, "stats", [P, 8])
        cv_scratch = sb(mixer, "cv_scratch", [P, CC, T])

        context = ExitStack()
        xc = sb(context, "xc", [P, KC, CTX])
        hc_hi = sb(context, "hc_hi", [P, KC, CTX], F32R)
        hc_lo = sb(context, "hc_lo", [P, KC, CTX], F32R)

        xc_in = pool.load(counter("s_xc"), xc[:, :, :], io["ctx"])
        c_row_in = pool.load(counter("s_crow"), silu_row[:, :], io["c_row"])
        sg_in = pool.load(counter("s_sg"), sg_small[:, :], io["sg_small"])

        silu_c = [act.do(lambda e: e.activation(silu_cols[:, :, i], cols_of(name), ACT.Silu), cols_in)
                  for i, name in enumerate(("c", "c_ctx"))]
        silu_r = act.do(lambda e: e.activation(silu_row[:, :], silu_row[:, :], ACT.Silu), c_row_in)

        norm1, norm_ctx = Norm(T), Norm(CTX)
        for k in range(KC):
            norm1.square(x[:, k, :], x_in[k // 2])
            norm1.sum()
        for k in range(KC):
            norm_ctx.square(xc[:, k, :], xc_in)
            norm_ctx.sum()

        ada_bank = banks.take()
        ada_v = bank[ada_bank][:, 0:4 * KC].rearrange("p (j c) -> p j c", c=2)
        ada_marks, row_free = {}, [None]

        def ada_product(tile, j, mark):
            def mm(e):
                for k in range(KC):
                    m = e.matmul(ada_v[:, j, :], tile[:, k * P:(k + 1) * P], silu_cols[:, k, :],
                                 start=(k == 0), stop=(k == KC - 1))
                return m
            ada_marks[j] = pe.do(mm, mark, silu_c)
            return ada_marks[j]

        def ada_row(tile, j, mark):
            ada_marks[j] = dve.do(lambda e: e.tensor_tensor_reduce(
                out=ada_products[:, :], in0=tile, in1=silu_row[:, :], scale=1.0, scalar=0.0, op0=ALU.mult,
                op1=ALU.add, accum_out=mod_raw[:, j:j + 1]), mark, silu_r, row_free[0])
            row_free[0] = ada_marks[j]
            return ada_marks[j]

        stream.takers = {"ada_product": ada_product, "ada_row": ada_row}
        for _ in range(2 * KC):
            stream.prepare_next()
        ada_b = cols_of("ada_b")
        first = [ada_marks[2 * KC - 1], cols_in]
        mod_c = dve.do(lambda e: e.tensor_tensor(mod[:, 0:2 * KC], ada_v[:, :, 0], ada_b[:, 0:2 * KC], ALU.add), first)
        mod_x = dve.do(lambda e: e.tensor_tensor(mod_ctx[:, :], ada_v[:, :, 1], ada_b[:, 0:2 * KC], ALU.add), first)
        free[ada_bank] = [mod_x]
        gain_m = dve.do(lambda e: e.scalar_tensor_tensor(out=gain[:, :], in0=mod[:, KC:2 * KC], scalar=1.0,
                                                         in1=cols_of("norm1_g"), op0=ALU.add, op1=ALU.mult), mod_c)
        gain_x = dve.do(lambda e: e.scalar_tensor_tensor(out=gain_ctx[:, :], in0=mod_ctx[:, KC:2 * KC], scalar=1.0,
                                                         in1=cols_of("norm1_g"), op0=ALU.add, op1=ALU.mult), mod_x)
        h_marks = apply_norm(norm1, lambda k: x[:, k, :], [x_in[k // 2] for k in range(KC)], T,
                             lambda k: gain[:, k:k + 1], lambda k: mod[:, k:k + 1], gain_m, h_hi, h_lo, None)
        hc_marks = apply_norm(norm_ctx, lambda k: xc[:, k, :], [xc_in] * KC, CTX,
                              lambda k: gain_ctx[:, k:k + 1], lambda k: mod_ctx[:, k:k + 1], gain_x, hc_hi, hc_lo, None)

        pads = [dve.do(lambda e: e.memset(cv_in[:, :, s], 0.0)) for s in (slice(0, PAD), slice(PAD + T, T + 2 * PAD))]
        cv_mark, cv_taps = [None] * CC, [0] * CC
        for c in range(CC):
            ba, ma = linear(1, KC, h_hi, h_lo, h_marks)
            bg, mg = linear(1, KC, h_hi, h_lo, h_marks)
            dst = cv_in[:, c, PAD:PAD + T]
            sig = act.do(lambda e: e.activation(dst, bank[bg][:, :], ACT.Sigmoid), mg)
            cv_mark[c] = dve.do(lambda e: e.tensor_tensor(dst, bank[ba][:, :], dst, ALU.mult), ma, sig)
            free[bg], free[ba] = [sig], [cv_mark[c]]

        def conv_taps(n):
            for c, q in ((0, dve), (1, pool)):
                for i in range(cv_taps[c], min(cv_taps[c] + n, TAPS)):
                    src, w, acc = cv_in[:, c, i:i + T], col("cv_w", c * TAPS + i), cv_acc[:, c, :]
                    if i and q is pool:
                        part = squares[:, i % 2, :]
                        m = pool.do(lambda e: e.tensor_scalar(part, src, w, 0.0, ALU.mult, ALU.add), cv_mark[c], square_free[i % 2])
                        cv_mark[c] = pool.do(lambda e: e.tensor_tensor(acc, acc, part, ALU.add), m)
                        square_free[i % 2] = [cv_mark[c]]
                        continue
                    if i == 0:
                        step = lambda e: e.tensor_scalar(acc, src, w, col("cv_b", c), ALU.mult, ALU.add)
                    else:
                        step = lambda e: e.scalar_tensor_tensor(out=acc, in0=src, scalar=w, in1=acc, op0=ALU.mult, op1=ALU.add)
                    cv_mark[c] = q.do(step, cv_mark[c], pads, cols_in)
                cv_taps[c] = min(cv_taps[c] + n, TAPS)

        vb = [banks.take() for _ in range(TT)]
        v_marks = [None] * TT
        for tile in range(SG * D // (P * SLOT)):
            s, w_marks, (k0, n) = stream.next_tile()
            for t in range(TT):
                def mm(e):
                    for j in range(n):
                        k, w, tok = k0 + j, slice(j * SG, (j + 1) * SG), slice(t * P, (t + 1) * P)
                        m = product(e, bank[vb[t]][:, 0:SG], h_hi[:, k, tok], h_lo[:, k, tok], w_hi[:, s, w],
                                    w_lo[:, s, w], k == 0, k == KC - 1)
                    return m
                v_marks[t] = pe.do(mm, w_marks, h_marks, free[vb[t]] if tile == 0 else None)
            stream.split_free[s] = [v_marks[-1]]
            conv_taps(2)
        sg_v_ready, before = [], None
        for t in range(TT):
            v = sg_v[:, t, :]
            m = act.do(lambda e: e.activation(v, bank[vb[t]][:, 0:SG], ACT.Gelu_apprx_tanh, accum_out=stats[:, 0:1]),
                       v_marks[t], before)
            free[vb[t]] = [m]
            m = dve.do(lambda e: e.tensor_scalar(stats[:, 1:2], stats[:, 0:1], 1.0 / SG, None, ALU.mult), m)
            m = dve.do(lambda e: e.tensor_scalar(v, v, stats[:, 1:2], None, ALU.subtract), m)
            m = act.do(lambda e: e.activation(cv_scratch[:, 0, 0:SG], v, ACT.Square, accum_out=stats[:, 2:3]), m)
            m = act.do(lambda e: e.activation(stats[:, 3:4], stats[:, 2:3], ACT.Sqrt, scale=1.0 / SG, bias=col("eps")), m)
            m = dve.do(lambda e: e.reciprocal(stats[:, 4:5], stats[:, 3:4]), m)
            m = dve.do(lambda e: e.scalar_tensor_tensor(out=v, in0=v, scalar=stats[:, 4:5], in1=sg_norm_g, op0=ALU.mult,
                                                        op1=ALU.mult), m, sg_in)
            before = dve.do(lambda e: e.tensor_tensor(v, v, sg_norm_b, ALU.add), m)
            sg_v_ready.append(before)

        q_marks, k_marks, kc_marks = [None] * AC, [None] * AC, [None] * AC
        for c in range(AC):
            b, bc = banks.take(), banks.take()
            s, w_marks, _ = stream.next_tile()

            def mm(e):
                for rhs_hi, rhs_lo, dst in ((h_hi, h_lo, bank[b][:, :]), (hc_hi, hc_lo, bank[bc][:, 0:CTX])):
                    for k in range(KC):
                        w = slice(k * P, (k + 1) * P)
                        m = product(e, dst, w_hi[:, s, w], w_lo[:, s, w], rhs_hi[:, k, :], rhs_lo[:, k, :], k == 0, k == KC - 1)
                return m
            m = pe.do(mm, w_marks, h_marks, hc_marks, free[b], free[bc])
            stream.split_free[s] = [m]
            k_marks[c] = act.do(lambda e: e.activation(k_loc[:, c, :], bank[b][:, :], ACT.Copy), m)
            kc_marks[c] = act.do(lambda e: e.activation(k_ctx[:, c, :], bank[bc][:, 0:CTX], ACT.Copy), m)
            free[b], free[bc] = [k_marks[c]], [kc_marks[c]]
            conv_taps(2)

        vb = [banks.take() for _ in range(TT + CT)]
        v_marks = [None] * len(vb)
        for tile in range(ATT * D // (P * SLOT)):
            s, w_marks, (k0, n) = stream.next_tile()
            for t in range(len(vb)):
                own_hi, own_lo = (h_hi, h_lo) if t < TT else (hc_hi, hc_lo)
                tok = slice(t % TT * P, (t % TT + 1) * P)

                def mm(e):
                    for j in range(n):
                        k, w = k0 + j, slice(j * ATT, (j + 1) * ATT)
                        m = product(e, bank[vb[t]][:, :], own_hi[:, k, tok], own_lo[:, k, tok], w_hi[:, s, w],
                                    w_lo[:, s, w], k == 0, k == KC - 1)
                    return m
                v_marks[t] = pe.do(mm, w_marks, h_marks, hc_marks, free[vb[t]] if tile == 0 else None)
            stream.split_free[s] = [v_marks[-1]]
            conv_taps(2)
        v_rows = q_loc
        for t in range(len(vb)):
            dst = v_rows[:, t, :] if t < TT else v_ctx[:, t - TT, :]
            v_marks[t] = act.do(lambda e: e.activation(dst, bank[vb[t]][:, :], ACT.Copy), v_marks[t])
            free[vb[t]] = [v_marks[t]]

        v_moved = counter("s_v_moved")
        for tiles, n_tiles, shift in ((v_loc, CBLK, 0), (v_mid, CBLK - 1, WIN // 2)):
            for j in range(n_tiles):
                for r in range(ROWS):
                    p0 = (r % 2) * GRID_W + WIN * j + shift
                    moved = sync.load(v_moved, tiles[r * WIN:(r + 1) * WIN, j, :], v_rows[p0:p0 + WIN, r // 2, :],
                                      v_marks[r // 2])

        context.close()
        handed = everyone()
        attention = ExitStack()
        rel = sb(attention, "rel", [P, HEADS, WINDOW])
        biased = sb(attention, "biased", [P, len(SPAN_OFFS), HEADS, SPAN // WIN, ROWS, WIN])
        rel_in = sync.load(counter("s_rel"), rel[:, :, :], io["rel_rows"], handed)

        sg_u, sg_done = [], []
        for c in range(SC):
            b, m = linear(1, KC, h_hi, h_lo, h_marks)
            sg_u.append(act.do(lambda e: e.activation(sg_out[:, c, :], bank[b][:, :], ACT.Gelu_apprx_tanh), m))
            free[b] = [sg_u[c]]
            conv_taps(3)
        for c in range(SC):
            b = banks.take()

            def mix(e):
                for t in range(TT):
                    for g in (2 * c, 2 * c + 1):
                        p0 = (g % 2) * 64
                        m = e.matmul(bank[b][p0:p0 + 64, t * P:(t + 1) * P], sg_v[:, t, g * 64:(g + 1) * 64],
                                     sg_wT[:, g, :], start=True, stop=True)
                return m
            m = pe.do(mix, sg_v_ready, sg_in, free[b])
            mixed = bank[b][:, :].rearrange("p (t q) -> p t q", t=TT)
            bias = sg_b[:, c, :].unsqueeze(1).to_broadcast([P, TT, P])
            m = dve.do(lambda e: e.tensor_tensor(mixed, mixed, bias, ALU.add), m)
            m = dve.do(lambda e: e.tensor_tensor(sg_out[:, c, :], bank[b][:, :], sg_out[:, c, :], ALU.mult), m, sg_u[c])
            free[b] = [m]
            sg_done.append(m)

        def by_row(a):
            return a.rearrange("p (r b c) -> p r b c", b=CBLK, c=WIN)

        def by_block(a):
            return a.rearrange("p (b r c) -> p r b c", b=CBLK, c=WIN)

        for c in range(AC):
            b, m = linear(1, KC, h_hi, h_lo, h_marks)
            q_marks[c] = act.do(lambda e: e.activation(by_block(q_loc[:, c, :]), by_row(bank[b][:, :]), ACT.Copy, scale=SCALE),
                                m, moved)
            free[b] = [q_marks[c]]
            conv_taps(3)
        h_read = m
        conv_taps(TAPS)

        for v, off in enumerate(SPAN_OFFS):
            hidden = const("window_neg")[:, v * SPAN:(v + 1) * SPAN]
            hidden = hidden.rearrange("p (n c) -> p n c", c=WIN).unsqueeze(1).to_broadcast([P, ROWS, SPAN // WIN, WIN])
            for h in range(HEADS):
                at = WIN + off
                rows = rel[:, h, at:at + ROWS * RPB_W].rearrange("p (r c) -> p r c", c=RPB_W)
                rows = bass.AP(rows.tensor, rows.offset, [rows.ap[0], [RPB_W, ROWS], [WIN, SPAN // WIN], [1, WIN]])
                bias_in = pool.do(lambda e: e.tensor_tensor(
                    biased[:, v, h, :, :, :].rearrange("p n r c -> p r n c"), rows, hidden, ALU.add),
                    rel_in, consts_in, handed)

        mix_marks = [None] * KC
        for c in range(CC):
            acc, y = cv_acc[:, c, :], cv_scratch[:, c, :]
            b = banks.take()
            m = pe.do(lambda e: e.matmul(bank[b][:, :], const("group_mean"), acc, start=True, stop=True),
                      cv_mark[c], consts_in, free[b])
            m = dve.do(lambda e: e.tensor_tensor(acc, acc, bank[b][:, :], ALU.subtract), m)
            m = act.do(lambda e: e.activation(y, acc, ACT.Square), m)
            free[b] = [m]
            m = pe.do(lambda e: e.matmul(bank[b][:, :], const("group_mean"), y, start=True, stop=True), m)
            m = act.do(lambda e: e.activation(y, bank[b][:, :], ACT.Sqrt, bias=col("eps")), m)
            free[b] = [m]
            m = dve.do(lambda e: e.reciprocal(y, y), m)
            m = dve.do(lambda e: e.tensor_tensor(acc, acc, y, ALU.mult), m)
            m = act.do(lambda e: e.activation(acc, acc, ACT.Silu, scale=col("cv_norm_g", c), bias=col("cv_norm_b", c)), m)
            k = AC + SC + c
            mix_marks[k] = split(acc, m, h_hi[:, k, :], h_lo[:, k, :], h_read)
        for c in range(SC):
            k = AC + c
            mix_marks[k] = split(sg_out[:, c, :], sg_done[c], h_hi[:, k, :], h_lo[:, k, :], h_read)

        probs, probs_t = normed, exact
        soft = sb(attention, "soft", [P, 2, 4])
        steps = [(h, b) for h in range(HEADS) for b in range(CBLK)]
        probs_free, probs_t_free = [handed, handed], [handed, handed]
        normalised, copied = {}, {}

        def scores(i):
            h, b = steps[i]
            c, part, u = h // 2, slice((h % 2) * HD, (h % 2 + 1) * HD), i % 2
            keys = slice(SPAN_START[b], SPAN_START[b] + SPAN)
            q = q_loc[part, c, b * P:(b + 1) * P]
            kl = k_loc[part, c, :].rearrange("p (r c) -> p r c", c=GRID_W)[:, :, keys]
            kl = kl.rearrange("p r (n c) -> p n r c", c=WIN)
            S = bank[u]
            local = S[:, 0:ROWS * SPAN]

            def mm(e):
                e.matmul(local, q, kl, start=True, stop=True)
                return e.matmul(S[:, ROWS * SPAN:T], q, k_ctx[part, c, :], start=True, stop=True)
            m = pe.do(mm, q_marks[c], k_marks[c], kc_marks[c], free[u])
            v = SPAN_OFFS.index(SPAN_START[b] - WIN * b)
            m = dve.do(lambda e: e.tensor_tensor(local, local, biased[:, v, h, :, :, :].rearrange("p n r c -> p (n r c)"), ALU.add), m, bias_in)
            m = dve.do(lambda e: e.reduce_max(soft[:, u, 0:1], S[:, :], AX.X), m, probs_free[u])
            m = dve.do(lambda e: e.tensor_scalar(soft[:, u, 1:2], soft[:, u, 0:1], -1.0, None, ALU.mult), m)
            m = act.do(lambda e: e.activation(probs[:, u, :], S[:, :], ACT.Exp, bias=soft[:, u, 1:2],
                                              accum_out=soft[:, u, 2:3]), m, probs_free[u])
            free[u] = [m]
            m = dve.do(lambda e: e.reciprocal(soft[:, u, 3:4], soft[:, u, 2:3]), m)
            normalised[i] = dve.do(lambda e: e.tensor_scalar(probs[:, u, :], probs[:, u, :], soft[:, u, 3:4], None,
                                                             ALU.mult), m)

        def turn_over(i):
            u = i % 2
            B = bank[2 + u]

            def mm(e):
                for n in range(T // P):
                    m = e.transpose(B[:, n * P:(n + 1) * P], probs[:, u, n * P:(n + 1) * P], identity)
                return m
            m = pe.do(mm, normalised[i], free[2 + u])
            probs_free[u] = [m]
            copied[i] = act.do(lambda e: e.activation(probs_t[:, u, :], B[:, :], ACT.Copy), m, probs_t_free[u])
            free[2 + u] = [copied[i]]

        def weighted(i):
            h, b = steps[i]
            c, p0, u = h // 2, (h % 2) * HD, i % 2
            ob = 4 + c % 2
            tiles = v_loc if SPAN_START[b] % WIN == 0 else v_mid
            values = [tiles[:, SPAN_START[b] // WIN + n, :] for n in range(2)] + [v_ctx[:, n, :] for n in range(CT)]

            def mm(e):
                for n, v in enumerate(values):
                    m = e.matmul(bank[ob][p0:p0 + HD, b * P:(b + 1) * P], v[:, h * HD:(h + 1) * HD],
                                 probs_t[:, u, n * P:(n + 1) * P], start=(n == 0), stop=(n == len(values) - 1))
                return m
            m = pe.do(mm, copied[i], v_marks, moved, free[ob] if (h % 2, b) == (0, 0) else None)
            probs_t_free[u] = [m]
            if (h % 2, b) == (1, CBLK - 1):
                mix_marks[c] = split(by_block(bank[ob][:, :]), m, by_row(h_hi[:, c, :]), by_row(h_lo[:, c, :]), h_read)
                free[ob] = [mix_marks[c][1]]

        for i in range(len(steps) + 2):
            if i < len(steps):
                scores(i)
            if 1 <= i <= len(steps):
                turn_over(i - 1)
            if 2 <= i:
                weighted(i - 2)
        attention.close()
        mixer.close()

        while stream.order[stream.prepared][0] != "split":
            stream.prepare_next()
        mod_rest = dve.do(lambda e: e.tensor_tensor(mod[:, 2 * KC:], mod_raw[:, 2 * KC:], ada_b[:, 2 * KC:], ALU.add),
                          [ada_marks[j] for j in range(2 * KC, 6 * KC)])
        gain_m = dve.do(lambda e: e.scalar_tensor_tensor(out=gain[:, :], in0=mod[:, 4 * KC:5 * KC], scalar=1.0,
                                                         in1=cols_of("norm2_g"), op0=ALU.add, op1=ALU.mult), mod_rest)
        ada.close()

        def add_to_x(n_tiles, k_total, src_hi, src_lo, src_marks, gate_at, norm):
            marks = []
            for o in range(KC):
                b, m = linear(n_tiles, k_total, src_hi, src_lo, src_marks)
                g = mod[:, gate_at + o:gate_at + o + 1]
                marks.append(dve.do(lambda e: e.scalar_tensor_tensor(
                    out=x[:, o, :], in0=bank[b][:, :], scalar=g, in1=x[:, o, :], op0=ALU.mult, op1=ALU.add), m, mod_rest))
                free[b] = [marks[o]]
                norm.square(x[:, o, :], marks[o])
                if o:
                    norm.sum()
            return marks

        buffer_free[:] = [everyone(), everyone()]
        norm2 = Norm(T)
        x_marks = add_to_x(1, KC, h_hi, h_lo, mix_marks, 2 * KC, norm2)
        h_marks = apply_norm(norm2, lambda k: x[:, k, :], x_marks, T, lambda k: gain[:, k:k + 1],
                             lambda k: mod[:, 3 * KC + k:3 * KC + k + 1], gain_m, h_hi, h_lo, (pe.sem, pe.count))

        ffn = ExitStack()
        a_hi = sb(ffn, "a_hi", [P, FC, T], F32R)
        a_lo = sb(ffn, "a_lo", [P, FC, T], F32R)
        handed = everyone()
        work_free = [handed, handed]
        a_marks = [None] * FC
        for f in range(FC):
            bg, mg = linear(1, KC, h_hi, h_lo, h_marks)
            bu, mu = linear(1, KC, h_hi, h_lo, h_marks)
            y = normed[:, f % 2, :]
            m = causal_or_centred(bank[bg][:, :], y, "ffn_conv_w", 3 * f, (-1, 0, 1), mg, work_free[f % 2], col("ffn_conv_b", f))
            free[bg] = [m]
            m = act.do(lambda e: e.activation(y, y, ACT.Silu), m)
            m = dve.do(lambda e: e.tensor_tensor(y, bank[bu][:, :], y, ALU.mult), m, mu)
            free[bu] = [m]
            a_marks[f] = split(y, m, a_hi[:, f, :], a_lo[:, f, :], handed)
            work_free[f % 2] = a_marks[f]
        norm_f = Norm(T)
        x_marks = add_to_x(3, FC, a_hi, a_lo, a_marks, 5 * KC, norm_f)
        ffn.close()

        r, m = norm_f.finish()
        norm3 = Norm(T)
        for k in range(KC):
            g = col("final_norm_g", k)
            x_marks[k] = dve.do(lambda e: e.scalar_tensor_tensor(out=x[:, k, :], in0=x[:, k, :], scalar=g,
                                                                 in1=bank[r][:, :], op0=ALU.mult, op1=ALU.mult), m, x_marks[k])
            norm3.square(x[:, k, :], x_marks[k])
            norm3.sum()
        free[r] = [x_marks[-1]]

        buffer_free[:] = [everyone(), everyone()]
        h_marks = apply_norm(norm3, lambda k: x[:, k, :], x_marks, T, lambda k: col("norm_mix_pre_2", k), None, None,
                             h_hi, h_lo, (pe.sem, pe.count))
        branch = ExitStack()
        att_hi = sb(branch, "att_hi", [P, AC, T], F32R)
        att_lo = sb(branch, "att_lo", [P, AC, T], F32R)
        cnv_hi = sb(branch, "cnv_hi", [P, AC, T], F32R)
        cnv_lo = sb(branch, "cnv_lo", [P, AC, T], F32R)
        stick = ExitStack()
        q2 = sb(stick, "q2", [P, AC, T])
        k2 = sb(stick, "k2", [P, AC, T])
        v2 = sb(stick, "v2", [P, TT, ATT])
        NZ = sum(T - P * j for j in range(TT))
        z = sb(stick, "z", [P, 3, NZ])
        sp = sb(stick, "sp", [P, 3, NZ])
        handed = everyone()

        qk_marks = []
        for c in range(2 * AC):
            b, m = linear(1, KC, h_hi, h_lo, h_marks)
            dst, scale = (q2[:, c, :], SCALE) if c < AC else (k2[:, c - AC, :], 1.0)
            qk_marks.append(act.do(lambda e: e.activation(dst, bank[b][:, :], ACT.Copy, scale=scale), m, handed))
            free[b] = [qk_marks[c]]
        vb = [banks.take() for _ in range(TT)]
        v_marks = [None] * TT
        for tile in range(ATT * D // (P * SLOT)):
            s, w_marks, (k0, n) = stream.next_tile()
            for t in range(TT):
                def mm(e):
                    for j in range(n):
                        k, w, tok = k0 + j, slice(j * ATT, (j + 1) * ATT), slice(t * P, (t + 1) * P)
                        m = product(e, bank[vb[t]][:, :], h_hi[:, k, tok], h_lo[:, k, tok], w_hi[:, s, w], w_lo[:, s, w],
                                    k == 0, k == KC - 1)
                    return m
                v_marks[t] = pe.do(mm, w_marks, h_marks, free[vb[t]] if tile == 0 else None)
            stream.split_free[s] = [v_marks[-1]]
        for t in range(TT):
            v_marks[t] = act.do(lambda e: e.activation(v2[:, t, :], bank[vb[t]][:, :], ACT.Copy), v_marks[t], handed)
            free[vb[t]] = [v_marks[t]]

        cnv_marks, work_free = [None] * AC, [[handed], [handed]]
        for c in range(AC):
            bc, mc = linear(1, KC, h_hi, h_lo, h_marks)
            bx, mx = linear(1, KC, h_hi, h_lo, h_marks)
            bb, mb = linear(1, KC, h_hi, h_lo, h_marks)
            u, y = normed[:, c % 2, :], exact[:, c % 2, :]
            m = act.do(lambda e: e.activation(u, bank[bc][:, :], ACT.Copy), mc, work_free[c % 2])
            free[bc] = [m]
            m = dve.do(lambda e: e.tensor_tensor(u, bank[bx][:, :], u, ALU.mult), mx, m)
            free[bx] = [m]
            m = causal_or_centred(u, y, "conv_mix_w_2", 3 * c, (-2, -1, 0), m, work_free[c % 2])
            m = dve.do(lambda e: e.tensor_tensor(y, bank[bb][:, :], y, ALU.mult), m, mb)
            free[bb] = [m]
            cnv_marks[c] = split(y, m, cnv_hi[:, c, :], cnv_lo[:, c, :], handed)
            work_free[c % 2] = [cnv_marks[c]]

        DIAG = [slice(j * P, (j + 1) * P) for j in range(TT)]
        OFF_AT = [T, T + 3 * P, T + 5 * P]

        def off(j, q_from, q_to=TT):
            return slice(OFF_AT[j] + (q_from - j - 1) * P, OFF_AT[j] + (q_to - j - 1) * P)

        PARTS = [(0, slice(0, T), 0), (1, slice(T, T + 3 * P), 0), (1, slice(T + 5 * P, NZ), 3 * P), (2, slice(T + 3 * P, T + 5 * P), 0)]

        def where(columns):
            for n, part, at in PARTS:
                if part.start <= columns.start and columns.stop <= part.stop:
                    return n, slice(columns.start - part.start + at, columns.stop - part.start + at)

        z_free, z_ready, w_ready = [handed] * 3, {}, {}
        att_marks = [None] * AC

        def stick_scores(h):
            c, part, u = h // 2, slice((h % 2) * HD, (h % 2 + 1) * HD), h % 3

            def mm(e):
                for j in range(TT):
                    keys = k2[part, c, j * P:(j + 1) * P]
                    m = e.matmul(bank[0][:, DIAG[j]], keys, q2[part, c, j * P:(j + 1) * P], start=True, stop=True)
                    if j < TT - 1:
                        n, at = where(off(j, j + 1))
                        m = e.matmul(bank[n][:, at], keys, q2[part, c, (j + 1) * P:T], start=True, stop=True)
                return m
            m = pe.do(mm, qk_marks[c], qk_marks[AC + c], free[0], free[1], free[2])
            hidden = const("causal_neg").unsqueeze(1).to_broadcast([P, TT, P])
            d = dve.do(lambda e: e.tensor_tensor(z[:, u, 0:T].rearrange("p (t q) -> p t q", t=TT),
                                                 bank[0][:, :].rearrange("p (t q) -> p t q", t=TT), hidden, ALU.add),
                       m, z_free[u])
            free[0] = [d]
            for n, part_, at in PARTS[1:]:
                o = act.do(lambda e: e.activation(z[:, u, part_], bank[n][:, at:at + part_.stop - part_.start], ACT.Copy),
                           m, z_free[u])
                free[n] = [o]
            zz, ss = z[:, u, :], sp[:, u, :]
            m = act.do(lambda e: e.activation(ss, zz, ACT.Abs), d, o, z_free[u])
            m = act.do(lambda e: e.activation(ss, ss, ACT.Exp, scale=-1.0), m)
            m = act.do(lambda e: e.activation(ss, ss, ACT.Ln, bias=col("one")), m)
            z_ready[h] = dve.do(lambda e: e.scalar_tensor_tensor(out=ss, in0=zz, scalar=0.0, in1=ss, op0=ALU.max,
                                                                 op1=ALU.add), m, d, o)

        def stick_weights(h):
            u = h % 3
            tri, all_ = const("minus_tri"), const("minus_ones")
            s = sp[:, u, :]

            def mm(e):
                e.matmul(bank[3][:, :], tri, s[:, 0:T], start=True, stop=True)
                m = None
                for j in range(TT - 1):
                    own = off(j, j + 1)
                    n, at = where(own)
                    e.matmul(bank[3 + n][:, at], tri, s[:, own], start=True, stop=False)
                    for i in range(j + 1, TT):
                        dn, dat = where(off(j, i, i + 1))
                        m = e.matmul(bank[3 + dn][:, dat], all_, s[:, DIAG[i]], start=False, stop=(i == TT - 1))
                        if i < TT - 1:
                            dn, dat = where(off(j, i + 1))
                            m = e.matmul(bank[3 + dn][:, dat], all_, s[:, off(i, i + 1)], start=False, stop=False)
                return m
            m = pe.do(mm, z_ready[h], free[3], free[4], free[5])
            for n, part, at in PARTS:
                a = dve.do(lambda e: e.tensor_tensor(z[:, u, part], z[:, u, part],
                                                     bank[3 + n][:, at:at + part.stop - part.start], ALU.add), m)
                free[3 + n] = [a]
            w_ready[h] = act.do(lambda e: e.activation(z[:, u, :], z[:, u, :], ACT.Exp), a)

        def stick_values(h):
            c, p0, u = h // 2, (h % 2) * HD, h % 3
            ob = NORM_BANKS[c % 2]

            def mm(e):
                for j in range(TT):
                    v = v2[:, j, h * HD:(h + 1) * HD]
                    m = e.matmul(bank[ob][p0:p0 + HD, DIAG[j]], v, z[:, u, DIAG[j]], start=(j == 0), stop=(j == TT - 1),
                                 skip_group_check=True)
                    if j < TT - 1:
                        m = e.matmul(bank[ob][p0:p0 + HD, (j + 1) * P:T], v, z[:, u, off(j, j + 1)], start=False,
                                     stop=False, skip_group_check=True)
                return m
            m = pe.do(mm, w_ready[h], v_marks, free[ob] if h % 2 == 0 else None)
            z_free[u] = [m]
            if h % 2:
                att_marks[c] = split(bank[ob][:, :], m, att_hi[:, c, :], att_lo[:, c, :])
                free[ob] = [att_marks[c][1]]

        for h in range(HEADS + 2):
            if h < HEADS:
                stick_scores(h)
            if 1 <= h <= HEADS:
                stick_weights(h - 1)
            if 2 <= h:
                stick_values(h - 2)
        stick.close()

        merge = ExitStack()
        m_hi = sb(merge, "m_hi", [P, KC, T], F32R)
        m_lo = sb(merge, "m_lo", [P, KC, T], F32R)
        handed = everyone()
        m_marks, work_free = [None] * KC, [[handed], [handed]]
        for o in range(KC):
            i = o % 2
            ga, ma = linear(1, KC, h_hi, h_lo, h_marks)
            gc, mc = linear(1, KC, h_hi, h_lo, h_marks)
            ya, na = linear(1, AC, att_hi, att_lo, att_marks)
            yc, nc_ = linear(1, AC, cnv_hi, cnv_lo, cnv_marks)
            u, y = normed[:, i, :], exact[:, i, :]
            sa = act.do(lambda e: e.activation(u, bank[ga][:, :], ACT.Sigmoid), ma, work_free[i])
            sc = act.do(lambda e: e.activation(y, bank[gc][:, :], ACT.Sigmoid), mc, work_free[i])
            pa = dve.do(lambda e: e.tensor_tensor(u, bank[ya][:, :], u, ALU.mult), na, sa)
            pc = dve.do(lambda e: e.tensor_tensor(y, bank[yc][:, :], y, ALU.mult), nc_, sc)
            free[ga], free[gc], free[ya], free[yc] = [sa], [sc], [pa], [pc]
            both = dve.do(lambda e: e.tensor_tensor(u, u, y, ALU.add), pa, pc)
            m_marks[o] = split(u, both, m_hi[:, o, :], m_lo[:, o, :], handed)
            work_free[i] = [m_marks[o]]

        def normed_into_x(y_buf, n_tiles, k_total, src_hi, src_lo, src_marks, gain_name, y_free, next_norm):
            norm, y_marks, marks = Norm(T), [], []
            for o in range(KC):
                b, m = linear(n_tiles, k_total, src_hi, src_lo, src_marks)
                y_marks.append(act.do(lambda e: e.activation(y_buf[:, o, :], bank[b][:, :], ACT.Copy), m, y_free))
                free[b] = [y_marks[o]]
                norm.square(y_buf[:, o, :], y_marks[o])
                if o:
                    norm.sum()
            r, m = norm.finish()
            for k in range(KC):
                y, g = y_buf[:, k, :], col(gain_name, k)
                n = dve.do(lambda e: e.scalar_tensor_tensor(out=y, in0=y, scalar=g, in1=bank[r][:, :], op0=ALU.mult,
                                                            op1=ALU.mult), m, y_marks[k])
                marks.append(dve.do(lambda e: e.tensor_tensor(x[:, k, :], x[:, k, :], y, ALU.add), n))
                if next_norm:
                    next_norm.square(x[:, k, :], marks[k])
                    next_norm.sum()
            free[r] = [n]
            return marks

        y_buf = sb(merge, "y_buf", [P, KC, T])
        norm4 = Norm(T)
        x_marks = normed_into_x(y_buf, 1, KC, m_hi, m_lo, m_marks, "norm_mix_post_2", handed, norm4)
        merge.close()
        branch.close()
        buffer_free[:] = [everyone(), everyone()]
        h_marks = apply_norm(norm4, lambda k: x[:, k, :], x_marks, T, lambda k: col("norm_ffn_pre_2", k), None, None,
                             h_hi, h_lo, (pe.sem, pe.count))

        ffn = ExitStack()
        a_hi = sb(ffn, "a2_hi", [P, FC, T], F32R)
        a_lo = sb(ffn, "a2_lo", [P, FC, T], F32R)
        y_buf = sb(ffn, "y2_buf", [P, KC, T])
        handed = everyone()
        work_free = [[handed], [handed]]
        for f in range(FC):
            ba, ma = linear(1, KC, h_hi, h_lo, h_marks)
            bg, mg = linear(1, KC, h_hi, h_lo, h_marks)
            u, y = normed[:, f % 2, :], exact[:, f % 2, :]
            m1 = causal_or_centred(bank[ba][:, :], u, "conv_ffn_w_2", 3 * f, (-2, -1, 0), ma, work_free[f % 2])
            m2 = causal_or_centred(bank[bg][:, :], y, "conv_ffn_w_2", 3 * (FC + f), (-2, -1, 0), mg, work_free[f % 2])
            free[ba], free[bg] = [m1], [m2]
            m2 = act.do(lambda e: e.activation(y, y, ACT.Gelu_apprx_tanh), m2)
            m = dve.do(lambda e: e.tensor_tensor(u, u, y, ALU.mult), m1, m2)
            a_marks[f] = split(u, m, a_hi[:, f, :], a_lo[:, f, :], handed)
            work_free[f % 2] = [a_marks[f], m]
        x_marks = normed_into_x(y_buf, 3, FC, a_hi, a_lo, a_marks, "norm_ffn_post_2", handed, None)
        ffn.close()

        done = counter("s_out")
        for i in range(KC // 2):
            stored = sync.load(done, out[:, 2 * i:2 * i + 2, :], x[:, 2 * i:2 * i + 2, :], x_marks[2 * i + 1])
        sync.wait(stored)


def columns(v):
    return v.reshape(-1, P).T


def tap_columns(w):
    return w.T.reshape(-1, P, w.shape[0]).transpose(1, 0, 2).reshape(P, -1)


def by_feature(v):
    return v.T.reshape(-1, P, v.shape[0]).transpose(1, 0, 2)


def blocks(w):
    k, n = w.shape
    return w.reshape(k // P, P, n // P, P).transpose(2, 1, 0, 3)


def wide(w):
    k, n = w.shape
    per = SLOT // n
    return w.reshape(k // P // per, per, P, n).transpose(0, 2, 1, 3)


def shape_constants():
    i = np.arange(P)
    group = (i[:, None] // HD == i[None, :] // HD) / float(CV // 4)
    tri = -(i[:, None] >= i[None, :]).astype(np.float32)
    causal = np.where(i[:, None] < i[None, :], 0.0, NEG)
    hidden = np.zeros((P, len(SPAN_OFFS), SPAN))
    for b in range(CBLK):
        q = WIN * b + i % WIN
        start = np.clip(q - WIN // 2, 0, GRID_W - WIN)
        key = SPAN_START[b] + np.arange(SPAN)
        inside = (key[None, :] >= start[:, None]) & (key[None, :] < start[:, None] + WIN)
        hidden[:, SPAN_OFFS.index(SPAN_START[b] - WIN * b), :] = np.where(inside, 0.0, NEG)
    return np.concatenate([np.eye(P), group, -np.ones((P, P)), tri, causal, hidden.reshape(P, -1)],
                          axis=1).astype(np.float32)


def laid_out(i):
    w_in, w_in2 = i["w_in"][0], i["w_in_2"][0]
    o_u, o_v, o_a, o_g = 3 * ATT, 3 * ATT + SG, 3 * ATT + 2 * SG, 3 * ATT + 2 * SG + CV
    ada_w = i["ada_w"][0]
    small = {
        "c": columns(i["c"][0]), "c_ctx": columns(i["c_ctx"]), "ada_b": columns(i["ada_b"][0]),
        "norm1_g": columns(i["norm1_g"][0]), "norm2_g": columns(i["norm2_g"][0]),
        "final_norm_g": columns(i["final_norm_g"]), "cv_w": tap_columns(i["cv_w"][0]), "cv_b": columns(i["cv_b"][0]),
        "cv_norm_g": columns(i["cv_norm_g"][0]), "cv_norm_b": columns(i["cv_norm_b"][0]),
        "ffn_conv_w": tap_columns(i["ffn_conv_w"][0]), "ffn_conv_b": columns(i["ffn_conv_b"][0]),
        "norm_mix_pre_2": columns(i["norm_mix_pre_2"][0]), "norm_mix_post_2": columns(i["norm_mix_post_2"][0]),
        "norm_ffn_pre_2": columns(i["norm_ffn_pre_2"][0]), "norm_ffn_post_2": columns(i["norm_ffn_post_2"][0]),
        "conv_mix_w_2": tap_columns(i["conv_mix_w_2"][0]), "conv_ffn_w_2": tap_columns(i["conv_ffn_w_2"][0]),
        "eps": np.full((P, 1), EPS, np.float32), "one": np.ones((P, 1), np.float32),
    }
    rel = np.zeros((HEADS, WIN + (2 * ROWS - 1) * RPB_W + WIN + SPAN), np.float32)
    rel[:, WIN:WIN + (2 * ROWS - 1) * RPB_W] = i["na_rpb"][0].reshape(HEADS, -1)
    starts = [(ROWS - 1 - q // WIN) * RPB_W + WIN - 1 - q % WIN for q in range(P)]
    b_cols, c_cols = blocks(w_in2[:, 3 * ATT:4 * ATT]), blocks(w_in2[:, 4 * ATT:5 * ATT])
    x_cols = blocks(w_in2[:, 5 * ATT:6 * ATT])
    a_blocks, g_blocks = blocks(w_in[:, o_a:o_g]), blocks(w_in[:, o_g:o_g + CV])
    sg_small = np.concatenate([
        np.repeat(i["sg_b"][0], SG // 4, axis=0).reshape(SC, P, P).transpose(1, 0, 2).reshape(P, -1),
        np.broadcast_to(i["sg_norm_g"][0], (P, SG)), np.broadcast_to(i["sg_norm_b"][0], (P, SG)),
        i["sg_w"][0].transpose(2, 0, 1).reshape(P, -1)], axis=1)
    arrays = {
        "x": by_feature(i["x"][0]), "ctx": by_feature(i["ctx"][0]),
        "cols": np.concatenate([small[n] for n, _ in COLUMN_SIZES], axis=1),
        "consts": shape_constants(), "c_row": np.broadcast_to(i["c"][0], (P, D)), "sg_small": sg_small,
        "rel_rows": np.stack([rel[:, s:s + WINDOW] for s in starts]),
        "ada_blocks": blocks(ada_w[:, 0:2 * D]), "ada_rows": ada_w[:, 2 * D:].T.reshape(4 * KC, P, D),
        "w_cv": np.stack([a_blocks, g_blocks], axis=1).reshape(2 * CC, P, KC, P),
        "w_sg_v": wide(w_in[:, o_v:o_a]), "w_sg_u": blocks(w_in[:, o_u:o_v]),
        "w_q": blocks(w_in[:, 0:ATT]), "w_k": blocks(w_in[:, ATT:2 * ATT]), "w_v": wide(w_in[:, 2 * ATT:3 * ATT]),
        "w_out": blocks(i["w_out"][0]), "w_ffn_up": blocks(i["ffn_w_up"][0]), "w_ffn_down": blocks(i["ffn_w_down"][0]),
        "w_qk2": blocks(w_in2[:, 0:2 * ATT]), "w_v2": wide(w_in2[:, 2 * ATT:3 * ATT]),
        "w_conv3": np.stack([c_cols, x_cols, b_cols], axis=1).reshape(3 * AC, P, KC, P),
        "w_gates2": blocks(w_in2[:, 6 * ATT:6 * ATT + 2 * D]),
        "w_att2": blocks(i["w_att_branch_2"][0]), "w_convb2": blocks(i["w_conv_branch_2"][0]),
        "w_out2": blocks(i["w_out_2"][0]), "w_up2": blocks(i["w_up_2"][0]), "w_down2": blocks(i["w_down_2"][0]),
    }
    return {name: np.ascontiguousarray(a) for name, a in arrays.items()}


def kernel(**inputs):
    import concourse.bacc as bacc
    from concourse.bass_utils import run_bass_kernel_spmd

    arrays = laid_out({name: np.asarray(v) for name, v in inputs.items()})
    nc = bacc.Bacc("TRN2", target_bir_lowering=False, num_devices=1)
    io = {name: nc.dram_tensor(f"in_{name}", a.shape, mybir.dt.from_np(a.dtype), kind="ExternalInput").ap()
          for name, a in arrays.items()}
    out = nc.dram_tensor("out_x", (P, KC, T), F32, kind="ExternalOutput").ap()
    two_blocks(nc, io, out)
    result = run_bass_kernel_spmd(nc, [{f"in_{name}": a for name, a in arrays.items()}], core_ids=[0])
    got = result.results[0]["out_x"]
    return np.ascontiguousarray(got.transpose(2, 1, 0).reshape(1, T, D))
```

```python
from contextlib import ExitStack

import numpy as np

import concourse.bass as bass
from concourse import mybir
from concourse.alu_op_type import AluOpType as ALU

F32 = mybir.dt.float32
F32R = mybir.dt.float32r
ACT = mybir.ActivationFunctionType
AX = mybir.AxisListType

P = 128
D = 1024
KC = D // P
T = 512
TT = T // P
CTX = 256
CT = CTX // P
HD = 64
HEADS = 8
ATT = HEADS * HD
AC = ATT // P
SG = 256
SC = SG // P
CV = 256
CC = CV // P
TAPS = 31
PAD = TAPS // 2
DFF = 2816
FC = DFF // P
GRID_W = 64
ROWS = T // GRID_W
WIN = 16
SPAN = 32
GROUP = 8
CBLK = GRID_W // WIN
RPB_W = 31
WINDOW = WIN + (ROWS - 1) * RPB_W + SPAN
SPAN_START = [min(max(WIN * b - WIN // 2, 0), GRID_W - SPAN) for b in range(CBLK)]
SPAN_OFFS = sorted({SPAN_START[b] - WIN * b for b in range(CBLK)}, reverse=True)
SCALE = HD ** -0.5
EPS = 1e-6
NEG = -1e30
SLOT = 1024

COLUMN_SIZES = [
    ("ada_b", 6 * KC), ("norm1_g", KC), ("norm2_g", KC), ("final_norm_g", KC),
    ("cv_w", CC * TAPS), ("cv_b", CC), ("cv_norm_g", CC), ("cv_norm_b", CC),
    ("ffn_conv_w", FC * 3), ("ffn_conv_b", FC),
    ("norm_mix_pre_2", KC), ("norm_mix_post_2", KC), ("norm_ffn_pre_2", KC), ("norm_ffn_post_2", KC),
    ("conv_mix_w_2", AC * 3), ("conv_ffn_w_2", 2 * FC * 3), ("eps", 1), ("one", 1),
]
COLUMNS = {}
_at = 0
for _name, _n in COLUMN_SIZES:
    COLUMNS[_name] = (_at, _n)
    _at += _n
N_COLUMNS = _at

CONST_SIZES = [
    ("identity", P), ("group_mean", P), ("minus_ones", P), ("minus_tri", P), ("causal_neg", P),
    ("window_neg", len(SPAN_OFFS) * SPAN),
]
CONSTS = {}
_at = 0
for _name, _n in CONST_SIZES:
    CONSTS[_name] = (_at, _n)
    _at += _n
N_CONSTS = _at


class Queue:

    def __init__(self, engine, sem):
        self.engine, self.sem, self.count, self.waited = engine, sem, 0, {}

    def wait(self, *after):
        need = {}
        for sem, count in flat(after):
            if count > self.waited.get(sem.num, 0):
                self.waited[sem.num] = count
                need[sem.num] = (sem, count)
        for sem, count in need.values():
            self.engine.wait_ge(sem, count)

    def do(self, step, *after):
        self.wait(*after)
        self.count += 1
        step(self.engine).then_inc(self.sem, 1)
        return (self.sem, self.count)

    def load(self, counter, dst, src, *after):
        self.wait(*after)
        counter[1] += 16
        self.engine.dma_start(dst, src).then_inc(counter[0], 16)
        return (counter[0], counter[1])


def flat(marks):
    out = []
    for m in marks:
        if m is None:
            continue
        out += flat(m) if isinstance(m, list) else [m]
    return out


class Banks:

    def __init__(self, tensors, turning):
        self.tensors, self.free, self.turning, self.at = tensors, [None] * len(tensors), turning, -1

    def take(self):
        self.at = (self.at + 1) % self.turning
        return self.at


class WeightStream:

    RAW, SPLIT = 3, 3

    def __init__(self, order, raw, hi, lo, counters, sync, act, dve):
        self.order, self.raw, self.hi, self.lo, self.counters = order, raw, hi, lo, counters
        self.sync, self.act, self.dve, self.takers = sync, act, dve, {}
        self.raw_free, self.split_free = [None] * self.RAW, [None] * self.SPLIT
        self.arrived, self.ready = {}, {}
        self.loaded = self.prepared = self.n_split = self.next = self.used = 0
        for _ in range(self.RAW):
            self.load_next()

    def load_next(self):
        i = self.loaded
        if i < len(self.order):
            _, src, n, _ = self.order[i]
            slot = i % self.RAW
            dst = self.raw[:, slot, 0:n]
            if len(src.shape) == 3:
                dst = dst.rearrange("p (k n) -> p k n", k=src.shape[1])
            self.arrived[i] = self.sync.load(self.counters[slot], dst, src, self.raw_free[slot])
            self.loaded += 1

    def prepare_next(self):
        i = self.prepared
        kind, _, n, detail = self.order[i]
        slot = i % self.RAW
        tile = self.raw[:, slot, 0:n]
        if kind == "split":
            s = self.n_split % self.SPLIT
            self.n_split += 1
            hi_s, lo_s = self.hi[:, s, 0:n], self.lo[:, s, 0:n]
            hi = self.act.do(lambda e: e.activation(hi_s, tile, ACT.Copy), self.arrived[i], self.split_free[s])
            lo = self.dve.do(lambda e: e.tensor_tensor(lo_s, tile, hi_s.bitcast(F32), ALU.subtract),
                             self.arrived[i], hi, self.split_free[s])
            self.ready[i] = (s, [hi, lo], detail)
            self.raw_free[slot] = [lo]
        else:
            self.raw_free[slot] = [self.takers[kind](tile, detail, self.arrived[i])]
        self.prepared += 1
        self.load_next()

    def prepare_ahead(self):
        while self.prepared < len(self.order) and self.n_split < self.used + self.SPLIT:
            self.prepare_next()

    def next_tile(self, ahead=True):
        if ahead:
            self.prepare_ahead()
        while self.order[self.next][0] != "split":
            self.next += 1
        self.next += 1
        self.used += 1
        return self.ready[self.next - 1]


def two_blocks(nc, io, out):
    with ExitStack() as whole:
        def sb(stack, name, shape, dt=F32):
            return stack.enter_context(nc.sbuf_tensor(name, shape, dt))

        def counter(name):
            return [whole.enter_context(nc.semaphore(name)), 0]

        pe, act, dve, pool, sync = (
            Queue(engine, counter(f"s_{name}")[0])
            for name, engine in (("pe", nc.tensor), ("act", nc.scalar), ("dve", nc.vector), ("pool", nc.gpsimd),
                                 ("sync", nc.sync)))

        def everyone():
            return [(q.sem, q.count) for q in (pe, act, dve, pool)]

        x = sb(whole, "x_res", [P, KC, T])
        h_hi = sb(whole, "h_hi", [P, KC, T], F32R)
        h_lo = sb(whole, "h_lo", [P, KC, T], F32R)
        cols = sb(whole, "cols_sb", [P, N_COLUMNS])
        consts = sb(whole, "consts_sb", [P, N_CONSTS])
        ones = sb(whole, "ones", [P, 1])
        mod = sb(whole, "mod", [P, 6 * KC])
        gain = sb(whole, "gain", [P, KC])
        squares = sb(whole, "squares", [P, 2, T])
        normed = sb(whole, "normed", [P, 2, T])
        exact = sb(whole, "exact", [P, 2, T])
        small = sb(whole, "small", [P, 3 * TT])
        std = sb(whole, "std", [P, 2 * TT])
        rstd = sb(whole, "rstd", [P, 2 * TT])
        raw = sb(whole, "raw_w", [P, WeightStream.RAW, SLOT])
        w_hi = sb(whole, "w_hi", [P, WeightStream.SPLIT, SLOT], F32R)
        w_lo = sb(whole, "w_lo", [P, WeightStream.SPLIT, SLOT], F32R)
        bank = [whole.enter_context(nc.psum_tensor(f"bank{b}", [P, T], F32)) for b in range(8)]
        banks = Banks(bank, 6)
        free = banks.free
        NORM_BANKS = (6, 7)

        def col(name, i=0):
            at = COLUMNS[name][0] + i
            return cols[:, at:at + 1]

        def cols_of(name):
            at, n = COLUMNS[name]
            return cols[:, at:at + n]

        def const(name):
            at, n = CONSTS[name]
            return consts[:, at:at + n]

        identity = const("identity")

        SIDE_BY_SIDE = 2

        def blocks_of(name):
            w = io[name]
            n_out, _, kc, _ = w.shape
            sizes = [kc] if kc <= KC else [8, 7, 7]
            return [[("split", w[o, :, sum(sizes[:i]):sum(sizes[:i + 1]), :], n * P, (sum(sizes[:i]), n))
                     for i, n in enumerate(sizes)] for o in range(n_out)]

        def wide_of(name):
            w = io[name]
            return [[("split", w[t, :, :, :], w.shape[2] * w.shape[3], (t * w.shape[2], w.shape[2]))]
                    for t in range(w.shape[0])]

        def in_turn(plans, extra=(), each=0):
            extra, order = list(extra), []
            for tile in (t for tiles in plans for t in tiles):
                order.append(tile)
                order += extra[:each]
                del extra[:each]
            return order + extra

        order = [("ada_turned", io["ada_turned"][half, k, :, :], SLOT, (half, k)) for half in (1, 0) for k in range(KC)]
        rest = [("ada_rows", io["ada_rows"][j - 2 * KC, :, :], SLOT, j) for j in range(2 * KC, 6 * KC)]
        gated, spatial = blocks_of("w_cv"), blocks_of("w_sg_v") + blocks_of("w_sg_u")
        order += in_turn(gated[:SIDE_BY_SIDE + 1])
        few = len(gated) - SIDE_BY_SIDE - 1 + len(spatial)
        order += in_turn(gated[SIDE_BY_SIDE + 1:] + spatial, rest[:few], 1)
        order += in_turn(blocks_of("w_k") + wide_of("w_v") + blocks_of("w_q")[:1], rest[few:], 3)
        order += in_turn(blocks_of("w_q")[1:])
        for half in (range(AC, KC), range(AC)):
            order += [("split", io["w_out"][o, :, half[0]:half[-1] + 1, :], AC * P, (half[0], AC)) for o in range(KC)]
        up = blocks_of("w_ffn_up")
        order += in_turn([up[i] for f in range(FC) for i in (f, FC + f)])
        order += in_turn(blocks_of("w_ffn_down"))
        order += in_turn(blocks_of("w_qk2") + wide_of("w_v2"))
        order += in_turn(blocks_of("w_conv3"))
        gates, atts, convs = blocks_of("w_gates2"), blocks_of("w_att2"), blocks_of("w_convb2")
        order += in_turn([p for o in range(KC) for p in (gates[o], gates[KC + o], atts[o], convs[o])])
        order += in_turn(blocks_of("w_out2"))
        up = blocks_of("w_up2")
        order += in_turn([up[i] for f in range(FC) for i in (f, FC + f)])
        order += in_turn(blocks_of("w_down2"))

        silu_c = sb(whole, "silu_c", [P, KC, 2])
        c_in = sync.load(counter("s_c"), silu_c[:, :, :], io["c_cols"])
        x_in = [act.load(counter(f"s_x{i}"), x[:, 2 * i:2 * i + 2, :], io["x"][:, 2 * i:2 * i + 2, :])
                for i in range(KC // 2)]
        cols_in = act.load(counter("s_cols"), cols[:, :], io["cols"])
        consts_in = act.load(counter("s_consts"), consts[:, :], io["consts"])
        stream = WeightStream(order, raw, w_hi, w_lo, [counter(f"s_raw{i}") for i in range(WeightStream.RAW)],
                              sync, act, dve)
        ones_set = dve.do(lambda e: e.memset(ones[:, :], 1.0))

        def product(e, dst, lhs_hi, lhs_lo, rhs_hi, rhs_lo, first, last):
            e.matmul(dst, lhs_hi, rhs_lo, start=first, stop=False)
            e.matmul(dst, lhs_lo, rhs_hi, start=False, stop=False)
            return e.matmul(dst, lhs_hi, rhs_hi, start=False, stop=last)

        def linear_steps(b, n_tiles, chunks, src_hi, src_lo, src_marks):
            first, last = min(chunks), max(chunks)
            for _ in range(n_tiles):
                s, w_marks, (k0, n) = stream.next_tile()
                for j in range(n):
                    k, w = k0 + j, slice(j * P, (j + 1) * P)
                    mark = pe.do(lambda e: product(e, bank[b][:, :], w_hi[:, s, w], w_lo[:, s, w], src_hi[:, k, :],
                                                   src_lo[:, k, :], k == first, k == last),
                                 w_marks, src_marks[k], free[b] if k == first else None)
                    if j == n - 1:
                        stream.split_free[s] = [mark]
                    yield
            return b, mark

        def finished(steps):
            while True:
                try:
                    next(steps)
                except StopIteration as end:
                    return end.value

        def linear(n_tiles, k_total, src_hi, src_lo, src_marks):
            return finished(linear_steps(banks.take(), n_tiles, range(k_total), src_hi, src_lo, src_marks))

        def linear_side_by_side(k_total, src_hi, src_lo, src_marks):
            tiles = [stream.next_tile(ahead=(i == 0)) for i in range(SIDE_BY_SIDE)]
            out_banks = [banks.take() for _ in tiles]
            marks = [None] * len(tiles)
            for k in range(k_total):
                w = slice(k * P, (k + 1) * P)
                for i, (s, w_marks, _) in enumerate(tiles):
                    b = out_banks[i]
                    marks[i] = pe.do(lambda e: product(e, bank[b][:, :], w_hi[:, s, w], w_lo[:, s, w], src_hi[:, k, :],
                                                       src_lo[:, k, :], k == 0, k == k_total - 1),
                                     w_marks, src_marks[k], free[b] if k == 0 else None)
            for i, (s, _, _) in enumerate(tiles):
                stream.split_free[s] = [marks[i]]
            return list(zip(out_banks, marks))

        def linears(n, k_total, src_hi, src_lo, src_marks):
            yield from linear_side_by_side(k_total, src_hi, src_lo, src_marks)
            for _ in range(n - SIDE_BY_SIDE):
                yield linear(1, k_total, src_hi, src_lo, src_marks)

        def split(value, mark, dst_hi, dst_lo, dst_free=None):
            hi = act.do(lambda e: e.activation(dst_hi, value, ACT.Copy), mark, dst_free)
            lo = dve.do(lambda e: e.tensor_tensor(dst_lo, value, dst_hi.bitcast(F32), ALU.subtract), mark, hi, dst_free)
            return [hi, lo]

        square_free, buffer_free = [None, None], [None, None]
        turn = {"norm": 0, "square": 0, "buffer": 0}

        class Norm:

            def __init__(self, n_tok, total=None):
                self.n_tok, self.total, self.total_mark = n_tok, total, everyone()
                self.waiting, self.seen, self.summed = None, 0, 0
                self.b = NORM_BANKS[turn["norm"] % 2]
                self.at = (turn["norm"] % 2) * TT
                turn["norm"] += 1

            def square(self, v, mark, scale=1.0):
                self.add_waiting()
                first, self.seen = self.seen == 0, self.seen + 1
                if self.total is not None and first:
                    self.total_mark = act.do(lambda e: e.activation(self.total, v, ACT.Square, scale=scale), mark,
                                             self.total_mark)
                    return
                i = turn["square"] % len(square_free)
                turn["square"] += 1
                m = act.do(lambda e: e.activation(squares[:, i, 0:self.n_tok], v, ACT.Square, scale=scale), mark,
                           square_free[i])
                self.waiting = (i, m)

            def add_waiting(self):
                if self.waiting is not None:
                    (i, m), self.waiting = self.waiting, None
                    part = squares[:, i, 0:self.n_tok]
                    if self.total is None:
                        self.sum_over_partitions(part, m, KC)
                        square_free[i] = [self.mark]
                    else:
                        self.total_mark = dve.do(lambda e: e.tensor_tensor(self.total, self.total, part, ALU.add), m,
                                                 self.total_mark)
                        square_free[i] = [self.total_mark]

            def sum_over_partitions(self, part, mark, parts):
                k, nt = self.summed, self.n_tok // P
                self.summed += 1

                def sums(e):
                    for t in range(nt):
                        mm = e.matmul(bank[self.b][:, t:t + 1], part[:, t * P:(t + 1) * P], ones[:, :],
                                      start=(k == 0 and t == 0), stop=(k == parts - 1 and t == nt - 1),
                                      skip_group_check=True)
                    return mm
                self.mark = pe.do(sums, mark, ones_set, free[self.b] if k == 0 else None)

            def end_of_sums(self):
                self.add_waiting()
                if self.total is not None and not self.summed:
                    self.sum_over_partitions(self.total, self.total_mark, 1)

            def factors(self):
                self.end_of_sums()
                nt, b, at = self.n_tok // P, self.b, self.at
                s, f = std[:, at:at + nt], rstd[:, at:at + nt]
                root = act.do(lambda e: e.activation(s, bank[b][:, 0:nt], ACT.Sqrt, scale=1.0 / D, bias=col("eps")),
                              self.mark, cols_in)
                return f, [dve.do(lambda e: e.reciprocal(f, s), root), root]

            def finish(self):
                f, marks = self.factors()
                return self.b, spread(f, marks, self.b)

        def spread(f, marks, b):
            def mm(e):
                for t in range(f.shape[1]):
                    m = e.matmul(bank[b][:, t * P:(t + 1) * P], f[:, t:t + 1].to_broadcast([P, P]), identity,
                                 start=True, stop=True)
                return m
            return pe.do(mm, marks, consts_in)

        def apply_norm(factor_bank, factor_mark, chunk, chunk_marks, n_tok, a_of, b_of, params, dst_hi, dst_lo, dst_free):
            marks, factor = [], bank[factor_bank][:, 0:n_tok]
            lows, last = [], None
            for k in range(KC):
                i = turn["buffer"] % 2
                turn["buffer"] += 1
                src, v, n, a = chunk(k), exact[:, i, 0:n_tok], normed[:, i, 0:n_tok], a_of(k)
                if b_of is None:
                    last = dve.do(lambda e: e.scalar_tensor_tensor(out=v, in0=src, scalar=a, in1=factor, op0=ALU.mult,
                                                                   op1=ALU.mult),
                                  factor_mark, chunk_marks[k], params, buffer_free[i])
                    value, hi = last, act.do(lambda e: e.activation(dst_hi(k), v, ACT.Copy), last, dst_free)
                else:
                    last = dve.do(lambda e: e.tensor_tensor(n, src, factor, ALU.mult),
                                  factor_mark, chunk_marks[k], buffer_free[i])
                    value, hi = modulate(n, last, a, b_of(k), params, i, dst_hi(k), dst_free)
                lows.append((k, i, v, value, hi))
                while len(lows) > (1 if k < KC - 1 else 0):
                    marks.append(low_part(dst_hi, dst_lo, dst_free, *lows.pop(0)))
            free[factor_bank] = [last]
            return marks

        def modulate(n, mark, a, b, params, i, hi_k, dst_free):
            v = exact[:, i, 0:n.shape[-1]]
            value = pool.do(lambda e: e.tensor_scalar(v, n, a, b, ALU.mult, ALU.add), mark, params, buffer_free[i])
            return value, act.do(lambda e: e.activation(hi_k, as_read(n, hi_k), ACT.Identity, scale=a, bias=b),
                                 mark, params, dst_free)

        def low_part(dst_hi, dst_lo, dst_free, k, i, v, value, hi):
            lo = dve.do(lambda e: e.tensor_tensor(dst_lo(k), as_read(v, dst_lo(k)), dst_hi(k).bitcast(F32), ALU.subtract),
                        value, hi, dst_free)
            buffer_free[i] = [value, hi, lo]
            return [hi, lo]

        def as_read(a, like):
            return a if len(like.shape) == 2 else a.rearrange("p (r g c) -> p r g c", g=like.shape[2], c=like.shape[3])

        def flat_chunks(h):
            return lambda k: h[:, k, :]

        def causal_or_centred(src, y, w_col, w0, shifts, mark, y_free, bias=None):
            centre = shifts.index(0)
            w = col(w_col, w0 + centre)
            if bias is None:
                m = act.do(lambda e: e.activation(y, src, ACT.Copy, scale=w), mark, y_free)
            else:
                m = act.do(lambda e: e.activation(y, src, ACT.Identity, scale=w, bias=bias), mark, y_free)
            for i, s in enumerate(shifts):
                if s == 0:
                    continue
                w = col(w_col, w0 + i)
                to, frm = (slice(-s, T), slice(0, T + s)) if s < 0 else (slice(0, T - s), slice(s, T))
                m = dve.do(lambda e: e.scalar_tensor_tensor(out=y[:, to], in0=src[:, frm], scalar=w, in1=y[:, to],
                                                            op0=ALU.mult, op1=ALU.add), mark, m)
            return m

        ada = ExitStack()
        mod_raw = sb(ada, "mod_raw", [P, 6 * KC])
        mod_ctx = sb(ada, "mod_ctx", [P, 2 * KC])
        gain_ctx = sb(ada, "gain_ctx", [P, KC])

        mixer = ExitStack()
        k_loc = sb(mixer, "k_loc", [P, AC, T])
        q_loc = sb(mixer, "q_loc", [P, AC, T])
        k_ctx = sb(mixer, "k_ctx", [P, AC, CTX])
        v_loc = sb(mixer, "v_loc", [P, CBLK, ATT])
        v_mid = sb(mixer, "v_mid", [P, CBLK - 1, ATT])
        v_ctx = sb(mixer, "v_ctx", [P, CT, ATT])
        cv_in = sb(mixer, "cv_in", [P, CC, T + 2 * PAD])
        cv_acc = sb(mixer, "cv_acc", [P, CC, T])
        sg_out = sb(mixer, "sg_out", [P, SC, T])
        sg_v = sb(mixer, "sg_v", [P, TT, SG])
        sg_small = sb(mixer, "sg_small_sb", [P, SC * P + 2 * SG + 4 * P])
        sg_b = sg_small[:, 0:SC * P].rearrange("p (s t) -> p s t", s=SC)
        sg_norm_g = sg_small[:, SC * P:SC * P + SG]
        sg_norm_b = sg_small[:, SC * P + SG:SC * P + 2 * SG]
        sg_wT = sg_small[:, SC * P + 2 * SG:SC * P + 2 * SG + 4 * P].rearrange("p (g t) -> p g t", g=4)
        stats = sb(mixer, "stats", [P, 8])
        sg_square = sb(mixer, "sg_square", [P, SG])
        cv_scratch = sb(mixer, "cv_scratch", [P, CC, T])

        context = ExitStack()
        silu_row = sb(context, "silu_row", [P, D])
        ada_products = sb(context, "ada_products", [P, D])
        xc = sb(context, "xc", [P, KC, CTX])
        hc_hi = sb(context, "hc_hi", [P, KC, CTX], F32R)
        hc_lo = sb(context, "hc_lo", [P, KC, CTX], F32R)

        silu_c_m = act.do(lambda e: e.activation(silu_c[:, :, :], silu_c[:, :, :], ACT.Silu), c_in)

        ada_marks, junk_free = {}, [None]

        def ada_turned(tile, what, mark):
            half, k = what

            def mm(e):
                for n in range(D // T):
                    m = e.matmul(bank[2 * half + n][0:2, :], silu_c[:, k, :], tile[:, n * T:(n + 1) * T],
                                 start=(k == 0), stop=(k == KC - 1))
                return m
            ada_marks[what] = pe.do(mm, mark, silu_c_m)
            return ada_marks[what]

        def turned_back(half, rows):
            copies = []
            for n, q in ((0, act), (1, dve)):
                src, dst = bank[2 * half + n][0:2, :], rows[0:2, n, :]
                step = (lambda e: e.activation(dst, src, ACT.Copy)) if q is act else (lambda e: e.tensor_copy(dst, src))
                copies.append(q.do(step, ada_marks[half, KC - 1]))
                free[2 * half + n] = [copies[n]]

            def mm(e):
                for j in range(KC):
                    m = e.transpose(bank[4][:, 2 * (half * KC + j):2 * (half * KC + j) + 2],
                                    rows[0:2, j // 4, j % 4 * P:(j % 4 + 1) * P], identity[0:2, 0:2])
                return m
            return pe.do(mm, copies, consts_in)

        def ada_rows(tile, j, mark):
            ada_marks[j] = dve.do(lambda e: e.tensor_tensor_reduce(
                out=ada_products[:, :], in0=tile, in1=silu_row[:, :], scale=1.0, scalar=0.0, op0=ALU.mult, op1=ALU.add,
                accum_out=mod_raw[:, j:j + 1]), mark, silu_row_m, junk_free[0])
            junk_free[0] = ada_marks[j]
            return ada_marks[j]

        stream.takers = {"ada_turned": ada_turned, "ada_rows": ada_rows}
        norm1 = Norm(T, exact[:, 0, :])
        for k in range(KC):
            norm1.square(x[:, k, :], x_in[k // 2])
            stream.prepare_next()
        for _ in range(2):
            stream.prepare_next()
        r, m = norm1.finish()
        factor = cv_acc[:, 0, :]
        factor_in = act.do(lambda e: e.activation(factor, bank[r][:, :], ACT.Copy), m)
        free[r] = [factor_in]
        for _ in range(2):
            stream.prepare_next()
        turned_back(1, sg_out)
        x_normed, x_normed_marks = [], []
        for k in range(KC):
            n = (k_loc if k < KC // 2 else v_loc)[:, k % (KC // 2), :]
            x_normed.append(n)
            x_normed_marks.append((pool if k % 3 == 2 else dve).do(
                lambda e: e.tensor_tensor(n, x[:, k, :], factor, ALU.mult), factor_in, x_in[k // 2]))
        for _ in range(4):
            stream.prepare_next()
        turned = turned_back(0, cv_scratch)
        row_in = pool.load(counter("s_crow"), silu_row[:, :], io["c_row"], ada_marks[0, KC - 3])
        xc_in = pool.load(counter("s_xc"), xc[:, :, :], io["ctx"])
        sg_in = pool.load(counter("s_sg"), sg_small[:, :], io["sg_small"])
        buffer_free[:] = [everyone(), everyone()]
        ada_b, shift_scale = cols_of("ada_b"), bank[4][:, 0:4 * KC].rearrange("p (j n) -> p n j", n=2)
        mod_m = dve.do(lambda e: e.tensor_tensor(mod[:, 0:2 * KC], shift_scale[:, 0, :], ada_b[:, 0:2 * KC], ALU.add),
                       turned, cols_in)
        gain_m = dve.do(lambda e: e.scalar_tensor_tensor(out=gain[:, :], in0=mod[:, KC:2 * KC], scalar=1.0,
                                                         in1=cols_of("norm1_g"), op0=ALU.add, op1=ALU.mult), mod_m)
        mod_x = dve.do(lambda e: e.tensor_tensor(mod_ctx[:, :], shift_scale[:, 1, :], ada_b[:, 0:2 * KC], ALU.add),
                       turned, cols_in)
        free[4] = [mod_x]
        gain_x = dve.do(lambda e: e.scalar_tensor_tensor(out=gain_ctx[:, :], in0=mod_ctx[:, KC:2 * KC], scalar=1.0,
                                                         in1=cols_of("norm1_g"), op0=ALU.add, op1=ALU.mult), mod_x)
        for _ in range(SIDE_BY_SIDE):
            stream.prepare_next()

        def grid_of(a):
            return a.rearrange("p (g r c) -> p r g c", r=ROWS, c=GROUP)

        def rows_of(a):
            return a.rearrange("p (r g c) -> p r g c", r=ROWS, c=GROUP)

        h_marks, lows = [], []
        dst_hi, dst_lo = lambda k: grid_of(h_hi[:, k, :]), lambda k: grid_of(h_lo[:, k, :])
        for k in range(KC):
            value, hi = modulate(x_normed[k], x_normed_marks[k], gain[:, k:k + 1], mod[:, k:k + 1], gain_m, k % 2,
                                 dst_hi(k), None)
            h_marks.append(low_part(dst_hi, dst_lo, None, k, k % 2, exact[:, k % 2, :], value, hi))
        silu_row_m = act.do(lambda e: e.activation(silu_row[:, :], silu_row[:, :], ACT.Silu), row_in)

        pads = [dve.do(lambda e: e.memset(cv_in[:, :, s], 0.0)) for s in (slice(0, PAD), slice(PAD + T, T + 2 * PAD))]
        cv_mark, cv_taps = [None] * CC, [0] * CC
        cv_products = linears(2 * CC, KC, h_hi, h_lo, h_marks)
        for c in range(CC):
            (ba, ma), (bg, mg) = next(cv_products), next(cv_products)
            dst = cv_in[:, c, PAD:PAD + T]
            sig = act.do(lambda e: e.activation(rows_of(dst), grid_of(bank[bg][:, :]), ACT.Sigmoid), mg)
            cv_mark[c] = dve.do(lambda e: e.tensor_tensor(rows_of(dst), grid_of(bank[ba][:, :]), rows_of(dst), ALU.mult),
                                ma, sig)
            free[bg], free[ba] = [sig], [cv_mark[c]]
            if c == 0:
                norm_ctx = Norm(CTX, cv_scratch[:, 0, 0:CTX])
                for k in range(KC):
                    norm_ctx.square(xc[:, k, :], xc_in)

        def conv_taps(n):
            for c, q in ((0, dve), (1, pool)):
                for i in range(cv_taps[c], min(cv_taps[c] + n, TAPS)):
                    src, w, acc = cv_in[:, c, i:i + T], col("cv_w", c * TAPS + i), cv_acc[:, c, :]
                    if i and q is pool:
                        part = squares[:, i % 2, :]
                        m = pool.do(lambda e: e.tensor_scalar(part, src, w, 0.0, ALU.mult, ALU.add), cv_mark[c], square_free[i % 2])
                        cv_mark[c] = pool.do(lambda e: e.tensor_tensor(acc, acc, part, ALU.add), m)
                        square_free[i % 2] = [cv_mark[c]]
                        continue
                    if i == 0:
                        step = lambda e: e.tensor_scalar(acc, src, w, col("cv_b", c), ALU.mult, ALU.add)
                    else:
                        step = lambda e: e.scalar_tensor_tensor(out=acc, in0=src, scalar=w, in1=acc, op0=ALU.mult, op1=ALU.add)
                    cv_mark[c] = q.do(step, cv_mark[c], pads, cols_in)
                cv_taps[c] = min(cv_taps[c] + n, TAPS)

        stream.prepare_ahead()
        r, m = norm_ctx.finish()
        hc_marks = apply_norm(r, m, lambda k: xc[:, k, :], [xc_in] * KC, CTX, lambda k: gain_ctx[:, k:k + 1],
                              lambda k: mod_ctx[:, k:k + 1], gain_x, flat_chunks(hc_hi), flat_chunks(hc_lo), None)

        sg_vT, sg_vT_marks = cv_scratch, []
        for c in range(SC):
            b, m = linear(1, KC, h_hi, h_lo, h_marks)
            sg_vT_marks.append(act.do(lambda e: e.activation(rows_of(sg_vT[:, c, :]), grid_of(bank[b][:, :]),
                                                             ACT.Gelu_apprx_tanh), m))
            free[b] = [sg_vT_marks[c]]
            conv_taps(2)
        sg_u = []
        for c in range(SC):
            b, m = linear(1, KC, h_hi, h_lo, h_marks)
            sg_u.append(act.do(lambda e: e.activation(rows_of(sg_out[:, c, :]), grid_of(bank[b][:, :]),
                                                      ACT.Gelu_apprx_tanh), m))
            free[b] = [sg_u[c]]
            conv_taps(2)
        sg_v_ready, before = [], None
        for t in range(TT):
            v, b = sg_v[:, t, :], banks.take()

            def turn_over(e):
                for c in range(SC):
                    m = e.transpose(bank[b][:, c * P:(c + 1) * P], sg_vT[:, c, t * P:(t + 1) * P], identity)
                return m
            m = pe.do(turn_over, sg_vT_marks, consts_in, free[b])
            m = act.do(lambda e: e.activation(v, bank[b][:, 0:SG], ACT.Copy, accum_out=stats[:, 0:1]), m, before)
            free[b] = [m]
            m = dve.do(lambda e: e.tensor_scalar(stats[:, 1:2], stats[:, 0:1], 1.0 / SG, None, ALU.mult), m)
            m = dve.do(lambda e: e.tensor_scalar(v, v, stats[:, 1:2], None, ALU.subtract), m)
            m = act.do(lambda e: e.activation(sg_square[:, :], v, ACT.Square, accum_out=stats[:, 2:3]), m)
            m = act.do(lambda e: e.activation(stats[:, 3:4], stats[:, 2:3], ACT.Sqrt, scale=1.0 / SG, bias=col("eps")), m)
            m = dve.do(lambda e: e.reciprocal(stats[:, 4:5], stats[:, 3:4]), m)
            m = dve.do(lambda e: e.scalar_tensor_tensor(out=v, in0=v, scalar=stats[:, 4:5], in1=sg_norm_g, op0=ALU.mult,
                                                        op1=ALU.mult), m, sg_in)
            before = dve.do(lambda e: e.tensor_tensor(v, v, sg_norm_b, ALU.add), m)
            sg_v_ready.append(before)

        q_marks, k_marks, kc_marks = [None] * AC, [None] * AC, [None] * AC
        for c in range(AC):
            b, bc = banks.take(), banks.take()
            s, w_marks, _ = stream.next_tile()

            def mm(e):
                for rhs_hi, rhs_lo, dst in ((h_hi, h_lo, bank[b][:, :]), (hc_hi, hc_lo, bank[bc][:, 0:CTX])):
                    for k in range(KC):
                        w = slice(k * P, (k + 1) * P)
                        m = product(e, dst, w_hi[:, s, w], w_lo[:, s, w], rhs_hi[:, k, :], rhs_lo[:, k, :], k == 0, k == KC - 1)
                return m
            m = pe.do(mm, w_marks, h_marks, hc_marks, free[b], free[bc])
            stream.split_free[s] = [m]
            k_marks[c] = act.do(lambda e: e.activation(k_loc[:, c, :], bank[b][:, :], ACT.Copy), m)
            kc_marks[c] = act.do(lambda e: e.activation(k_ctx[:, c, :], bank[bc][:, 0:CTX], ACT.Copy), m)
            free[b], free[bc] = [k_marks[c]], [kc_marks[c]]
            conv_taps(3)

        vb = [banks.take() for _ in range(TT + CT)]
        v_marks = [None] * len(vb)
        for tile in range(ATT * D // (P * SLOT)):
            s, w_marks, (k0, n) = stream.next_tile()
            for t in range(len(vb)):
                own_hi, own_lo = (h_hi, h_lo) if t < TT else (hc_hi, hc_lo)
                tok = slice(t % TT * P, (t % TT + 1) * P)

                def mm(e):
                    for j in range(n):
                        k, w = k0 + j, slice(j * ATT, (j + 1) * ATT)
                        m = product(e, bank[vb[t]][:, :], own_hi[:, k, tok], own_lo[:, k, tok], w_hi[:, s, w],
                                    w_lo[:, s, w], k == 0, k == KC - 1)
                    return m
                v_marks[t] = pe.do(mm, w_marks, h_marks, hc_marks, free[vb[t]] if tile == 0 else None)
            stream.split_free[s] = [v_marks[-1]]
            conv_taps(3)
        for t in range(len(vb)):
            dst = v_loc[:, t, :] if t < TT else v_ctx[:, t - TT, :]
            v_marks[t] = act.do(lambda e: e.activation(dst, bank[vb[t]][:, :], ACT.Copy), v_marks[t])
            free[vb[t]] = [v_marks[t]]
        v_moved, low, high = counter("s_v_moved"), slice(0, P // 2), slice(P // 2, P)
        sync.load(v_moved, v_mid[low, :, :], v_loc[high, 0:CBLK - 1, :], v_marks)
        moved = sync.load(v_moved, v_mid[high, :, :], v_loc[low, 1:CBLK, :], v_marks)

        assert len(ada_marks) == 2 * KC + 4 * KC
        context.close()
        handed = everyone()
        attention = ExitStack()
        rel = sb(attention, "rel", [P, HEADS, WINDOW])
        biased = sb(attention, "biased", [P, len(SPAN_OFFS), HEADS, SPAN // GROUP, ROWS, GROUP])
        rel_in = sync.load(counter("s_rel"), rel[:, :, :], io["rel_rows"], handed)

        sg_done = []
        for c in range(SC):
            b = banks.take()

            def mix(e):
                for t in range(TT):
                    for g in (2 * c, 2 * c + 1):
                        p0 = (g % 2) * 64
                        m = e.matmul(bank[b][p0:p0 + 64, t * P:(t + 1) * P], sg_v[:, t, g * 64:(g + 1) * 64],
                                     sg_wT[:, g, :], start=True, stop=True)
                return m
            m = pe.do(mix, sg_v_ready, sg_in, free[b])
            mixed = bank[b][:, :].rearrange("p (t q) -> p t q", t=TT)
            bias = sg_b[:, c, :].unsqueeze(1).to_broadcast([P, TT, P])
            m = dve.do(lambda e: e.tensor_tensor(mixed, mixed, bias, ALU.add), m)
            m = dve.do(lambda e: e.tensor_tensor(sg_out[:, c, :], bank[b][:, :], sg_out[:, c, :], ALU.mult), m, sg_u[c])
            free[b] = [m]
            sg_done.append(m)

        def take_queries(c, b, m):
            q_marks[c] = act.do(lambda e: e.activation(q_loc[:, c, :], bank[b][:, :], ACT.Copy, scale=SCALE), m)
            free[b] = [q_marks[c]]

        b, m = linear(1, KC, h_hi, h_lo, h_marks)
        take_queries(0, b, m)
        conv_taps(TAPS)

        bias_in = {}
        for h in range(HEADS):
            for v, off in enumerate(SPAN_OFFS):
                hidden = const("window_neg")[:, v * SPAN:(v + 1) * SPAN].rearrange("p (g c) -> p g c", c=GROUP)
                hidden = hidden.unsqueeze(1).to_broadcast([P, ROWS, SPAN // GROUP, GROUP])
                rows = rel[:, h, WIN + off:WIN + off + ROWS * RPB_W]
                rows = bass.AP(rows.tensor, rows.offset, [rows.ap[0], [RPB_W, ROWS], [GROUP, SPAN // GROUP], [1, GROUP]])
                bias_in[v, h] = pool.do(lambda e: e.tensor_tensor(
                    biased[:, v, h, :, :, :].rearrange("p g r c -> p r g c"), rows, hidden, ALU.add),
                    rel_in, consts_in, handed)

        mix_marks = [None] * KC
        for c in range(CC):
            acc, y = cv_acc[:, c, :], cv_scratch[:, c, :]
            b = banks.take()
            m = pe.do(lambda e: e.matmul(bank[b][:, :], const("group_mean"), acc, start=True, stop=True),
                      cv_mark[c], consts_in, free[b])
            m = dve.do(lambda e: e.tensor_tensor(acc, acc, bank[b][:, :], ALU.subtract), m)
            m = act.do(lambda e: e.activation(y, acc, ACT.Square), m)
            free[b] = [m]
            m = pe.do(lambda e: e.matmul(bank[b][:, :], const("group_mean"), y, start=True, stop=True), m)
            m = act.do(lambda e: e.activation(y, bank[b][:, :], ACT.Sqrt, bias=col("eps")), m)
            free[b] = [m]
            m = dve.do(lambda e: e.reciprocal(y, y), m)
            m = dve.do(lambda e: e.tensor_tensor(acc, acc, y, ALU.mult), m)
            m = act.do(lambda e: e.activation(acc, acc, ACT.Silu, scale=col("cv_norm_g", c), bias=col("cv_norm_b", c)), m)
            cv_mark[c] = m

        probs, probs_t = normed, exact
        soft = sb(attention, "soft", [P, 2, 4])
        steps = [(h, b) for h in range(HEADS) for b in range(CBLK)]
        h_read = [None]

        assert len(ada_marks) == 2 * KC + 4 * KC
        mod_rest = dve.do(lambda e: e.tensor_tensor(mod[:, 2 * KC:], mod_raw[:, 2 * KC:], ada_b[:, 2 * KC:], ALU.add),
                          [ada_marks[j] for j in range(2 * KC, 6 * KC)])

        def add_gated(o, b, m, gate_at):
            g = mod[:, gate_at + o:gate_at + o + 1]
            x_marks[o] = dve.do(lambda e: e.scalar_tensor_tensor(
                out=x[:, o, :], in0=bank[b][:, :], scalar=g, in1=x[:, o, :], op0=ALU.mult, op1=ALU.add),
                m, mod_rest, x_marks[o])
            free[b] = [x_marks[o]]

        x_marks = [None] * KC

        def between():
            for c in range(1, AC):
                b, m = yield from linear_steps(NORM_BANKS[c % 2], 1, range(KC), h_hi, h_lo, h_marks)
                take_queries(c, b, m)
            h_read[0] = m
            for c in range(SC):
                k = AC + c
                mix_marks[k] = split(sg_out[:, c, :], sg_done[c], h_hi[:, k, :], h_lo[:, k, :], m)
            for c in range(CC):
                k = AC + SC + c
                mix_marks[k] = split(cv_acc[:, c, :], cv_mark[c], h_hi[:, k, :], h_lo[:, k, :], m)
            for o in range(KC):
                b, m = yield from linear_steps(NORM_BANKS[o % 2], 1, range(AC, KC), h_hi, h_lo, mix_marks)
                add_gated(o, b, m, 2 * KC)

        filler = between()
        probs_free, probs_t_free = [handed, handed], [handed, handed]
        normalised, copied = {}, {}

        def scores(i):
            h, b = steps[i]
            c, part, u = h // 2, slice((h % 2) * HD, (h % 2 + 1) * HD), i % 2
            q = q_loc[part, c, b * P:(b + 1) * P]
            kl = k_loc[part, c, SPAN_START[b] * ROWS:(SPAN_START[b] + SPAN) * ROWS]
            S = bank[u]
            local = S[:, 0:ROWS * SPAN]

            def mm(e):
                e.matmul(local, q, kl, start=True, stop=True)
                return e.matmul(S[:, ROWS * SPAN:T], q, k_ctx[part, c, :], start=True, stop=True)
            m = pe.do(mm, q_marks[c], k_marks[c], kc_marks[c], free[u])
            v = SPAN_OFFS.index(SPAN_START[b] - WIN * b)
            m = dve.do(lambda e: e.tensor_tensor(local, local, biased[:, v, h, :, :, :].rearrange("p g r c -> p (g r c)"), ALU.add), m, bias_in[v, h])
            m = dve.do(lambda e: e.reduce_max(soft[:, u, 1:2], S[:, :], AX.X, negate=True), m, probs_free[u])
            m = act.do(lambda e: e.activation(probs[:, u, :], S[:, :], ACT.Exp, bias=soft[:, u, 1:2],
                                              accum_out=soft[:, u, 2:3]), m, probs_free[u])
            free[u] = [m]
            m = dve.do(lambda e: e.reciprocal(soft[:, u, 3:4], soft[:, u, 2:3]), m)
            normalised[i] = dve.do(lambda e: e.tensor_scalar(probs[:, u, :], probs[:, u, :], soft[:, u, 3:4], None,
                                                             ALU.mult), m)

        def turn_over(i):
            u = i % 2
            B = bank[2 + u]

            def mm(e):
                for n in range(T // P):
                    m = e.transpose(B[:, n * P:(n + 1) * P], probs[:, u, n * P:(n + 1) * P], identity)
                return m
            m = pe.do(mm, normalised[i], free[2 + u])
            probs_free[u] = [m]
            copied[i] = act.do(lambda e: e.activation(probs_t[:, u, :], B[:, :], ACT.Copy), m, probs_t_free[u])
            free[2 + u] = [copied[i]]

        def weighted(i):
            h, b = steps[i]
            c, p0, u = h // 2, (h % 2) * HD, i % 2
            ob = 4 + c % 2
            tiles = v_loc if SPAN_START[b] % WIN == 0 else v_mid
            values = [tiles[:, SPAN_START[b] // WIN + n, :] for n in range(2)] + [v_ctx[:, n, :] for n in range(CT)]

            def mm(e):
                for n, v in enumerate(values):
                    m = e.matmul(bank[ob][p0:p0 + HD, b * P:(b + 1) * P], v[:, h * HD:(h + 1) * HD],
                                 probs_t[:, u, n * P:(n + 1) * P], start=(n == 0), stop=(n == len(values) - 1))
                return m
            m = pe.do(mm, copied[i], v_marks, moved, free[ob] if (h % 2, b) == (0, 0) else None)
            probs_t_free[u] = [m]
            if (h % 2, b) == (1, CBLK - 1):
                mix_marks[c] = split(grid_of(bank[ob][:, :]), m, rows_of(h_hi[:, c, :]), rows_of(h_lo[:, c, :]), h_read[0])
                free[ob] = [mix_marks[c][1]]

        for i in range(len(steps) + 2):
            if i < len(steps):
                scores(i)
            for _ in range(2 if i < KC else i % 2):
                next(filler, None)
            if 1 <= i <= len(steps):
                turn_over(i - 1)
            next(filler, None)
            if 2 <= i:
                weighted(i - 2)
        for _ in filler:
            pass
        attention.close()
        mixer.close()

        gain_m = dve.do(lambda e: e.scalar_tensor_tensor(out=gain[:, :], in0=mod[:, 4 * KC:5 * KC], scalar=1.0,
                                                         in1=cols_of("norm2_g"), op0=ALU.add, op1=ALU.mult), mod_rest)
        ada.close()
        buffer_free[:] = [everyone(), everyone()]
        norm2 = Norm(T, exact[:, 0, :])
        for o, (b, m) in enumerate(linears(KC, AC, h_hi, h_lo, mix_marks)):
            add_gated(o, b, m, 2 * KC)
            norm2.square(x[:, o, :], x_marks[o])
        stream.prepare_ahead()
        r, m = norm2.finish()
        h_marks = apply_norm(r, m, lambda k: x[:, k, :], x_marks, T, lambda k: gain[:, k:k + 1],
                             lambda k: mod[:, 3 * KC + k:3 * KC + k + 1], gain_m, flat_chunks(h_hi), flat_chunks(h_lo), (pe.sem, pe.count))

        ffn = ExitStack()
        a_hi = sb(ffn, "a_hi", [P, FC, T], F32R)
        a_lo = sb(ffn, "a_lo", [P, FC, T], F32R)
        handed = everyone()
        work_free = [handed, handed]
        a_marks = [None] * FC
        products = linears(2 * FC, KC, h_hi, h_lo, h_marks)
        for f in range(FC):
            (bg, mg), (bu, mu) = next(products), next(products)
            y = normed[:, f % 2, :]
            m = causal_or_centred(bank[bg][:, :], y, "ffn_conv_w", 3 * f, (-1, 0, 1), mg, work_free[f % 2], col("ffn_conv_b", f))
            free[bg] = [m]
            m = act.do(lambda e: e.activation(y, y, ACT.Silu), m)
            m = dve.do(lambda e: e.tensor_tensor(y, bank[bu][:, :], y, ALU.mult), m, mu)
            free[bu] = [m]
            a_marks[f] = split(y, m, a_hi[:, f, :], a_lo[:, f, :], handed)
            work_free[f % 2] = a_marks[f]
        norm_f, norm3 = Norm(T, exact[:, 0, :]), Norm(T, exact[:, 1, :])
        for o in range(KC):
            b, m = linear(3, FC, a_hi, a_lo, a_marks)
            add_gated(o, b, m, 5 * KC)
            norm_f.square(x[:, o, :], x_marks[o])
            norm3.square(x[:, o, :], x_marks[o], col("final_norm_g", o))
        ffn.close()

        stream.prepare_ahead()

        gain_m = dve.do(lambda e: e.tensor_tensor(gain[:, :], cols_of("final_norm_g"), cols_of("norm_mix_pre_2"), ALU.mult),
                        cols_in, everyone())
        r1, r1_marks = norm_f.factors()
        norm3.end_of_sums()
        scaled, r3, both = small[:, 0:TT], small[:, TT:2 * TT], small[:, 2 * TT:3 * TT]
        m = dve.do(lambda e: e.tensor_tensor(scaled, r1, r1, ALU.mult), r1_marks)
        m = dve.do(lambda e: e.tensor_tensor(scaled, bank[norm3.b][:, 0:TT], scaled, ALU.mult), m, norm3.mark)
        read = m
        m = act.do(lambda e: e.activation(scaled, scaled, ACT.Sqrt, scale=1.0 / D, bias=col("eps")), m)
        m = dve.do(lambda e: e.reciprocal(r3, scaled), m)
        m = dve.do(lambda e: e.tensor_tensor(both, r3, r1, ALU.mult), m)
        both_spread = spread(both, [m, read], norm3.b)

        buffer_free[:] = [everyone(), everyone()]
        h_marks = apply_norm(norm3.b, both_spread, lambda k: x[:, k, :], x_marks, T, lambda k: gain[:, k:k + 1], None,
                             gain_m, flat_chunks(h_hi), flat_chunks(h_lo), (pe.sem, pe.count))
        r1_spread = spread(r1, r1_marks, norm_f.b)
        for k in range(KC):
            x_marks[k] = dve.do(lambda e: e.scalar_tensor_tensor(
                out=x[:, k, :], in0=x[:, k, :], scalar=col("final_norm_g", k), in1=bank[norm_f.b][:, :], op0=ALU.mult,
                op1=ALU.mult), r1_spread, x_marks[k], h_marks[k])
        free[norm_f.b] = [x_marks[-1]]
        branch = ExitStack()
        att_hi = sb(branch, "att_hi", [P, AC, T], F32R)
        att_lo = sb(branch, "att_lo", [P, AC, T], F32R)
        cnv_hi = sb(branch, "cnv_hi", [P, AC, T], F32R)
        cnv_lo = sb(branch, "cnv_lo", [P, AC, T], F32R)
        stick = ExitStack()
        q2 = sb(stick, "q2", [P, AC, T])
        k2 = sb(stick, "k2", [P, AC, T])
        v2 = sb(stick, "v2", [P, TT, ATT])
        NZ = sum(T - P * j for j in range(TT))
        z = sb(stick, "z", [P, 3, NZ])
        sp = sb(stick, "sp", [P, NZ])
        sp_hi = sb(stick, "sp_hi", [P, 2, NZ], F32R)
        sp_lo = sb(stick, "sp_lo", [P, 2, NZ], F32R)
        minus = sb(stick, "minus", [P, 2 * P], F32R)
        handed = everyone()

        all_, tri = minus[:, 0:P], minus[:, P:2 * P]
        minus_in = act.do(lambda e: e.activation(minus[:, :], consts[:, CONSTS["minus_ones"][0]:CONSTS["minus_ones"][0] + 2 * P],
                                                 ACT.Copy), consts_in, handed)

        qk_marks = []
        for c, (b, m) in enumerate(linears(2 * AC, KC, h_hi, h_lo, h_marks)):
            dst, scale = (q2[:, c, :], SCALE) if c < AC else (k2[:, c - AC, :], 1.0)
            qk_marks.append(act.do(lambda e: e.activation(dst, bank[b][:, :], ACT.Copy, scale=scale), m, handed))
            free[b] = [qk_marks[c]]
        vb = [banks.take() for _ in range(TT)]
        v_marks = [None] * TT
        for tile in range(ATT * D // (P * SLOT)):
            s, w_marks, (k0, n) = stream.next_tile()
            for t in range(TT):
                def mm(e):
                    for j in range(n):
                        k, w, tok = k0 + j, slice(j * ATT, (j + 1) * ATT), slice(t * P, (t + 1) * P)
                        m = product(e, bank[vb[t]][:, :], h_hi[:, k, tok], h_lo[:, k, tok], w_hi[:, s, w], w_lo[:, s, w],
                                    k == 0, k == KC - 1)
                    return m
                v_marks[t] = pe.do(mm, w_marks, h_marks, free[vb[t]] if tile == 0 else None)
            stream.split_free[s] = [v_marks[-1]]
        for t in range(TT):
            v_marks[t] = act.do(lambda e: e.activation(v2[:, t, :], bank[vb[t]][:, :], ACT.Copy), v_marks[t], handed)
            free[vb[t]] = [v_marks[t]]

        cnv_marks = [None] * AC
        VALUES_BANK, BETWEEN_BANK = NORM_BANKS

        def between_sticks():
            work_free = [[handed], [handed]]
            for c in range(AC):
                u, y = normed[:, c % 2, :], exact[:, c % 2, :]

                def own_product():
                    return finished(linear_steps(BETWEEN_BANK, 1, range(KC), h_hi, h_lo, h_marks))
                b, m = own_product()
                m = act.do(lambda e: e.activation(u, bank[b][:, :], ACT.Copy), m, work_free[c % 2])
                free[b] = [m]
                yield
                b, mx = own_product()
                m = dve.do(lambda e: e.tensor_tensor(u, bank[b][:, :], u, ALU.mult), mx, m)
                free[b] = [m]
                m = causal_or_centred(u, y, "conv_mix_w_2", 3 * c, (-2, -1, 0), m, work_free[c % 2])
                yield
                b, mb = own_product()
                m = dve.do(lambda e: e.tensor_tensor(y, bank[b][:, :], y, ALU.mult), m, mb)
                free[b] = [m]
                cnv_marks[c] = split(y, m, cnv_hi[:, c, :], cnv_lo[:, c, :], handed)
                work_free[c % 2] = [cnv_marks[c]]
                yield

        DIAG = [slice(j * P, (j + 1) * P) for j in range(TT)]
        OFF_AT = [T, T + 3 * P, T + 5 * P]

        def off(j, q_from, q_to=TT):
            return slice(OFF_AT[j] + (q_from - j - 1) * P, OFF_AT[j] + (q_to - j - 1) * P)

        PARTS = [(0, slice(0, T), 0), (1, slice(T, T + 3 * P), 0), (1, slice(T + 5 * P, NZ), 3 * P), (2, slice(T + 3 * P, T + 5 * P), 0)]

        def where(columns):
            for n, part, at in PARTS:
                if part.start <= columns.start and columns.stop <= part.stop:
                    return n, slice(columns.start - part.start + at, columns.stop - part.start + at)

        z_free, sp_free, split_sp_free = [handed] * 3, [handed], [handed] * 2
        z_ready, w_ready = {}, {}
        att_marks = [None] * AC

        def stick_scores(h):
            c, part, u = h // 2, slice((h % 2) * HD, (h % 2 + 1) * HD), h % 3

            def mm(e):
                for j in range(TT):
                    keys = k2[part, c, j * P:(j + 1) * P]
                    m = e.matmul(bank[0][:, DIAG[j]], keys, q2[part, c, j * P:(j + 1) * P], start=True, stop=True)
                    if j < TT - 1:
                        n, at = where(off(j, j + 1))
                        m = e.matmul(bank[n][:, at], keys, q2[part, c, (j + 1) * P:T], start=True, stop=True)
                return m
            m = pe.do(mm, qk_marks[c], qk_marks[AC + c], free[0], free[1], free[2])
            hidden = const("causal_neg").unsqueeze(1).to_broadcast([P, TT, P])
            d = dve.do(lambda e: e.tensor_tensor(z[:, u, 0:T].rearrange("p (t q) -> p t q", t=TT),
                                                 bank[0][:, :].rearrange("p (t q) -> p t q", t=TT), hidden, ALU.add),
                       m, z_free[u])
            free[0] = [d]
            for n, part_, at in PARTS[1:]:
                o = act.do(lambda e: e.activation(z[:, u, part_], bank[n][:, at:at + part_.stop - part_.start], ACT.Copy),
                           m, z_free[u])
                free[n] = [o]
            zz, ss, v = z[:, u, :], sp[:, :], h % 2
            m = dve.do(lambda e: e.scalar_tensor_tensor(out=ss, in0=zz, scalar=-1.0, in1=zz, op0=ALU.mult, op1=ALU.min),
                       d, o, sp_free[0])
            m = act.do(lambda e: e.activation(ss, ss, ACT.Exp), m)
            m = act.do(lambda e: e.activation(ss, ss, ACT.Ln, bias=col("one")), m)
            m = dve.do(lambda e: e.scalar_tensor_tensor(out=ss, in0=zz, scalar=0.0, in1=ss, op0=ALU.max, op1=ALU.add), m)
            hi = dve.do(lambda e: e.tensor_copy(sp_hi[:, v, :], ss), m, split_sp_free[v])
            lo = dve.do(lambda e: e.tensor_tensor(sp_lo[:, v, :], ss, sp_hi[:, v, :].bitcast(F32), ALU.subtract), hi)
            sp_free[0] = [lo]
            z_ready[h] = [hi, lo]

        def stick_weights(h):
            u, v = h % 3, h % 2

            def add_up(e, dst, minus_what, columns, first, last):
                e.matmul(dst, minus_what, sp_hi[:, v, columns], start=first, stop=False)
                return e.matmul(dst, minus_what, sp_lo[:, v, columns], start=False, stop=last)

            def mm(e):
                add_up(e, bank[3][:, :], tri, slice(0, T), True, True)
                for j in range(TT - 1):
                    own = off(j, j + 1)
                    n, at = where(own)
                    add_up(e, bank[3 + n][:, at], tri, own, True, False)
                    for i in range(j + 1, TT):
                        if i < TT - 1:
                            n, at = where(off(j, i + 1))
                            add_up(e, bank[3 + n][:, at], all_, off(i, i + 1), False, False)
                        n, at = where(off(j, i, i + 1))
                        m = add_up(e, bank[3 + n][:, at], all_, DIAG[i], False, i == TT - 1)
                return m
            m = pe.do(mm, z_ready[h], minus_in, free[3], free[4], free[5])
            split_sp_free[v] = [m]
            for n, part, at in PARTS:
                a = dve.do(lambda e: e.tensor_tensor(z[:, u, part], z[:, u, part],
                                                     bank[3 + n][:, at:at + part.stop - part.start], ALU.add), m)
                free[3 + n] = [a]
            w_ready[h] = act.do(lambda e: e.activation(z[:, u, :], z[:, u, :], ACT.Exp), a)

        def stick_values(h):
            c, p0, u = h // 2, (h % 2) * HD, h % 3
            ob = VALUES_BANK

            def mm(e):
                for j in range(TT):
                    v = v2[:, j, h * HD:(h + 1) * HD]
                    m = e.matmul(bank[ob][p0:p0 + HD, DIAG[j]], v, z[:, u, DIAG[j]], start=(j == 0), stop=(j == TT - 1),
                                 skip_group_check=True)
                    if j < TT - 1:
                        m = e.matmul(bank[ob][p0:p0 + HD, (j + 1) * P:T], v, z[:, u, off(j, j + 1)], start=False,
                                     stop=False, skip_group_check=True)
                return m
            m = pe.do(mm, w_ready[h], v_marks, free[ob] if h % 2 == 0 else None)
            z_free[u] = [m]
            if h % 2:
                att_marks[c] = split(bank[ob][:, :], m, att_hi[:, c, :], att_lo[:, c, :])
                free[ob] = [att_marks[c][1]]

        filler = between_sticks()
        for h in range(HEADS + 2):
            if h < HEADS:
                stick_scores(h)
            next(filler, None)
            if 1 <= h <= HEADS:
                stick_weights(h - 1)
            if h % 5 == 1:
                next(filler, None)
            if 2 <= h:
                stick_values(h - 2)
        for _ in filler:
            pass
        stick.close()

        merge = ExitStack()
        m_hi = sb(merge, "m_hi", [P, KC, T], F32R)
        m_lo = sb(merge, "m_lo", [P, KC, T], F32R)
        handed = everyone()
        m_marks, work_free = [None] * KC, [[handed], [handed]]
        for o in range(KC):
            i = o % 2
            ga, ma = linear(1, KC, h_hi, h_lo, h_marks)
            gc, mc = linear(1, KC, h_hi, h_lo, h_marks)
            ya, na = linear(1, AC, att_hi, att_lo, att_marks)
            yc, nc_ = linear(1, AC, cnv_hi, cnv_lo, cnv_marks)
            u, y = normed[:, i, :], exact[:, i, :]
            sa = act.do(lambda e: e.activation(u, bank[ga][:, :], ACT.Sigmoid), ma, work_free[i])
            sc = act.do(lambda e: e.activation(y, bank[gc][:, :], ACT.Sigmoid), mc, work_free[i])
            pa = dve.do(lambda e: e.tensor_tensor(u, bank[ya][:, :], u, ALU.mult), na, sa)
            pc = dve.do(lambda e: e.tensor_tensor(y, bank[yc][:, :], y, ALU.mult), nc_, sc)
            free[ga], free[gc], free[ya], free[yc] = [sa], [sc], [pa], [pc]
            both = dve.do(lambda e: e.tensor_tensor(u, u, y, ALU.add), pa, pc)
            m_marks[o] = split(u, both, m_hi[:, o, :], m_lo[:, o, :], handed)
            work_free[i] = [m_marks[o]]

        def normed_into_x(y_buf, products, gain_name, y_free, next_norm):
            norm, y_marks, marks = Norm(T, exact[:, 0, :]), [], []
            for o, (b, m) in enumerate(products):
                y_marks.append(act.do(lambda e: e.activation(y_buf[:, o, :], bank[b][:, :], ACT.Copy), m, y_free))
                free[b] = [y_marks[o]]
                norm.square(y_buf[:, o, :], y_marks[o])
            stream.prepare_ahead()
            r, m = norm.finish()
            for k in range(KC):
                y, g = y_buf[:, k, :], col(gain_name, k)
                n = dve.do(lambda e: e.scalar_tensor_tensor(out=y, in0=y, scalar=g, in1=bank[r][:, :], op0=ALU.mult,
                                                            op1=ALU.mult), m, y_marks[k])
                marks.append((pool if k % 2 else dve).do(
                    lambda e: e.tensor_tensor(x[:, k, :], x[:, k, :], y, ALU.add), n, x_marks[k]))
                if next_norm:
                    next_norm.square(x[:, k, :], marks[k])
            free[r] = [n]
            return marks

        y_buf = sb(merge, "y_buf", [P, KC, T])
        norm4 = Norm(T)
        x_marks = normed_into_x(y_buf, linears(KC, KC, m_hi, m_lo, m_marks), "norm_mix_post_2", handed, norm4)
        merge.close()
        branch.close()
        buffer_free[:] = [everyone(), everyone()]
        r, m = norm4.finish()
        h_marks = apply_norm(r, m, lambda k: x[:, k, :], x_marks, T, lambda k: col("norm_ffn_pre_2", k), None, None,
                             flat_chunks(h_hi), flat_chunks(h_lo), (pe.sem, pe.count))

        ffn = ExitStack()
        a_hi = sb(ffn, "a2_hi", [P, FC, T], F32R)
        a_lo = sb(ffn, "a2_lo", [P, FC, T], F32R)
        y_buf = sb(ffn, "y2_buf", [P, KC, T])
        handed = everyone()
        work_free = [[handed], [handed]]
        products = linears(2 * FC, KC, h_hi, h_lo, h_marks)
        for f in range(FC):
            (ba, ma), (bg, mg) = next(products), next(products)
            u, y = normed[:, f % 2, :], exact[:, f % 2, :]
            m1 = causal_or_centred(bank[ba][:, :], u, "conv_ffn_w_2", 3 * f, (-2, -1, 0), ma, work_free[f % 2])
            m2 = causal_or_centred(bank[bg][:, :], y, "conv_ffn_w_2", 3 * (FC + f), (-2, -1, 0), mg, work_free[f % 2])
            free[ba], free[bg] = [m1], [m2]
            m2 = act.do(lambda e: e.activation(y, y, ACT.Gelu_apprx_tanh), m2)
            m = dve.do(lambda e: e.tensor_tensor(u, u, y, ALU.mult), m1, m2)
            a_marks[f] = split(u, m, a_hi[:, f, :], a_lo[:, f, :], handed)
            work_free[f % 2] = [a_marks[f], m]
        x_marks = normed_into_x(y_buf, (linear(3, FC, a_hi, a_lo, a_marks) for _ in range(KC)), "norm_ffn_post_2",
                                handed, None)
        ffn.close()

        done = counter("s_out")
        for i in range(KC // 2):
            stored = sync.load(done, out[:, 2 * i:2 * i + 2, :], x[:, 2 * i:2 * i + 2, :], x_marks[2 * i + 1])
        sync.wait(stored)


def columns(v):
    return v.reshape(-1, P).T


def tap_columns(w):
    return w.T.reshape(-1, P, w.shape[0]).transpose(1, 0, 2).reshape(P, -1)


def by_feature(v):
    return v.T.reshape(-1, P, v.shape[0]).transpose(1, 0, 2)


def blocks(w):
    k, n = w.shape
    return w.reshape(k // P, P, n // P, P).transpose(2, 1, 0, 3)


def wide(w):
    k, n = w.shape
    per = SLOT // n
    return w.reshape(k // P // per, per, P, n).transpose(0, 2, 1, 3)


def row_and_column(p):
    return p // GROUP % ROWS, p // (GROUP * ROWS) * GROUP + p % GROUP


def shape_constants():
    i = np.arange(P)
    group = (i[:, None] // HD == i[None, :] // HD) / float(CV // 4)
    tri = -(i[:, None] >= i[None, :]).astype(np.float32)
    causal = np.where(i[:, None] < i[None, :], 0.0, NEG)
    hidden = np.zeros((P, len(SPAN_OFFS), SPAN))
    for b in range(CBLK):
        q = WIN * b + np.array([row_and_column(p)[1] for p in range(P)])
        start = np.clip(q - WIN // 2, 0, GRID_W - WIN)
        key = SPAN_START[b] + np.arange(SPAN)
        inside = (key[None, :] >= start[:, None]) & (key[None, :] < start[:, None] + WIN)
        hidden[:, SPAN_OFFS.index(SPAN_START[b] - WIN * b), :] = np.where(inside, 0.0, NEG)
    return np.concatenate([np.eye(P), group, -np.ones((P, P)), tri, causal, hidden.reshape(P, -1)],
                          axis=1).astype(np.float32)


def laid_out(i):
    w_in, w_in2 = i["w_in"][0], i["w_in_2"][0]
    o_u, o_v, o_a, o_g = 3 * ATT, 3 * ATT + SG, 3 * ATT + 2 * SG, 3 * ATT + 2 * SG + CV
    ada_w = i["ada_w"][0]
    small = {
        "ada_b": columns(i["ada_b"][0]),
        "norm1_g": columns(i["norm1_g"][0]), "norm2_g": columns(i["norm2_g"][0]),
        "final_norm_g": columns(i["final_norm_g"]), "cv_w": tap_columns(i["cv_w"][0]), "cv_b": columns(i["cv_b"][0]),
        "cv_norm_g": columns(i["cv_norm_g"][0]), "cv_norm_b": columns(i["cv_norm_b"][0]),
        "ffn_conv_w": tap_columns(i["ffn_conv_w"][0]), "ffn_conv_b": columns(i["ffn_conv_b"][0]),
        "norm_mix_pre_2": columns(i["norm_mix_pre_2"][0]), "norm_mix_post_2": columns(i["norm_mix_post_2"][0]),
        "norm_ffn_pre_2": columns(i["norm_ffn_pre_2"][0]), "norm_ffn_post_2": columns(i["norm_ffn_post_2"][0]),
        "conv_mix_w_2": tap_columns(i["conv_mix_w_2"][0]), "conv_ffn_w_2": tap_columns(i["conv_ffn_w_2"][0]),
        "eps": np.full((P, 1), EPS, np.float32), "one": np.ones((P, 1), np.float32),
    }
    rel = np.zeros((HEADS, WIN + (2 * ROWS - 1) * RPB_W + WIN + SPAN), np.float32)
    rel[:, WIN:WIN + (2 * ROWS - 1) * RPB_W] = i["na_rpb"][0].reshape(HEADS, -1)
    starts = [(ROWS - 1 - row) * RPB_W + WIN - 1 - column for row, column in map(row_and_column, range(P))]
    b_cols, c_cols = blocks(w_in2[:, 3 * ATT:4 * ATT]), blocks(w_in2[:, 4 * ATT:5 * ATT])
    x_cols = blocks(w_in2[:, 5 * ATT:6 * ATT])
    a_blocks, g_blocks = blocks(w_in[:, o_a:o_g]), blocks(w_in[:, o_g:o_g + CV])
    sg_small = np.concatenate([
        np.repeat(i["sg_b"][0], SG // 4, axis=0).reshape(SC, P, P).transpose(1, 0, 2).reshape(P, -1),
        np.broadcast_to(i["sg_norm_g"][0], (P, SG)), np.broadcast_to(i["sg_norm_b"][0], (P, SG)),
        i["sg_w"][0].transpose(2, 0, 1).reshape(P, -1)], axis=1)
    arrays = {
        "x": by_feature(i["x"][0]), "ctx": by_feature(i["ctx"][0]),
        "cols": np.concatenate([small[n] for n, _ in COLUMN_SIZES], axis=1),
        "consts": shape_constants(), 
        "c_cols": np.stack([columns(i["c"][0]), columns(i["c_ctx"])], axis=2),
        "c_row": np.broadcast_to(i["c"][0], (P, D)), "sg_small": sg_small,
        "rel_rows": np.stack([rel[:, s:s + WINDOW] for s in starts]),
        "ada_turned": ada_w[:, :2 * D].reshape(KC, P, 2, D).transpose(2, 0, 1, 3), "ada_rows": ada_w[:, 2 * D:].T.reshape(4 * KC, P, D),
        "w_cv": np.stack([a_blocks, g_blocks], axis=1).reshape(2 * CC, P, KC, P),
        "w_sg_v": blocks(w_in[:, o_v:o_a]), "w_sg_u": blocks(w_in[:, o_u:o_v]),
        "w_q": blocks(w_in[:, 0:ATT]), "w_k": blocks(w_in[:, ATT:2 * ATT]), "w_v": wide(w_in[:, 2 * ATT:3 * ATT]),
        "w_out": blocks(i["w_out"][0]), "w_ffn_up": blocks(i["ffn_w_up"][0]), "w_ffn_down": blocks(i["ffn_w_down"][0]),
        "w_qk2": blocks(w_in2[:, 0:2 * ATT]), "w_v2": wide(w_in2[:, 2 * ATT:3 * ATT]),
        "w_conv3": np.stack([c_cols, x_cols, b_cols], axis=1).reshape(3 * AC, P, KC, P),
        "w_gates2": blocks(w_in2[:, 6 * ATT:6 * ATT + 2 * D]),
        "w_att2": blocks(i["w_att_branch_2"][0]), "w_convb2": blocks(i["w_conv_branch_2"][0]),
        "w_out2": blocks(i["w_out_2"][0]), "w_up2": blocks(i["w_up_2"][0]), "w_down2": blocks(i["w_down_2"][0]),
    }
    return {name: np.ascontiguousarray(a) for name, a in arrays.items()}


def kernel(**inputs):
    import concourse.bacc as bacc
    from concourse.bass_utils import run_bass_kernel_spmd

    arrays = laid_out({name: np.asarray(v) for name, v in inputs.items()})
    nc = bacc.Bacc("TRN2", target_bir_lowering=False, num_devices=1)
    io = {name: nc.dram_tensor(f"in_{name}", a.shape, mybir.dt.from_np(a.dtype), kind="ExternalInput").ap()
          for name, a in arrays.items()}
    out = nc.dram_tensor("out_x", (P, KC, T), F32, kind="ExternalOutput").ap()
    two_blocks(nc, io, out)
    result = run_bass_kernel_spmd(nc, [{f"in_{name}": a for name, a in arrays.items()}], core_ids=[0])
    got = result.results[0]["out_x"]
    return np.ascontiguousarray(got.transpose(2, 1, 0).reshape(1, T, D))
```

```python
from contextlib import ExitStack

import numpy as np

import concourse.bass as bass
from concourse import mybir
from concourse.alu_op_type import AluOpType as ALU

F32 = mybir.dt.float32
F32R = mybir.dt.float32r
ACT = mybir.ActivationFunctionType
AX = mybir.AxisListType

P = 128
D = 1024
KC = D // P
T = 512
TT = T // P
CTX = 256
CT = CTX // P
HD = 64
HEADS = 8
ATT = HEADS * HD
AC = ATT // P
SG = 256
SC = SG // P
CV = 256
CC = CV // P
TAPS = 31
PAD = TAPS // 2
DFF = 2816
FC = DFF // P
GRID_W = 64
ROWS = T // GRID_W
WIN = 16
SPAN = 32
GROUP = 8
CBLK = GRID_W // WIN
RPB_W = 31
WINDOW = WIN + (ROWS - 1) * RPB_W + SPAN
SPAN_START = [min(max(WIN * b - WIN // 2, 0), GRID_W - SPAN) for b in range(CBLK)]
SPAN_OFFS = sorted({SPAN_START[b] - WIN * b for b in range(CBLK)}, reverse=True)
SCALE = HD ** -0.5
EPS = 1e-6
NEG = -1e30
SLOT = 1024

COLUMN_SIZES = [
    ("ada_b", 6 * KC), ("norm1_g", KC), ("norm2_g", KC), ("final_norm_g", KC),
    ("cv_w", CC * TAPS), ("cv_b", CC), ("cv_norm_g", CC), ("cv_norm_b", CC),
    ("ffn_conv_w", FC * 3), ("ffn_conv_b", FC),
    ("norm_mix_pre_2", KC), ("norm_mix_post_2", KC), ("norm_ffn_pre_2", KC), ("norm_ffn_post_2", KC),
    ("conv_mix_w_2", AC * 3), ("conv_ffn_w_2", 2 * FC * 3), ("eps", 1), ("one", 1),
]
COLUMNS = {}
_at = 0
for _name, _n in COLUMN_SIZES:
    COLUMNS[_name] = (_at, _n)
    _at += _n
N_COLUMNS = _at

CONST_SIZES = [
    ("identity", P), ("group_mean", P), ("minus_ones", P), ("minus_tri", P), ("causal_neg", P),
    ("window_neg", len(SPAN_OFFS) * SPAN),
]
CONSTS = {}
_at = 0
for _name, _n in CONST_SIZES:
    CONSTS[_name] = (_at, _n)
    _at += _n
N_CONSTS = _at


class Queue:

    def __init__(self, engine, sem):
        self.engine, self.sem, self.count, self.waited = engine, sem, 0, {}

    def wait(self, *after):
        need = {}
        for sem, count in flat(after):
            if count > self.waited.get(sem.num, 0):
                self.waited[sem.num] = count
                need[sem.num] = (sem, count)
        for sem, count in need.values():
            self.engine.wait_ge(sem, count)

    def do(self, step, *after):
        self.wait(*after)
        self.count += 1
        step(self.engine).then_inc(self.sem, 1)
        return (self.sem, self.count)

    def load(self, counter, dst, src, *after):
        self.wait(*after)
        counter[1] += 16
        self.engine.dma_start(dst, src).then_inc(counter[0], 16)
        return (counter[0], counter[1])


def flat(marks):
    out = []
    for m in marks:
        if m is None:
            continue
        out += flat(m) if isinstance(m, list) else [m]
    return out


class Banks:

    def __init__(self, tensors, turning):
        self.tensors, self.free, self.turning, self.at = tensors, [None] * len(tensors), turning, -1

    def take(self):
        self.at = (self.at + 1) % self.turning
        return self.at


class WeightStream:

    RAW, SPLIT = 3, 3

    def __init__(self, order, pauses, raw, hi, lo, counters, sync, act, dve):
        self.order, self.pauses, self.raw, self.hi, self.lo = order, list(pauses), raw, hi, lo
        self.counters = counters
        self.sync, self.act, self.dve, self.takers = sync, act, dve, {}
        self.raw_free, self.split_free = [None] * self.RAW, [None] * self.SPLIT
        self.arrived, self.ready = {}, {}
        self.loaded = self.prepared = self.n_split = self.next = self.used = 0
        for _ in range(self.RAW):
            self.load_next()

    def load_next(self):
        i = self.loaded
        if i < len(self.order):
            _, src, n, _ = self.order[i]
            slot = i % self.RAW
            dst = self.raw[:, slot, 0:n]
            if len(src.shape) == 3:
                dst = dst.rearrange("p (k n) -> p k n", k=src.shape[1])
            self.arrived[i] = self.sync.load(self.counters[slot], dst, src, self.raw_free[slot])
            self.loaded += 1

    def prepare_next(self):
        i = self.prepared
        kind, _, n, detail = self.order[i]
        slot = i % self.RAW
        tile = self.raw[:, slot, 0:n]
        if kind == "split":
            s = self.n_split % self.SPLIT
            self.n_split += 1
            hi_s, lo_s = self.hi[:, s, 0:n], self.lo[:, s, 0:n]
            hi = self.act.do(lambda e: e.activation(hi_s, tile, ACT.Copy), self.arrived[i], self.split_free[s])
            lo = self.dve.do(lambda e: e.tensor_tensor(lo_s, tile, hi_s.bitcast(F32), ALU.subtract),
                             self.arrived[i], hi, self.split_free[s])
            self.ready[i] = (s, [hi, lo], detail)
            self.raw_free[slot] = [lo]
        else:
            self.raw_free[slot] = [self.takers[kind](tile, detail, self.arrived[i])]
        self.prepared += 1
        self.load_next()

    def prepare_ahead(self):
        while (self.prepared < len(self.order) and self.n_split < self.used + self.SPLIT
               and self.prepared not in self.pauses[:1]):
            self.prepare_next()

    def resume(self):
        if self.prepared in self.pauses[:1]:
            self.pauses.pop(0)
            self.prepare_next()

    def next_tile(self, ahead=True):
        if ahead:
            self.prepare_ahead()
        while self.order[self.next][0] != "split":
            self.next += 1
        self.next += 1
        self.used += 1
        return self.ready[self.next - 1]


def two_blocks(nc, io, out):
    with ExitStack() as whole:
        def sb(stack, name, shape, dt=F32):
            return stack.enter_context(nc.sbuf_tensor(name, shape, dt))

        def counter(name):
            return [whole.enter_context(nc.semaphore(name)), 0]

        pe, act, dve, pool, sync = (
            Queue(engine, counter(f"s_{name}")[0])
            for name, engine in (("pe", nc.tensor), ("act", nc.scalar), ("dve", nc.vector), ("pool", nc.gpsimd),
                                 ("sync", nc.sync)))

        def everyone():
            return [(q.sem, q.count) for q in (pe, act, dve, pool)]

        x = sb(whole, "x_res", [P, KC, T])
        h_hi = sb(whole, "h_hi", [P, KC, T], F32R)
        h_lo = sb(whole, "h_lo", [P, KC, T], F32R)
        cols = sb(whole, "cols_sb", [P, N_COLUMNS])
        consts = sb(whole, "consts_sb", [P, N_CONSTS])
        ones = sb(whole, "ones", [P, 1])
        mod = sb(whole, "mod", [P, 6 * KC])
        gain = sb(whole, "gain", [P, KC])
        squares = sb(whole, "squares", [P, 2, T])
        normed = sb(whole, "normed", [P, 2, T])
        exact = sb(whole, "exact", [P, 2, T])
        small = sb(whole, "small", [P, TT])
        std = sb(whole, "std", [P, 2 * TT])
        rstd = sb(whole, "rstd", [P, 2 * TT])
        raw = sb(whole, "raw_w", [P, WeightStream.RAW, SLOT])
        w_hi = sb(whole, "w_hi", [P, WeightStream.SPLIT, SLOT], F32R)
        w_lo = sb(whole, "w_lo", [P, WeightStream.SPLIT, SLOT], F32R)
        bank = [whole.enter_context(nc.psum_tensor(f"bank{b}", [P, T], F32)) for b in range(8)]
        banks = Banks(bank, 6)
        free = banks.free
        NORM_BANKS = (6, 7)

        def col(name, i=0):
            at = COLUMNS[name][0] + i
            return cols[:, at:at + 1]

        def cols_of(name):
            at, n = COLUMNS[name]
            return cols[:, at:at + n]

        def const(name):
            at, n = CONSTS[name]
            return consts[:, at:at + n]

        identity = const("identity")

        SIDE_BY_SIDE = 2

        def blocks_of(name):
            w = io[name]
            n_out, _, kc, _ = w.shape
            sizes = [kc] if kc <= KC else [8, 7, 7]
            return [[("split", w[o, :, sum(sizes[:i]):sum(sizes[:i + 1]), :], n * P, (sum(sizes[:i]), n))
                     for i, n in enumerate(sizes)] for o in range(n_out)]

        def wide_of(name):
            w = io[name]
            return [[("split", w[t, :, :, :], w.shape[2] * w.shape[3], (t * w.shape[2], w.shape[2]))]
                    for t in range(w.shape[0])]

        def in_turn(plans, extra=(), each=0):
            extra, order = list(extra), []
            for tile in (t for tiles in plans for t in tiles):
                order.append(tile)
                order += extra[:each]
                del extra[:each]
            return order + extra

        order = [("ada_turned", io["ada_turned"][half, k, :, :], SLOT, (half, k)) for half in (1, 0) for k in range(KC)]
        rest = [("ada_rows", io["ada_rows"][j - 2 * KC, :, :], SLOT, j) for j in range(2 * KC, 6 * KC)]
        gated, spatial = blocks_of("w_cv"), blocks_of("w_sg_v") + blocks_of("w_sg_u")
        order += in_turn(gated[:SIDE_BY_SIDE + 1])
        few = len(gated) - SIDE_BY_SIDE - 1 + len(spatial)
        order += in_turn(gated[SIDE_BY_SIDE + 1:] + spatial, rest[:few], 1)
        order += in_turn(blocks_of("w_k") + wide_of("w_v") + blocks_of("w_q")[:1], rest[few:], 3)
        order += in_turn(blocks_of("w_q")[1:])
        for half in (range(AC, KC), range(AC)):
            order += [("split", io["w_out"][o, :, half[0]:half[-1] + 1, :], AC * P, (half[0], AC)) for o in range(KC)]
        pauses = [len(order) + 1]
        up = blocks_of("w_ffn_up")
        order += in_turn([up[i] for f in range(FC) for i in (f, FC + f)])
        order += in_turn(blocks_of("w_ffn_down"))
        pauses.append(len(order) + 1)
        order += in_turn(blocks_of("w_qk2") + wide_of("w_v2"))
        order += in_turn(blocks_of("w_conv3"))
        gates, atts, convs = blocks_of("w_gates2"), blocks_of("w_att2"), blocks_of("w_convb2")
        order += in_turn([p for o in range(KC) for p in (gates[o], gates[KC + o], atts[o], convs[o])])
        order += in_turn(blocks_of("w_out2"))
        pauses.append(len(order) + 1)
        up = blocks_of("w_up2")
        order += in_turn([up[i] for f in range(FC) for i in (f, FC + f)])
        order += in_turn(blocks_of("w_down2"))

        silu_c = sb(whole, "silu_c", [P, KC, 2])
        c_in = sync.load(counter("s_c"), silu_c[:, :, :], io["c_cols"])
        stream = WeightStream(order, pauses, raw, w_hi, w_lo, [counter(f"s_raw{i}") for i in range(WeightStream.RAW)],
                              sync, act, dve)
        x_in = [sync.load(counter(f"s_x{i}"), x[:, 2 * i:2 * i + 2, :], io["x"][:, 2 * i:2 * i + 2, :])
                for i in range(KC // 2)]
        cols_in = sync.load(counter("s_cols"), cols[:, :], io["cols"])
        consts_in = sync.load(counter("s_consts"), consts[:, :], io["consts"])
        ones_set = dve.do(lambda e: e.memset(ones[:, :], 1.0))

        def product(e, dst, lhs_hi, lhs_lo, rhs_hi, rhs_lo, first, last):
            e.matmul(dst, lhs_hi, rhs_lo, start=first, stop=False)
            e.matmul(dst, lhs_lo, rhs_hi, start=False, stop=False)
            return e.matmul(dst, lhs_hi, rhs_hi, start=False, stop=last)

        def linear_steps(b, n_tiles, chunks, src_hi, src_lo, src_marks):
            first, last = min(chunks), max(chunks)
            for _ in range(n_tiles):
                s, w_marks, (k0, n) = stream.next_tile()
                for j in range(n):
                    k, w = k0 + j, slice(j * P, (j + 1) * P)
                    mark = pe.do(lambda e: product(e, bank[b][:, :], w_hi[:, s, w], w_lo[:, s, w], src_hi[:, k, :],
                                                   src_lo[:, k, :], k == first, k == last),
                                 w_marks, src_marks[k], free[b] if k == first else None)
                    if j == n - 1:
                        stream.split_free[s] = [mark]
                    yield
            return b, mark

        def finished(steps):
            while True:
                try:
                    next(steps)
                except StopIteration as end:
                    return end.value

        def linear(n_tiles, k_total, src_hi, src_lo, src_marks):
            return finished(linear_steps(banks.take(), n_tiles, range(k_total), src_hi, src_lo, src_marks))

        def linear_side_by_side(k_total, src_hi, src_lo, src_marks):
            tiles = [stream.next_tile(ahead=(i == 0)) for i in range(SIDE_BY_SIDE)]
            out_banks = [banks.take() for _ in tiles]
            marks = [None] * len(tiles)
            for k in range(k_total):
                w = slice(k * P, (k + 1) * P)
                for i, (s, w_marks, _) in enumerate(tiles):
                    b = out_banks[i]
                    marks[i] = pe.do(lambda e: product(e, bank[b][:, :], w_hi[:, s, w], w_lo[:, s, w], src_hi[:, k, :],
                                                       src_lo[:, k, :], k == 0, k == k_total - 1),
                                     w_marks, src_marks[k], free[b] if k == 0 else None)
            for i, (s, _, _) in enumerate(tiles):
                stream.split_free[s] = [marks[i]]
            return list(zip(out_banks, marks))

        def linears(n, k_total, src_hi, src_lo, src_marks):
            yield from linear_side_by_side(k_total, src_hi, src_lo, src_marks)
            for _ in range(n - SIDE_BY_SIDE):
                yield linear(1, k_total, src_hi, src_lo, src_marks)

        def split(value, mark, dst_hi, dst_lo, dst_free=None):
            hi = act.do(lambda e: e.activation(dst_hi, value, ACT.Copy), mark, dst_free)
            lo = dve.do(lambda e: e.tensor_tensor(dst_lo, value, dst_hi.bitcast(F32), ALU.subtract), mark, hi, dst_free)
            return [hi, lo]

        square_free, buffer_free = [None, None], [None, None]
        turn = {"norm": 0, "square": 0, "buffer": 0}

        class Norm:

            def __init__(self, n_tok, total=None, pairs=None):
                self.n_tok, self.total, self.total_mark = n_tok, total, everyone()
                self.pairs, self.pair_free, self.pair = pairs, [everyone()] * 4, []
                self.waiting, self.seen, self.summed = None, 0, 0
                self.b = NORM_BANKS[turn["norm"] % 2]
                self.at = (turn["norm"] % 2) * TT
                turn["norm"] += 1

            def square(self, v, mark, scale=1.0):
                if self.pairs is not None:
                    return self.square_of_pair(v, mark)
                self.add_waiting()
                first, self.seen = self.seen == 0, self.seen + 1
                if first:
                    self.total_mark = act.do(lambda e: e.activation(self.total, v, ACT.Square, scale=scale), mark,
                                             self.total_mark)
                    return
                i = turn["square"] % len(square_free)
                turn["square"] += 1
                m = act.do(lambda e: e.activation(squares[:, i, 0:self.n_tok], v, ACT.Square, scale=scale), mark,
                           square_free[i])
                self.waiting = (i, m)

            def square_of_pair(self, v, mark):
                i, self.seen = self.seen % 4, self.seen + 1
                self.pair.append(act.do(lambda e: e.activation(self.pairs[:, i, :], v, ACT.Square), mark, self.pair_free[i]))
                if self.seen > KC - 2:
                    self.sum_over_partitions(self.pairs[:, i, :], self.pair.pop(), KC // 2 + 1)
                elif i % 2:
                    one, other = self.pairs[:, i - 1, :], self.pairs[:, i, :]
                    m = pool.do(lambda e: e.tensor_tensor(one, one, other, ALU.add), self.pair)
                    self.sum_over_partitions(one, m, KC // 2 + 1)
                    self.pair_free[i - 1] = self.pair_free[i] = [self.mark]
                    self.pair = []

            def add_waiting(self):
                if self.waiting is not None:
                    (i, m), self.waiting = self.waiting, None
                    part = squares[:, i, 0:self.n_tok]
                    self.total_mark = dve.do(lambda e: e.tensor_tensor(self.total, self.total, part, ALU.add), m,
                                             self.total_mark)
                    square_free[i] = [self.total_mark]

            def sum_over_partitions(self, part, mark, parts):
                k, nt = self.summed, self.n_tok // P
                self.summed += 1

                def sums(e):
                    for t in range(nt):
                        mm = e.matmul(bank[self.b][:, t:t + 1], part[:, t * P:(t + 1) * P], ones[:, :],
                                      start=(k == 0 and t == 0), stop=(k == parts - 1 and t == nt - 1),
                                      skip_group_check=True)
                    return mm
                self.mark = pe.do(sums, mark, ones_set, free[self.b] if k == 0 else None)

            def end_of_sums(self):
                if self.pairs is None and not self.summed:
                    self.sum_over_partitions(self.total, self.total_mark, 2)
                    (i, m), self.waiting = self.waiting, None
                    self.sum_over_partitions(squares[:, i, 0:self.n_tok], m, 2)
                    square_free[i] = [self.mark]
                stream.resume()

            def factors(self):
                self.end_of_sums()
                nt, b, at = self.n_tok // P, self.b, self.at
                s, f = std[:, at:at + nt], rstd[:, at:at + nt]
                root = act.do(lambda e: e.activation(s, bank[b][:, 0:nt], ACT.Sqrt, scale=1.0 / D, bias=col("eps")),
                              self.mark, cols_in)
                return f, [dve.do(lambda e: e.reciprocal(f, s), root), root]

            def finish(self):
                f, marks = self.factors()
                return self.b, spread(f, marks, self.b)

        def spread(f, marks, b):
            def mm(e):
                for t in range(f.shape[1]):
                    m = e.matmul(bank[b][:, t * P:(t + 1) * P], f[:, t:t + 1].to_broadcast([P, P]), identity,
                                 start=True, stop=True)
                return m
            return pe.do(mm, marks, consts_in)

        def apply_norm(factor_bank, factor_mark, chunk, chunk_marks, n_tok, a_of, b_of, params, dst_hi, dst_lo, dst_free):
            marks, factor = [], bank[factor_bank][:, 0:n_tok]
            lows, last = [], None
            for k in range(KC):
                i = turn["buffer"] % 2
                turn["buffer"] += 1
                src, v, n, a = chunk(k), exact[:, i, 0:n_tok], normed[:, i, 0:n_tok], a_of(k)
                if b_of is None:
                    last = dve.do(lambda e: e.scalar_tensor_tensor(out=v, in0=src, scalar=a, in1=factor, op0=ALU.mult,
                                                                   op1=ALU.mult),
                                  factor_mark, chunk_marks[k], params, buffer_free[i])
                    value, hi = last, act.do(lambda e: e.activation(dst_hi(k), v, ACT.Copy), last, dst_free)
                else:
                    last = dve.do(lambda e: e.tensor_tensor(n, src, factor, ALU.mult),
                                  factor_mark, chunk_marks[k], buffer_free[i])
                    value, hi = modulate(n, last, a, b_of(k), params, i, dst_hi(k), dst_free)
                lows.append((k, i, v, value, hi))
                while len(lows) > (1 if k < KC - 1 else 0):
                    marks.append(low_part(dst_hi, dst_lo, dst_free, *lows.pop(0)))
            free[factor_bank] = [last]
            return marks

        def modulate(n, mark, a, b, params, i, hi_k, dst_free):
            v = exact[:, i, 0:n.shape[-1]]
            value = pool.do(lambda e: e.tensor_scalar(v, n, a, b, ALU.mult, ALU.add), mark, params, buffer_free[i])
            return value, act.do(lambda e: e.activation(hi_k, as_read(n, hi_k), ACT.Identity, scale=a, bias=b),
                                 mark, params, dst_free)

        def low_part(dst_hi, dst_lo, dst_free, k, i, v, value, hi):
            lo = dve.do(lambda e: e.tensor_tensor(dst_lo(k), as_read(v, dst_lo(k)), dst_hi(k).bitcast(F32), ALU.subtract),
                        value, hi, dst_free)
            buffer_free[i] = [value, hi, lo]
            return [hi, lo]

        def as_read(a, like):
            return a if len(like.shape) == 2 else a.rearrange("p (r g c) -> p r g c", g=like.shape[2], c=like.shape[3])

        def flat_chunks(h):
            return lambda k: h[:, k, :]

        def causal_or_centred(src, y, w_col, w0, shifts, mark, y_free, bias=None):
            centre = shifts.index(0)
            w = col(w_col, w0 + centre)
            if bias is None:
                m = act.do(lambda e: e.activation(y, src, ACT.Copy, scale=w), mark, y_free)
            else:
                m = act.do(lambda e: e.activation(y, src, ACT.Identity, scale=w, bias=bias), mark, y_free)
            for i, s in enumerate(shifts):
                if s == 0:
                    continue
                w = col(w_col, w0 + i)
                to, frm = (slice(-s, T), slice(0, T + s)) if s < 0 else (slice(0, T - s), slice(s, T))
                m = dve.do(lambda e: e.scalar_tensor_tensor(out=y[:, to], in0=src[:, frm], scalar=w, in1=y[:, to],
                                                            op0=ALU.mult, op1=ALU.add), mark, m)
            return m

        ada = ExitStack()
        mod_raw = sb(ada, "mod_raw", [P, 6 * KC])
        mod_ctx = sb(ada, "mod_ctx", [P, 2 * KC])
        gain_ctx = sb(ada, "gain_ctx", [P, KC])

        mixer = ExitStack()
        k_loc = sb(mixer, "k_loc", [P, AC, T])
        q_loc = sb(mixer, "q_loc", [P, AC, T])
        k_ctx = sb(mixer, "k_ctx", [P, AC, CTX])
        v_loc = sb(mixer, "v_loc", [P, CBLK, ATT])
        v_mid = sb(mixer, "v_mid", [P, CBLK - 1, ATT])
        v_ctx = sb(mixer, "v_ctx", [P, CT, ATT])
        cv_in = sb(mixer, "cv_in", [P, CC, T + 2 * PAD])
        cv_acc = sb(mixer, "cv_acc", [P, CC, T])
        sg_out = sb(mixer, "sg_out", [P, SC, T])
        sg_v = sb(mixer, "sg_v", [P, TT, SG])
        sg_small = sb(mixer, "sg_small_sb", [P, SC * P + 2 * SG + 4 * P])
        sg_b = sg_small[:, 0:SC * P].rearrange("p (s t) -> p s t", s=SC)
        sg_norm_g = sg_small[:, SC * P:SC * P + SG]
        sg_norm_b = sg_small[:, SC * P + SG:SC * P + 2 * SG]
        sg_wT = sg_small[:, SC * P + 2 * SG:SC * P + 2 * SG + 4 * P].rearrange("p (g t) -> p g t", g=4)
        stats = sb(mixer, "stats", [P, 5 * TT])
        sg_square = sb(mixer, "sg_square", [P, SG])
        cv_scratch = sb(mixer, "cv_scratch", [P, CC, T])

        context = ExitStack()
        silu_row = sb(context, "silu_row", [P, D])
        ada_products = sb(context, "ada_products", [P, D])
        xc = sb(context, "xc", [P, KC, CTX])
        hc_hi = sb(context, "hc_hi", [P, KC, CTX], F32R)
        hc_lo = sb(context, "hc_lo", [P, KC, CTX], F32R)

        silu_c_m = act.do(lambda e: e.activation(silu_c[:, :, :], silu_c[:, :, :], ACT.Silu), c_in)

        ada_marks, junk_free = {}, [None]

        def ada_turned(tile, what, mark):
            half, k = what

            def mm(e):
                for n in range(D // T):
                    m = e.matmul(bank[2 * half + n][0:2, :], silu_c[:, k, :], tile[:, n * T:(n + 1) * T],
                                 start=(k == 0), stop=(k == KC - 1))
                return m
            ada_marks[what] = pe.do(mm, mark, silu_c_m)
            return ada_marks[what]

        def turned_back(half, rows):
            copies = []
            for n, q in ((0, act), (1, dve)):
                src, dst = bank[2 * half + n][0:2, :], rows[0:2, n, :]
                step = (lambda e: e.activation(dst, src, ACT.Copy)) if q is act else (lambda e: e.tensor_copy(dst, src))
                copies.append(q.do(step, ada_marks[half, KC - 1]))
                free[2 * half + n] = [copies[n]]

            def mm(e):
                for j in range(KC):
                    m = e.transpose(bank[4][:, 2 * (half * KC + j):2 * (half * KC + j) + 2],
                                    rows[0:2, j // 4, j % 4 * P:(j % 4 + 1) * P], identity[0:2, 0:2])
                return m
            return pe.do(mm, copies, consts_in)

        cv_mark, cv_taps, taps_done = [None] * CC, [0] * CC, [None]
        pads = [dve.do(lambda e: e.memset(cv_in[:, :, s], 0.0)) for s in (slice(0, PAD), slice(PAD + T, T + 2 * PAD))]

        def conv_taps(n):
            for c, q in ((0, dve), (1, pool)):
                for i in range(cv_taps[c], min(cv_taps[c] + n, TAPS) if cv_mark[c] else 0):
                    src, w, acc = cv_in[:, c, i:i + T], col("cv_w", c * TAPS + i), cv_acc[:, c, :]
                    if i and q is pool:
                        part = q_loc[:, 2 + i % 2, :]
                        m = pool.do(lambda e: e.tensor_scalar(part, src, w, 0.0, ALU.mult, ALU.add), cv_mark[c])
                        cv_mark[c] = taps_done[0] = pool.do(lambda e: e.tensor_tensor(acc, acc, part, ALU.add), m)
                        continue
                    if i == 0:
                        step = lambda e: e.tensor_scalar(acc, src, w, col("cv_b", c), ALU.mult, ALU.add)
                    else:
                        step = lambda e: e.scalar_tensor_tensor(out=acc, in0=src, scalar=w, in1=acc, op0=ALU.mult, op1=ALU.add)
                    cv_mark[c] = q.do(step, cv_mark[c], pads, cols_in)
                if cv_mark[c]:
                    cv_taps[c] = min(cv_taps[c] + n, TAPS)

        def ada_rows(tile, j, mark):
            ada_marks[j] = dve.do(lambda e: e.tensor_tensor_reduce(
                out=ada_products[:, :], in0=tile, in1=silu_row[:, :], scale=1.0, scalar=0.0, op0=ALU.mult, op1=ALU.add,
                accum_out=mod_raw[:, j:j + 1]), mark, silu_row_m, junk_free[0])
            junk_free[0] = ada_marks[j]
            conv_taps(1)
            return ada_marks[j]

        stream.takers = {"ada_turned": ada_turned, "ada_rows": ada_rows}
        norm1 = Norm(T, exact[:, 0, :])
        for k in range(KC):
            norm1.square(x[:, k, :], x_in[k // 2])
            stream.prepare_next()
        for _ in range(2):
            stream.prepare_next()
        r, m = norm1.finish()
        factor = cv_acc[:, 0, :]
        factor_in = act.do(lambda e: e.activation(factor, bank[r][:, :], ACT.Copy), m)
        free[r] = [factor_in]
        for _ in range(2):
            stream.prepare_next()
        turned_back(1, sg_out)
        x_normed, x_normed_marks = [], []
        for k in range(KC):
            n = (k_loc if k < KC // 2 else v_loc)[:, k % (KC // 2), :]
            x_normed.append(n)
            x_normed_marks.append((pool if k % 3 == 2 else dve).do(
                lambda e: e.tensor_tensor(n, x[:, k, :], factor, ALU.mult), factor_in, x_in[k // 2]))
        for _ in range(4):
            stream.prepare_next()
        turned = turned_back(0, cv_scratch)
        row_in = pool.load(counter("s_crow"), silu_row[:, :], io["c_row"], stream.arrived[2 * KC + SIDE_BY_SIDE - 1])
        xc_in = pool.load(counter("s_xc"), xc[:, :, :], io["ctx"])
        sg_in = pool.load(counter("s_sg"), sg_small[:, :], io["sg_small"])
        buffer_free[:] = [everyone(), everyone()]
        ada_b, shift_scale = cols_of("ada_b"), bank[4][:, 0:4 * KC].rearrange("p (j n) -> p n j", n=2)
        mod_m = dve.do(lambda e: e.tensor_tensor(mod[:, 0:2 * KC], shift_scale[:, 0, :], ada_b[:, 0:2 * KC], ALU.add),
                       turned, cols_in)
        gain_m = dve.do(lambda e: e.scalar_tensor_tensor(out=gain[:, :], in0=mod[:, KC:2 * KC], scalar=1.0,
                                                         in1=cols_of("norm1_g"), op0=ALU.add, op1=ALU.mult), mod_m)
        mod_x = dve.do(lambda e: e.tensor_tensor(mod_ctx[:, :], shift_scale[:, 1, :], ada_b[:, 0:2 * KC], ALU.add),
                       turned, cols_in)
        free[4] = [mod_x]
        gain_x = dve.do(lambda e: e.scalar_tensor_tensor(out=gain_ctx[:, :], in0=mod_ctx[:, KC:2 * KC], scalar=1.0,
                                                         in1=cols_of("norm1_g"), op0=ALU.add, op1=ALU.mult), mod_x)
        for _ in range(SIDE_BY_SIDE):
            stream.prepare_next()

        def grid_of(a):
            return a.rearrange("p (g r c) -> p r g c", r=ROWS, c=GROUP)

        def rows_of(a):
            return a.rearrange("p (r g c) -> p r g c", r=ROWS, c=GROUP)

        h_marks = []
        dst_hi, dst_lo = lambda k: grid_of(h_hi[:, k, :]), lambda k: grid_of(h_lo[:, k, :])
        for k in range(KC):
            value, hi = modulate(x_normed[k], x_normed_marks[k], gain[:, k:k + 1], mod[:, k:k + 1], gain_m, k % 2,
                                 dst_hi(k), None)
            h_marks.append(low_part(dst_hi, dst_lo, None, k, k % 2, exact[:, k % 2, :], value, hi))
        silu_row_m = act.do(lambda e: e.activation(silu_row[:, :], silu_row[:, :], ACT.Silu), row_in)

        cv_products = linears(2 * CC, KC, h_hi, h_lo, h_marks)
        for c in range(CC):
            (ba, ma), (bg, mg) = next(cv_products), next(cv_products)
            dst = cv_in[:, c, PAD:PAD + T]
            sig = act.do(lambda e: e.activation(rows_of(dst), grid_of(bank[bg][:, :]), ACT.Sigmoid), mg)
            cv_mark[c] = dve.do(lambda e: e.tensor_tensor(rows_of(dst), grid_of(bank[ba][:, :]), rows_of(dst), ALU.mult),
                                ma, sig)
            free[bg], free[ba] = [sig], [cv_mark[c]]
            if c == 0:
                stream.prepare_ahead()
                norm_ctx = Norm(CTX, k_ctx[:, 0, :])
                for k in range(KC):
                    norm_ctx.square(xc[:, k, :], xc_in)

        sg_vT, sg_vT_marks = cv_scratch, []
        for c in range(SC):
            b, m = linear(1, KC, h_hi, h_lo, h_marks)
            sg_vT_marks.append(act.do(lambda e: e.activation(rows_of(sg_vT[:, c, :]), grid_of(bank[b][:, :]),
                                                             ACT.Gelu_apprx_tanh), m))
            free[b] = [sg_vT_marks[c]]
            conv_taps(1)
            if c == 0:
                stream.prepare_ahead()
                r, m = norm_ctx.finish()
                hc_marks = apply_norm(r, m, lambda k: xc[:, k, :], [xc_in] * KC, CTX, lambda k: gain_ctx[:, k:k + 1],
                                      lambda k: mod_ctx[:, k:k + 1], gain_x, flat_chunks(hc_hi), flat_chunks(hc_lo), None)
        sg_u = []
        for c in range(SC):
            b, m = linear(1, KC, h_hi, h_lo, h_marks)
            sg_u.append(act.do(lambda e: e.activation(rows_of(sg_out[:, c, :]), grid_of(bank[b][:, :]),
                                                      ACT.Gelu_apprx_tanh), m))
            free[b] = [sg_u[c]]
            conv_taps(1)
        sums, means, square_sums, stds, factors = (stats[:, n * TT:(n + 1) * TT] for n in range(5))
        summed = []
        for t in range(TT):
            v, b = sg_v[:, t, :], banks.take()

            def turn_over(e):
                for c in range(SC):
                    m = e.transpose(bank[b][:, c * P:(c + 1) * P], sg_vT[:, c, t * P:(t + 1) * P], identity)
                return m
            m = pe.do(turn_over, sg_vT_marks, consts_in, free[b])
            summed.append(act.do(lambda e: e.activation(v, bank[b][:, 0:SG], ACT.Copy, accum_out=sums[:, t:t + 1]), m))
            free[b] = [summed[t]]
        mean = dve.do(lambda e: e.tensor_scalar(means, sums, 1.0 / SG, None, ALU.mult), summed)
        centred = [dve.do(lambda e: e.tensor_scalar(sg_v[:, t, :], sg_v[:, t, :], means[:, t:t + 1], None, ALU.subtract), mean)
                   for t in range(TT)]
        squared = [None]
        for t in range(TT):
            squared.append(act.do(lambda e: e.activation(sg_square[:, :], sg_v[:, t, :], ACT.Square,
                                                         accum_out=square_sums[:, t:t + 1]), centred[t], squared[-1]))
        m = act.do(lambda e: e.activation(stds, square_sums, ACT.Sqrt, scale=1.0 / SG, bias=col("eps")), squared)
        m = dve.do(lambda e: e.reciprocal(factors, stds), m)
        sg_v_ready = []
        for t in range(TT):
            v = sg_v[:, t, :]
            g = dve.do(lambda e: e.scalar_tensor_tensor(out=v, in0=v, scalar=factors[:, t:t + 1], in1=sg_norm_g,
                                                        op0=ALU.mult, op1=ALU.mult), m, sg_in)
            sg_v_ready.append(dve.do(lambda e: e.tensor_tensor(v, v, sg_norm_b, ALU.add), g))

        q_marks, k_marks, kc_marks = [None] * AC, [None] * AC, [None] * AC
        for c in range(AC):
            b, bc = banks.take(), banks.take()
            s, w_marks, _ = stream.next_tile()

            def mm(e):
                for rhs_hi, rhs_lo, dst in ((h_hi, h_lo, bank[b][:, :]), (hc_hi, hc_lo, bank[bc][:, 0:CTX])):
                    for k in range(KC):
                        w = slice(k * P, (k + 1) * P)
                        m = product(e, dst, w_hi[:, s, w], w_lo[:, s, w], rhs_hi[:, k, :], rhs_lo[:, k, :], k == 0, k == KC - 1)
                return m
            m = pe.do(mm, w_marks, h_marks, hc_marks, free[b], free[bc])
            stream.split_free[s] = [m]
            k_marks[c] = act.do(lambda e: e.activation(k_loc[:, c, :], bank[b][:, :], ACT.Copy), m)
            kc_marks[c] = act.do(lambda e: e.activation(k_ctx[:, c, :], bank[bc][:, 0:CTX], ACT.Copy), m)
            free[b], free[bc] = [k_marks[c]], [kc_marks[c]]

        vb = [banks.take() for _ in range(TT + CT)]
        v_marks = [None] * len(vb)
        for tile in range(ATT * D // (P * SLOT)):
            s, w_marks, (k0, n) = stream.next_tile()
            for t in range(len(vb)):
                own_hi, own_lo = (h_hi, h_lo) if t < TT else (hc_hi, hc_lo)
                tok = slice(t % TT * P, (t % TT + 1) * P)

                def mm(e):
                    for j in range(n):
                        k, w = k0 + j, slice(j * ATT, (j + 1) * ATT)
                        m = product(e, bank[vb[t]][:, :], own_hi[:, k, tok], own_lo[:, k, tok], w_hi[:, s, w],
                                    w_lo[:, s, w], k == 0, k == KC - 1)
                    return m
                v_marks[t] = pe.do(mm, w_marks, h_marks, hc_marks, free[vb[t]] if tile == 0 else None)
            stream.split_free[s] = [v_marks[-1]]
        for t in range(len(vb)):
            dst = v_loc[:, t, :] if t < TT else v_ctx[:, t - TT, :]
            v_marks[t] = act.do(lambda e: e.activation(dst, bank[vb[t]][:, :], ACT.Copy), v_marks[t])
            free[vb[t]] = [v_marks[t]]
        v_moved, low, high = counter("s_v_moved"), slice(0, P // 2), slice(P // 2, P)
        sync.load(v_moved, v_mid[low, :, :], v_loc[high, 0:CBLK - 1, :], v_marks)
        moved = sync.load(v_moved, v_mid[high, :, :], v_loc[low, 1:CBLK, :], v_marks)

        assert len(ada_marks) == 2 * KC + 4 * KC
        context.close()
        handed = everyone()
        attention = ExitStack()
        rel = sb(attention, "rel", [P, HEADS, WINDOW])
        biased = sb(attention, "biased", [P, len(SPAN_OFFS), HEADS, SPAN // GROUP, ROWS, GROUP])
        rel_in = sync.load(counter("s_rel"), rel[:, :, :], io["rel_rows"], handed)

        sg_done = []
        for c in range(SC):
            b = banks.take()

            def mix(e):
                for t in range(TT):
                    for g in (2 * c, 2 * c + 1):
                        p0 = (g % 2) * 64
                        m = e.matmul(bank[b][p0:p0 + 64, t * P:(t + 1) * P], sg_v[:, t, g * 64:(g + 1) * 64],
                                     sg_wT[:, g, :], start=True, stop=True)
                return m
            m = pe.do(mix, sg_v_ready, sg_in, free[b])
            mixed = bank[b][:, :].rearrange("p (t q) -> p t q", t=TT)
            bias = sg_b[:, c, :].unsqueeze(1).to_broadcast([P, TT, P])
            m = dve.do(lambda e: e.tensor_tensor(mixed, mixed, bias, ALU.add), m)
            m = dve.do(lambda e: e.tensor_tensor(sg_out[:, c, :], bank[b][:, :], sg_out[:, c, :], ALU.mult), m, sg_u[c])
            free[b] = [m]
            sg_done.append(m)

        def take_queries(c, b, m):
            q_marks[c] = act.do(lambda e: e.activation(q_loc[:, c, :], bank[b][:, :], ACT.Copy, scale=SCALE), m,
                                taps_done)
            free[b] = [q_marks[c]]

        b, m = linear(1, KC, h_hi, h_lo, h_marks)
        take_queries(0, b, m)
        conv_taps(TAPS)

        bias_in = {}
        for h in range(HEADS):
            for v, off in enumerate(SPAN_OFFS):
                hidden = const("window_neg")[:, v * SPAN:(v + 1) * SPAN].rearrange("p (g c) -> p g c", c=GROUP)
                hidden = hidden.unsqueeze(1).to_broadcast([P, ROWS, SPAN // GROUP, GROUP])
                rows = rel[:, h, WIN + off:WIN + off + ROWS * RPB_W]
                rows = bass.AP(rows.tensor, rows.offset, [rows.ap[0], [RPB_W, ROWS], [GROUP, SPAN // GROUP], [1, GROUP]])
                bias_in[v, h] = pool.do(lambda e: e.tensor_tensor(
                    biased[:, v, h, :, :, :].rearrange("p g r c -> p r g c"), rows, hidden, ALU.add),
                    rel_in, consts_in, handed)

        mix_marks = [None] * KC

        probs, probs_t = normed, exact
        soft = sb(attention, "soft", [P, 2, 4])
        steps = [(h, b) for h in range(HEADS) for b in range(CBLK)]
        h_read = [None]

        assert len(ada_marks) == 2 * KC + 4 * KC
        mod_rest = dve.do(lambda e: e.tensor_tensor(mod[:, 2 * KC:], mod_raw[:, 2 * KC:], ada_b[:, 2 * KC:], ALU.add),
                          [ada_marks[j] for j in range(2 * KC, 6 * KC)])

        def add_gated(o, b, m, gate_at):
            g = mod[:, gate_at + o:gate_at + o + 1]
            x_marks[o] = dve.do(lambda e: e.scalar_tensor_tensor(
                out=x[:, o, :], in0=bank[b][:, :], scalar=g, in1=x[:, o, :], op0=ALU.mult, op1=ALU.add),
                m, mod_rest, x_marks[o])
            free[b] = [x_marks[o]]

        x_marks = [None] * KC

        def group_norms():
            b, chunks = NORM_BANKS[0], range(CC)
            mean_of = lambda src: lambda e: e.matmul(bank[b][:, :], const("group_mean"), src, start=True, stop=True)
            for c in chunks:
                acc, y = cv_acc[:, c, :], cv_scratch[:, c, :]
                m = pe.do(mean_of(acc), cv_mark[c], consts_in, free[b])
                m = dve.do(lambda e: e.tensor_tensor(acc, acc, bank[b][:, :], ALU.subtract), m)
                free[b] = [m]
                m = act.do(lambda e: e.activation(y, acc, ACT.Square), m)
                yield
                m = pe.do(mean_of(y), m, free[b])
                m = act.do(lambda e: e.activation(y, bank[b][:, :], ACT.Sqrt, bias=col("eps")), m)
                free[b] = [m]
                for t in range(TT):
                    part = slice(t * P, (t + 1) * P)
                    r = dve.do(lambda e: e.reciprocal(y[:, part], y[:, part]), m)
                    yield
                cv_mark[c] = dve.do(lambda e: e.tensor_tensor(acc, acc, y, ALU.mult), r)
            for c in chunks:
                acc = cv_acc[:, c, :]
                cv_mark[c] = act.do(lambda e: e.activation(acc, acc, ACT.Silu, scale=col("cv_norm_g", c),
                                                           bias=col("cv_norm_b", c)), cv_mark[c])

        def between():
            groups = group_norms()
            for c in range(1, AC):
                product_steps = linear_steps(NORM_BANKS[1], 1, range(KC), h_hi, h_lo, h_marks)
                while True:
                    try:
                        next(product_steps)
                    except StopIteration as end:
                        b, m = end.value
                        break
                    next(groups, None)
                    yield
                take_queries(c, b, m)
            for _ in groups:
                pass
            h_read[0] = m
            for c in range(SC):
                k = AC + c
                mix_marks[k] = split(sg_out[:, c, :], sg_done[c], h_hi[:, k, :], h_lo[:, k, :], m)
            for c in range(CC):
                k = AC + SC + c
                mix_marks[k] = split(cv_acc[:, c, :], cv_mark[c], h_hi[:, k, :], h_lo[:, k, :], m)
            for _ in range(3):
                yield
            for o in range(KC):
                b, m = yield from linear_steps(NORM_BANKS[o % 2], 1, range(AC, KC), h_hi, h_lo, mix_marks)
                add_gated(o, b, m, 2 * KC)

        filler = between()
        probs_free, probs_t_free = [handed, handed], [handed, handed]
        normalised, copied = {}, {}

        def scores(i):
            h, b = steps[i]
            c, part, u = h // 2, slice((h % 2) * HD, (h % 2 + 1) * HD), i % 2
            q = q_loc[part, c, b * P:(b + 1) * P]
            kl = k_loc[part, c, SPAN_START[b] * ROWS:(SPAN_START[b] + SPAN) * ROWS]
            S = bank[u]
            local = S[:, 0:ROWS * SPAN]

            def mm(e):
                e.matmul(local, q, kl, start=True, stop=True)
                return e.matmul(S[:, ROWS * SPAN:T], q, k_ctx[part, c, :], start=True, stop=True)
            m = pe.do(mm, q_marks[c], k_marks[c], kc_marks[c], free[u])
            v = SPAN_OFFS.index(SPAN_START[b] - WIN * b)
            m = dve.do(lambda e: e.tensor_tensor(local, local, biased[:, v, h, :, :, :].rearrange("p g r c -> p (g r c)"), ALU.add), m, bias_in[v, h])
            m = dve.do(lambda e: e.reduce_max(soft[:, u, 1:2], S[:, :], AX.X, negate=True), m, probs_free[u])
            m = act.do(lambda e: e.activation(probs[:, u, :], S[:, :], ACT.Exp, bias=soft[:, u, 1:2],
                                              accum_out=soft[:, u, 2:3]), m, probs_free[u])
            free[u] = [m]
            m = dve.do(lambda e: e.reciprocal(soft[:, u, 3:4], soft[:, u, 2:3]), m)
            normalised[i] = dve.do(lambda e: e.tensor_scalar(probs[:, u, :], probs[:, u, :], soft[:, u, 3:4], None,
                                                             ALU.mult), m)

        def turn_over(i):
            u = i % 2
            B = bank[2 + u]

            def mm(e):
                for n in range(T // P):
                    m = e.transpose(B[:, n * P:(n + 1) * P], probs[:, u, n * P:(n + 1) * P], identity)
                return m
            m = pe.do(mm, normalised[i], free[2 + u])
            probs_free[u] = [m]
            copied[i] = act.do(lambda e: e.activation(probs_t[:, u, :], B[:, :], ACT.Copy), m, probs_t_free[u])
            free[2 + u] = [copied[i]]

        def weighted(i):
            h, b = steps[i]
            c, p0, u = h // 2, (h % 2) * HD, i % 2
            ob = 4 + c % 2
            tiles = v_loc if SPAN_START[b] % WIN == 0 else v_mid
            values = [tiles[:, SPAN_START[b] // WIN + n, :] for n in range(2)] + [v_ctx[:, n, :] for n in range(CT)]

            def mm(e):
                for n, v in enumerate(values):
                    m = e.matmul(bank[ob][p0:p0 + HD, b * P:(b + 1) * P], v[:, h * HD:(h + 1) * HD],
                                 probs_t[:, u, n * P:(n + 1) * P], start=(n == 0), stop=(n == len(values) - 1))
                return m
            m = pe.do(mm, copied[i], v_marks, moved, free[ob] if (h % 2, b) == (0, 0) else None)
            probs_t_free[u] = [m]
            if (h % 2, b) == (1, CBLK - 1):
                mix_marks[c] = split(grid_of(bank[ob][:, :]), m, rows_of(h_hi[:, c, :]), rows_of(h_lo[:, c, :]), h_read[0])
                free[ob] = [mix_marks[c][1]]

        for i in range(len(steps) + 2):
            if i < len(steps):
                scores(i)
            for _ in range(2 if i < KC else i % 2):
                next(filler, None)
            if 1 <= i <= len(steps):
                turn_over(i - 1)
            next(filler, None)
            if 2 <= i:
                weighted(i - 2)
        for _ in filler:
            pass
        attention.close()
        mixer.close()

        gain_m = dve.do(lambda e: e.scalar_tensor_tensor(out=gain[:, :], in0=mod[:, 4 * KC:5 * KC], scalar=1.0,
                                                         in1=cols_of("norm2_g"), op0=ALU.add, op1=ALU.mult), mod_rest)
        ada.close()
        buffer_free[:] = [everyone(), everyone()]
        norm2 = Norm(T, exact[:, 0, :])
        for o, (b, m) in enumerate(linears(KC, AC, h_hi, h_lo, mix_marks)):
            add_gated(o, b, m, 2 * KC)
            norm2.square(x[:, o, :], x_marks[o])
        r, m = norm2.finish()
        h_marks = apply_norm(r, m, lambda k: x[:, k, :], x_marks, T, lambda k: gain[:, k:k + 1],
                             lambda k: mod[:, 3 * KC + k:3 * KC + k + 1], gain_m, flat_chunks(h_hi), flat_chunks(h_lo), (pe.sem, pe.count))

        ffn = ExitStack()
        a_hi = sb(ffn, "a_hi", [P, FC, T], F32R)
        a_lo = sb(ffn, "a_lo", [P, FC, T], F32R)
        handed = everyone()
        work_free = [handed, handed]
        a_marks = [None] * FC
        products = linears(2 * FC, KC, h_hi, h_lo, h_marks)
        for f in range(FC):
            (bg, mg), (bu, mu) = next(products), next(products)
            y = normed[:, f % 2, :]
            m = causal_or_centred(bank[bg][:, :], y, "ffn_conv_w", 3 * f, (-1, 0, 1), mg, work_free[f % 2], col("ffn_conv_b", f))
            free[bg] = [m]
            m = act.do(lambda e: e.activation(y, y, ACT.Silu), m)
            m = dve.do(lambda e: e.tensor_tensor(y, bank[bu][:, :], y, ALU.mult), m, mu)
            free[bu] = [m]
            a_marks[f] = split(y, m, a_hi[:, f, :], a_lo[:, f, :], handed)
            work_free[f % 2] = a_marks[f]
        gain_read = (pe.sem, pe.count)
        norm_f, norm3 = Norm(T, exact[:, 0, :]), Norm(T, exact[:, 1, :])
        for o in range(KC):
            b, m = linear(3, FC, a_hi, a_lo, a_marks)
            add_gated(o, b, m, 5 * KC)
            norm_f.square(x[:, o, :], x_marks[o])
            norm3.square(x[:, o, :], x_marks[o], col("final_norm_g", o))
        ffn.close()

        gain_m = dve.do(lambda e: e.tensor_tensor(gain[:, :], cols_of("final_norm_g"), cols_of("norm_mix_pre_2"), ALU.mult),
                        cols_in, gain_read)
        norm_f.end_of_sums()
        norm3.end_of_sums()
        both = small[:, 0:TT]
        m = dve.do(lambda e: e.tensor_scalar(both, bank[norm_f.b][:, 0:TT], EPS, EPS * EPS * D, ALU.mult, ALU.add), norm_f.mark)
        m = dve.do(lambda e: e.tensor_tensor(both, bank[norm3.b][:, 0:TT], both, ALU.add), m, norm3.mark)
        read = m
        m = act.do(lambda e: e.activation(both, both, ACT.Sqrt, scale=1.0 / D), m)
        m = dve.do(lambda e: e.reciprocal(both, both), m)
        both_spread = spread(both, [m, read], norm3.b)
        r1, r1_marks = norm_f.factors()

        buffer_free[:] = [everyone(), everyone()]
        h_marks = apply_norm(norm3.b, both_spread, lambda k: x[:, k, :], x_marks, T, lambda k: gain[:, k:k + 1], None,
                             gain_m, flat_chunks(h_hi), flat_chunks(h_lo), (pe.sem, pe.count))
        stream.prepare_ahead()
        r1_spread = spread(r1, r1_marks, norm_f.b)
        for k in range(KC):
            x_marks[k] = dve.do(lambda e: e.scalar_tensor_tensor(
                out=x[:, k, :], in0=x[:, k, :], scalar=col("final_norm_g", k), in1=bank[norm_f.b][:, :], op0=ALU.mult,
                op1=ALU.mult), r1_spread, x_marks[k], h_marks[k])
        free[norm_f.b] = [x_marks[-1]]
        branch = ExitStack()
        att_hi = sb(branch, "att_hi", [P, AC, T], F32R)
        att_lo = sb(branch, "att_lo", [P, AC, T], F32R)
        cnv_hi = sb(branch, "cnv_hi", [P, AC, T], F32R)
        cnv_lo = sb(branch, "cnv_lo", [P, AC, T], F32R)
        stick = ExitStack()
        q2 = sb(stick, "q2", [P, AC, T])
        k2 = sb(stick, "k2", [P, AC, T])
        v2 = sb(stick, "v2", [P, TT, ATT])
        NZ = sum(T - P * j for j in range(TT))
        z = sb(stick, "z", [P, 3, NZ])
        sp = sb(stick, "sp", [P, 2, NZ])
        sp_hi = sb(stick, "sp_hi", [P, 2, NZ], F32R)
        sp_lo = sb(stick, "sp_lo", [P, 2, NZ], F32R)
        minus = sb(stick, "minus", [P, 2 * P], F32R)
        handed = everyone()

        all_, tri = minus[:, 0:P], minus[:, P:2 * P]
        minus_in = act.do(lambda e: e.activation(minus[:, :], consts[:, CONSTS["minus_ones"][0]:CONSTS["minus_ones"][0] + 2 * P],
                                                 ACT.Copy), consts_in, handed)

        qk_marks = []
        for c, (b, m) in enumerate(linears(2 * AC, KC, h_hi, h_lo, h_marks)):
            dst, scale = (q2[:, c, :], SCALE) if c < AC else (k2[:, c - AC, :], 1.0)
            qk_marks.append(act.do(lambda e: e.activation(dst, bank[b][:, :], ACT.Copy, scale=scale), m, handed))
            free[b] = [qk_marks[c]]
        vb = [banks.take() for _ in range(TT)]
        v_marks = [None] * TT
        for tile in range(ATT * D // (P * SLOT)):
            s, w_marks, (k0, n) = stream.next_tile()
            for t in range(TT):
                def mm(e):
                    for j in range(n):
                        k, w, tok = k0 + j, slice(j * ATT, (j + 1) * ATT), slice(t * P, (t + 1) * P)
                        m = product(e, bank[vb[t]][:, :], h_hi[:, k, tok], h_lo[:, k, tok], w_hi[:, s, w], w_lo[:, s, w],
                                    k == 0, k == KC - 1)
                    return m
                v_marks[t] = pe.do(mm, w_marks, h_marks, free[vb[t]] if tile == 0 else None)
            stream.split_free[s] = [v_marks[-1]]
        for t in range(TT):
            v_marks[t] = act.do(lambda e: e.activation(v2[:, t, :], bank[vb[t]][:, :], ACT.Copy), v_marks[t], handed)
            free[vb[t]] = [v_marks[t]]

        cnv_marks = [None] * AC
        VALUES_BANK, BETWEEN_BANK = NORM_BANKS

        def between_sticks():
            work_free = [[handed], [handed]]
            for c in range(AC):
                u, y = normed[:, c % 2, :], exact[:, c % 2, :]

                def own_product():
                    return finished(linear_steps(BETWEEN_BANK, 1, range(KC), h_hi, h_lo, h_marks))
                b, m = own_product()
                m = act.do(lambda e: e.activation(u, bank[b][:, :], ACT.Copy), m, work_free[c % 2])
                free[b] = [m]
                yield
                b, mx = own_product()
                m = dve.do(lambda e: e.tensor_tensor(u, bank[b][:, :], u, ALU.mult), mx, m)
                free[b] = [m]
                m = causal_or_centred(u, y, "conv_mix_w_2", 3 * c, (-2, -1, 0), m, work_free[c % 2])
                yield
                b, mb = own_product()
                m = dve.do(lambda e: e.tensor_tensor(y, bank[b][:, :], y, ALU.mult), m, mb)
                free[b] = [m]
                cnv_marks[c] = split(y, m, cnv_hi[:, c, :], cnv_lo[:, c, :], handed)
                work_free[c % 2] = [cnv_marks[c]]
                yield

        DIAG = [slice(j * P, (j + 1) * P) for j in range(TT)]
        OFF_AT = [T, T + 3 * P, T + 5 * P]

        def off(j, q_from, q_to=TT):
            return slice(OFF_AT[j] + (q_from - j - 1) * P, OFF_AT[j] + (q_to - j - 1) * P)

        PARTS = [(0, slice(0, T), 0), (1, slice(T, T + 3 * P), 0), (1, slice(T + 5 * P, NZ), 3 * P), (2, slice(T + 3 * P, T + 5 * P), 0)]

        def where(columns):
            for n, part, at in PARTS:
                if part.start <= columns.start and columns.stop <= part.stop:
                    return n, slice(columns.start - part.start + at, columns.stop - part.start + at)

        z_free, sp_free, split_sp_free = [handed] * 3, [handed] * 2, [handed] * 2
        exp_ready, ln_ready, z_ready, w_ready = {}, {}, {}, {}
        att_marks = [None] * AC

        def stick_scores(h):
            c, part, u = h // 2, slice((h % 2) * HD, (h % 2 + 1) * HD), h % 3

            def mm(e):
                for j in range(TT):
                    keys = k2[part, c, j * P:(j + 1) * P]
                    m = e.matmul(bank[0][:, DIAG[j]], keys, q2[part, c, j * P:(j + 1) * P], start=True, stop=True)
                    if j < TT - 1:
                        n, at = where(off(j, j + 1))
                        m = e.matmul(bank[n][:, at], keys, q2[part, c, (j + 1) * P:T], start=True, stop=True)
                return m
            m = pe.do(mm, qk_marks[c], qk_marks[AC + c], free[0], free[1], free[2])
            hidden = const("causal_neg").unsqueeze(1).to_broadcast([P, TT, P])
            d = dve.do(lambda e: e.tensor_tensor(z[:, u, 0:T].rearrange("p (t q) -> p t q", t=TT),
                                                 bank[0][:, :].rearrange("p (t q) -> p t q", t=TT), hidden, ALU.add),
                       m, z_free[u])
            free[0] = [d]
            for n, part_, at in PARTS[1:]:
                o = act.do(lambda e: e.activation(z[:, u, part_], bank[n][:, at:at + part_.stop - part_.start], ACT.Copy),
                           m, z_free[u])
                free[n] = [o]
            m = dve.do(lambda e: e.scalar_tensor_tensor(out=sp[:, h % 2, :], in0=z[:, u, :], scalar=-1.0, in1=z[:, u, :],
                                                        op0=ALU.mult, op1=ALU.min), d, o, sp_free[h % 2])
            exp_ready[h] = act.do(lambda e: e.activation(sp[:, h % 2, :], sp[:, h % 2, :], ACT.Exp), m)

        def stick_logarithm(h):
            ss = sp[:, h % 2, :]
            ln_ready[h] = act.do(lambda e: e.activation(ss, ss, ACT.Ln, bias=col("one")), exp_ready[h])

        def stick_softplus(h):
            zz, ss, v = z[:, h % 3, :], sp[:, h % 2, :], h % 2
            m = dve.do(lambda e: e.scalar_tensor_tensor(out=ss, in0=zz, scalar=0.0, in1=ss, op0=ALU.max, op1=ALU.add), ln_ready[h])
            hi = dve.do(lambda e: e.tensor_copy(sp_hi[:, v, :], ss), m, split_sp_free[v])
            lo = dve.do(lambda e: e.tensor_tensor(sp_lo[:, v, :], ss, sp_hi[:, v, :].bitcast(F32), ALU.subtract), hi)
            sp_free[h % 2] = [lo]
            z_ready[h] = [hi, lo]

        def stick_weights(h):
            u, v = h % 3, h % 2

            def add_up(e, dst, minus_what, columns, first, last):
                e.matmul(dst, minus_what, sp_hi[:, v, columns], start=first, stop=False)
                return e.matmul(dst, minus_what, sp_lo[:, v, columns], start=False, stop=last)

            def mm(e):
                add_up(e, bank[3][:, :], tri, slice(0, T), True, True)
                for j in range(TT - 1):
                    own = off(j, j + 1)
                    n, at = where(own)
                    add_up(e, bank[3 + n][:, at], tri, own, True, False)
                    for i in range(j + 1, TT):
                        if i < TT - 1:
                            n, at = where(off(j, i + 1))
                            add_up(e, bank[3 + n][:, at], all_, off(i, i + 1), False, False)
                        n, at = where(off(j, i, i + 1))
                        m = add_up(e, bank[3 + n][:, at], all_, DIAG[i], False, i == TT - 1)
                return m
            m = pe.do(mm, z_ready[h], minus_in, free[3], free[4], free[5])
            split_sp_free[v] = [m]
            for n, part, at in PARTS:
                a = dve.do(lambda e: e.tensor_tensor(z[:, u, part], z[:, u, part],
                                                     bank[3 + n][:, at:at + part.stop - part.start], ALU.add), m)
                free[3 + n] = [a]
            w_ready[h] = act.do(lambda e: e.activation(z[:, u, :], z[:, u, :], ACT.Exp), a)

        def stick_values(h):
            c, p0, u = h // 2, (h % 2) * HD, h % 3
            ob = VALUES_BANK

            def mm(e):
                for j in range(TT):
                    v = v2[:, j, h * HD:(h + 1) * HD]
                    m = e.matmul(bank[ob][p0:p0 + HD, DIAG[j]], v, z[:, u, DIAG[j]], start=(j == 0), stop=(j == TT - 1),
                                 skip_group_check=True)
                    if j < TT - 1:
                        m = e.matmul(bank[ob][p0:p0 + HD, (j + 1) * P:T], v, z[:, u, off(j, j + 1)], start=False,
                                     stop=False, skip_group_check=True)
                return m
            m = pe.do(mm, w_ready[h], v_marks, free[ob] if h % 2 == 0 else None)
            z_free[u] = [m]
            if h % 2:
                att_marks[c] = split(bank[ob][:, :], m, att_hi[:, c, :], att_lo[:, c, :])
                free[ob] = [att_marks[c][1]]

        filler = between_sticks()
        for h in range(HEADS + 2):
            if h < HEADS:
                stick_scores(h)
            if 2 <= h:
                stick_weights(h - 2)
            if h < HEADS:
                stick_logarithm(h)
            if 1 <= h <= HEADS:
                stick_softplus(h - 1)
            next(filler, None)
            if h in (0, HEADS):
                next(filler, None)
            if 2 <= h:
                stick_values(h - 2)
        for _ in filler:
            pass
        stick.close()

        merge = ExitStack()
        m_hi = sb(merge, "m_hi", [P, KC, T], F32R)
        m_lo = sb(merge, "m_lo", [P, KC, T], F32R)
        handed = everyone()
        m_marks, work_free = [None] * KC, [[handed], [handed]]
        for o in range(KC):
            i = o % 2
            ga, ma = linear(1, KC, h_hi, h_lo, h_marks)
            gc, mc = linear(1, KC, h_hi, h_lo, h_marks)
            ya, na = linear(1, AC, att_hi, att_lo, att_marks)
            yc, nc_ = linear(1, AC, cnv_hi, cnv_lo, cnv_marks)
            u, y = normed[:, i, :], exact[:, i, :]
            sa = act.do(lambda e: e.activation(u, bank[ga][:, :], ACT.Sigmoid), ma, work_free[i])
            sc = act.do(lambda e: e.activation(y, bank[gc][:, :], ACT.Sigmoid), mc, work_free[i])
            pa = dve.do(lambda e: e.tensor_tensor(u, bank[ya][:, :], u, ALU.mult), na, sa)
            pc = dve.do(lambda e: e.tensor_tensor(y, bank[yc][:, :], y, ALU.mult), nc_, sc)
            free[ga], free[gc], free[ya], free[yc] = [sa], [sc], [pa], [pc]
            both = dve.do(lambda e: e.tensor_tensor(u, u, y, ALU.add), pa, pc)
            m_marks[o] = split(u, both, m_hi[:, o, :], m_lo[:, o, :], handed)
            work_free[i] = [m_marks[o]]

        def normed_into_x(y_buf, products, gain_name, y_free, next_norm):
            norm, y_marks, marks = Norm(T, exact[:, 0, :]), [], []
            for o, (b, m) in enumerate(products):
                norm.square(bank[b][:, :], m)
                y_marks.append(act.do(lambda e: e.activation(y_buf[:, o, :], bank[b][:, :], ACT.Copy), m, y_free))
                free[b] = [y_marks[o]]
            r, m = norm.finish()
            for k in range(KC):
                y, g = y_buf[:, k, :], col(gain_name, k)
                n = dve.do(lambda e: e.scalar_tensor_tensor(out=y, in0=y, scalar=g, in1=bank[r][:, :], op0=ALU.mult,
                                                            op1=ALU.mult), m, y_marks[k])
                marks.append((pool if k in (1, 4) else dve).do(
                    lambda e: e.tensor_tensor(x[:, k, :], x[:, k, :], y, ALU.add), n, x_marks[k]))
                next_norm.square(x[:, k, :], marks[k])
            free[r] = [n]
            return marks

        y_buf = sb(merge, "y_buf", [P, KC, T])
        norm4 = Norm(T, pairs=sb(merge, "square_pairs", [P, 4, T]))
        x_marks = normed_into_x(y_buf, linears(KC, KC, m_hi, m_lo, m_marks), "norm_mix_post_2", handed, norm4)
        merge.close()
        branch.close()
        buffer_free[:] = [everyone(), everyone()]
        r, m = norm4.finish()
        h_marks = apply_norm(r, m, lambda k: x[:, k, :], x_marks, T, lambda k: col("norm_ffn_pre_2", k), None, None,
                             flat_chunks(h_hi), flat_chunks(h_lo), (pe.sem, pe.count))

        ffn = ExitStack()
        a_hi = sb(ffn, "a2_hi", [P, FC, T], F32R)
        a_lo = sb(ffn, "a2_lo", [P, FC, T], F32R)
        y_buf = sb(ffn, "y2_buf", [P, KC, T])
        handed = everyone()
        work_free = [[handed], [handed]]
        products = linears(2 * FC, KC, h_hi, h_lo, h_marks)
        for f in range(FC):
            (ba, ma), (bg, mg) = next(products), next(products)
            u, y = normed[:, f % 2, :], exact[:, f % 2, :]
            m1 = causal_or_centred(bank[ba][:, :], u, "conv_ffn_w_2", 3 * f, (-2, -1, 0), ma, work_free[f % 2])
            m2 = causal_or_centred(bank[bg][:, :], y, "conv_ffn_w_2", 3 * (FC + f), (-2, -1, 0), mg, work_free[f % 2])
            free[ba], free[bg] = [m1], [m2]
            m2 = act.do(lambda e: e.activation(y, y, ACT.Gelu_apprx_tanh), m2)
            m = dve.do(lambda e: e.tensor_tensor(u, u, y, ALU.mult), m1, m2)
            a_marks[f] = split(u, m, a_hi[:, f, :], a_lo[:, f, :], handed)
            work_free[f % 2] = [a_marks[f], m]
        norm, y_marks = Norm(T, exact[:, 0, :]), [None] * KC
        for o in range(KC - 1):
            b, m = linear(3, FC, a_hi, a_lo, a_marks)
            norm.square(bank[b][:, :], m)
            y_marks[o] = act.do(lambda e: e.activation(y_buf[:, o, :], bank[b][:, :], ACT.Copy), m, handed)
            free[b] = [y_marks[o]]
        norm.add_waiting()
        tiles = [stream.next_tile() for _ in range(3)]
        done, o, nt = counter("s_out"), KC - 1, TT // 2
        n_tok = nt * P
        halves = [slice(half * n_tok, (half + 1) * n_tok) for half in range(2)]
        product_b, factor_b = [banks.take(), banks.take()], [banks.take(), banks.take()]
        product_m, factors = [None, None], {}

        def last_product(half, tile):
            (s, w_marks, (k0, n)), b, tok = tiles[tile], product_b[half], halves[half]

            def mm(e):
                for j in range(n):
                    k, w = k0 + j, slice(j * P, (j + 1) * P)
                    m = product(e, bank[b][:, 0:n_tok], w_hi[:, s, w], w_lo[:, s, w], a_hi[:, k, tok], a_lo[:, k, tok],
                                k == 0, k == FC - 1)
                return m
            product_m[half] = pe.do(mm, w_marks, a_marks, free[b])

        def half_sums(half):
            b, norm_b, tok, at = product_b[half], NORM_BANKS[half], halves[half], nt * half
            part, f, m = squares[:, half, 0:n_tok], rstd[:, at:at + nt], product_m[half]
            sq = act.do(lambda e: e.activation(part, bank[b][:, 0:n_tok], ACT.Square), m, square_free[half])
            y_marks[o] = act.do(lambda e: e.activation(y_buf[:, o, tok], bank[b][:, 0:n_tok], ACT.Copy), m, handed)

            def sums(e, src, first, last):
                for t in range(nt):
                    m = e.matmul(bank[norm_b][:, t:t + 1], src[:, t * P:(t + 1) * P], ones[:, :],
                                 start=(first and t == 0), stop=(last and t == nt - 1), skip_group_check=True)
                return m
            m = pe.do(lambda e: sums(e, norm.total[:, tok], True, False), norm.total_mark, free[norm_b])
            m = pe.do(lambda e: sums(e, part, False, True), m, sq)
            root = act.do(lambda e: e.activation(std[:, at:at + nt], bank[norm_b][:, 0:nt], ACT.Sqrt, scale=1.0 / D,
                                                 bias=col("eps")), m)
            factors[half] = (f, [dve.do(lambda e: e.reciprocal(f, std[:, at:at + nt]), root), root])

        def finish_half(half):
            b, tok, (f, marks) = factor_b[half], halves[half], factors[half]
            factor_m = spread(f, [marks, free[b]], b)
            result = []
            for k in range(KC):
                y, g, xk = y_buf[:, k, tok], col("norm_ffn_post_2", k), x[:, k, tok]
                m = dve.do(lambda e: e.scalar_tensor_tensor(out=y, in0=y, scalar=g, in1=bank[b][:, 0:n_tok],
                                                            op0=ALU.mult, op1=ALU.mult), factor_m, y_marks[k])
                result.append((pool if k in (1, 4) else dve).do(lambda e: e.tensor_tensor(xk, xk, y, ALU.add), m, x_marks[k]))
                if k % 2:
                    stored = sync.load(done, out[:, k - 1:k + 1, tok], x[:, k - 1:k + 1, tok], result[k - 1:])
            return stored

        for tile in range(len(tiles)):
            last_product(0, tile)
        half_sums(0)
        last_product(1, 0)
        finish_half(0)
        last_product(1, 1)
        last_product(1, 2)
        half_sums(1)
        stored = finish_half(1)
        ffn.close()
        sync.wait(stored)


def columns(v):
    return v.reshape(-1, P).T


def tap_columns(w):
    return w.T.reshape(-1, P, w.shape[0]).transpose(1, 0, 2).reshape(P, -1)


def by_feature(v):
    return v.T.reshape(-1, P, v.shape[0]).transpose(1, 0, 2)


def blocks(w):
    k, n = w.shape
    return w.reshape(k // P, P, n // P, P).transpose(2, 1, 0, 3)


def wide(w):
    k, n = w.shape
    per = SLOT // n
    return w.reshape(k // P // per, per, P, n).transpose(0, 2, 1, 3)


def row_and_column(p):
    return p // GROUP % ROWS, p // (GROUP * ROWS) * GROUP + p % GROUP


def shape_constants():
    i = np.arange(P)
    group = (i[:, None] // HD == i[None, :] // HD) / float(CV // 4)
    tri = -(i[:, None] >= i[None, :]).astype(np.float32)
    causal = np.where(i[:, None] < i[None, :], 0.0, NEG)
    hidden = np.zeros((P, len(SPAN_OFFS), SPAN))
    for b in range(CBLK):
        q = WIN * b + np.array([row_and_column(p)[1] for p in range(P)])
        start = np.clip(q - WIN // 2, 0, GRID_W - WIN)
        key = SPAN_START[b] + np.arange(SPAN)
        inside = (key[None, :] >= start[:, None]) & (key[None, :] < start[:, None] + WIN)
        hidden[:, SPAN_OFFS.index(SPAN_START[b] - WIN * b), :] = np.where(inside, 0.0, NEG)
    return np.concatenate([np.eye(P), group, -np.ones((P, P)), tri, causal, hidden.reshape(P, -1)],
                          axis=1).astype(np.float32)


def laid_out(i):
    w_in, w_in2 = i["w_in"][0], i["w_in_2"][0]
    o_u, o_v, o_a, o_g = 3 * ATT, 3 * ATT + SG, 3 * ATT + 2 * SG, 3 * ATT + 2 * SG + CV
    ada_w = i["ada_w"][0]
    small = {
        "ada_b": columns(i["ada_b"][0]),
        "norm1_g": columns(i["norm1_g"][0]), "norm2_g": columns(i["norm2_g"][0]),
        "final_norm_g": columns(i["final_norm_g"]), "cv_w": tap_columns(i["cv_w"][0]), "cv_b": columns(i["cv_b"][0]),
        "cv_norm_g": columns(i["cv_norm_g"][0]), "cv_norm_b": columns(i["cv_norm_b"][0]),
        "ffn_conv_w": tap_columns(i["ffn_conv_w"][0]), "ffn_conv_b": columns(i["ffn_conv_b"][0]),
        "norm_mix_pre_2": columns(i["norm_mix_pre_2"][0]), "norm_mix_post_2": columns(i["norm_mix_post_2"][0]),
        "norm_ffn_pre_2": columns(i["norm_ffn_pre_2"][0]), "norm_ffn_post_2": columns(i["norm_ffn_post_2"][0]),
        "conv_mix_w_2": tap_columns(i["conv_mix_w_2"][0]), "conv_ffn_w_2": tap_columns(i["conv_ffn_w_2"][0]),
        "eps": np.full((P, 1), EPS, np.float32), "one": np.ones((P, 1), np.float32),
    }
    rel = np.zeros((HEADS, WIN + (2 * ROWS - 1) * RPB_W + WIN + SPAN), np.float32)
    rel[:, WIN:WIN + (2 * ROWS - 1) * RPB_W] = i["na_rpb"][0].reshape(HEADS, -1)
    starts = [(ROWS - 1 - row) * RPB_W + WIN - 1 - column for row, column in map(row_and_column, range(P))]
    b_cols, c_cols = blocks(w_in2[:, 3 * ATT:4 * ATT]), blocks(w_in2[:, 4 * ATT:5 * ATT])
    x_cols = blocks(w_in2[:, 5 * ATT:6 * ATT])
    a_blocks, g_blocks = blocks(w_in[:, o_a:o_g]), blocks(w_in[:, o_g:o_g + CV])
    sg_small = np.concatenate([
        np.repeat(i["sg_b"][0], SG // 4, axis=0).reshape(SC, P, P).transpose(1, 0, 2).reshape(P, -1),
        np.broadcast_to(i["sg_norm_g"][0], (P, SG)), np.broadcast_to(i["sg_norm_b"][0], (P, SG)),
        i["sg_w"][0].transpose(2, 0, 1).reshape(P, -1)], axis=1)
    arrays = {
        "x": by_feature(i["x"][0]), "ctx": by_feature(i["ctx"][0]),
        "cols": np.concatenate([small[n] for n, _ in COLUMN_SIZES], axis=1),
        "consts": shape_constants(),
        "c_cols": np.stack([columns(i["c"][0]), columns(i["c_ctx"])], axis=2),
        "c_row": np.broadcast_to(i["c"][0], (P, D)), "sg_small": sg_small,
        "rel_rows": np.stack([rel[:, s:s + WINDOW] for s in starts]),
        "ada_turned": ada_w[:, :2 * D].reshape(KC, P, 2, D).transpose(2, 0, 1, 3), "ada_rows": ada_w[:, 2 * D:].T.reshape(4 * KC, P, D),
        "w_cv": np.stack([a_blocks, g_blocks], axis=1).reshape(2 * CC, P, KC, P),
        "w_sg_v": blocks(w_in[:, o_v:o_a]), "w_sg_u": blocks(w_in[:, o_u:o_v]),
        "w_q": blocks(w_in[:, 0:ATT]), "w_k": blocks(w_in[:, ATT:2 * ATT]), "w_v": wide(w_in[:, 2 * ATT:3 * ATT]),
        "w_out": blocks(i["w_out"][0]), "w_ffn_up": blocks(i["ffn_w_up"][0]), "w_ffn_down": blocks(i["ffn_w_down"][0]),
        "w_qk2": blocks(w_in2[:, 0:2 * ATT]), "w_v2": wide(w_in2[:, 2 * ATT:3 * ATT]),
        "w_conv3": np.stack([c_cols, x_cols, b_cols], axis=1).reshape(3 * AC, P, KC, P),
        "w_gates2": blocks(w_in2[:, 6 * ATT:6 * ATT + 2 * D]),
        "w_att2": blocks(i["w_att_branch_2"][0]), "w_convb2": blocks(i["w_conv_branch_2"][0]),
        "w_out2": blocks(i["w_out_2"][0]), "w_up2": blocks(i["w_up_2"][0]), "w_down2": blocks(i["w_down_2"][0]),
    }
    return {name: np.ascontiguousarray(a) for name, a in arrays.items()}


def kernel(**inputs):
    import concourse.bacc as bacc
    from concourse.bass_utils import run_bass_kernel_spmd

    arrays = laid_out({name: np.asarray(v) for name, v in inputs.items()})
    nc = bacc.Bacc("TRN2", target_bir_lowering=False, num_devices=1)
    io = {name: nc.dram_tensor(f"in_{name}", a.shape, mybir.dt.from_np(a.dtype), kind="ExternalInput").ap()
          for name, a in arrays.items()}
    out = nc.dram_tensor("out_x", (P, KC, T), F32, kind="ExternalOutput").ap()
    two_blocks(nc, io, out)
    result = run_bass_kernel_spmd(nc, [{f"in_{name}": a for name, a in arrays.items()}], core_ids=[0])
    got = result.results[0]["out_x"]
    return np.ascontiguousarray(got.transpose(2, 1, 0).reshape(1, T, D))
```
